# Optimizing a Trainium2 kernel written in Bass

```python
import math
import jax, jax.numpy as jnp
from jax import lax
import numpy as np

D_MODEL = 1024
BATCH = 1
SEQ = 256
DEPTH = 1
DEC_BATCH = 8
DEC_SEQ = 1
PAST_LEN = 2048
PAGE_SIZE = 128

CONV_DIM = D_MODEL
CONV_W = 3
HEAD_DIM = 64
N_HEADS = D_MODEL // HEAD_DIM
N_KV = max(N_HEADS // 8, 1)
GROUP = N_HEADS // N_KV
WINDOW = 128
ATTN_BLOCK = 128
ATTN_SCALE = HEAD_DIM ** -0.5
N_BUCKETS = 32
MAX_DISTANCE = 128
NEG_INF = -1e30
N_EXPERTS = 32
TOP_K = 4
D_EXPERT = D_MODEL
SWIGLU_ALPHA = 1.702
SWIGLU_LIMIT = 7.0
MOE_BLOCK = 128
EPS = 1e-5
IN_SPLITS = (CONV_DIM, CONV_DIM, CONV_DIM, N_HEADS * HEAD_DIM, N_KV * HEAD_DIM, N_KV * HEAD_DIM, D_MODEL, D_MODEL)
IN_DIM = sum(IN_SPLITS)

kernel_name = 'hybrid_shortconv_swa_moe_step'

def rmsnorm(x, w):
    xf = x.astype(jnp.float32)
    y = xf * lax.rsqrt(jnp.mean(xf * xf, axis=-1, keepdims=True) + EPS) * w.astype(jnp.float32)
    return y.astype(x.dtype)

def t5_bucket(rel):
    n = jnp.maximum(rel, 0)
    max_exact = N_BUCKETS // 2
    nf = jnp.maximum(n, 1).astype(jnp.float32)
    large = max_exact + (jnp.log(nf / max_exact) / math.log(MAX_DISTANCE / max_exact) * (N_BUCKETS - max_exact)).astype(jnp.int32)
    large = jnp.minimum(large, N_BUCKETS - 1)
    return jnp.where(n < max_exact, n, large)

def causal_short_conv(u, prefix, w):
    T = u.shape[1]
    full = jnp.concatenate([prefix.astype(u.dtype), u], axis=1)
    out = full[:, 0:T] * w[0]
    for j in range(1, CONV_W):
        out = out + full[:, j:j + T] * w[j]
    return out, full[:, -(CONV_W - 1):]

def attn_core(qb, kk, vv, rel, valid, rel_bias, sinks):
    Q, S = rel.shape
    s = jnp.einsum('bnqkgd,bnskd->bnkgqs', qb, kk).astype(jnp.float32) * ATTN_SCALE
    bias = rel_bias[t5_bucket(rel)].astype(jnp.float32)
    s = s + bias.transpose(2, 0, 1).reshape(N_KV, GROUP, Q, S)
    s = jnp.where(valid[None, :, None, None], s, NEG_INF)
    sink = jnp.broadcast_to(sinks.astype(jnp.float32).reshape(N_KV, GROUP, 1, 1), s.shape[:-1] + (1,))
    p = jax.nn.softmax(jnp.concatenate([s, sink], axis=-1), axis=-1)[..., :-1]
    return jnp.einsum('bnkgqs,bnskd->bnqkgd', p.astype(vv.dtype), vv)

def window_attention_prompt(q, k, v, rel_bias, sinks):
    b, T = q.shape[:2]
    nb = T // ATTN_BLOCK
    qb = q.reshape(b, nb, ATTN_BLOCK, N_KV, GROUP, HEAD_DIM)
    kb = k.reshape(b, nb, ATTN_BLOCK, N_KV, HEAD_DIM)
    vb = v.reshape(b, nb, ATTN_BLOCK, N_KV, HEAD_DIM)
    pad = ((0, 0), (1, 0), (0, 0), (0, 0), (0, 0))
    kk = jnp.concatenate([jnp.pad(kb, pad)[:, :-1], kb], axis=2)
    vv = jnp.concatenate([jnp.pad(vb, pad)[:, :-1], vb], axis=2)
    rel = jnp.arange(ATTN_BLOCK)[:, None] + ATTN_BLOCK - jnp.arange(2 * ATTN_BLOCK)[None, :]
    k_pos = (jnp.arange(nb) * ATTN_BLOCK)[:, None] - ATTN_BLOCK + jnp.arange(2 * ATTN_BLOCK)[None, :]
    valid = ((rel >= 0) & (rel < WINDOW))[None] & (k_pos >= 0)[:, None, :]
    out = attn_core(qb, kk, vv, rel, valid, rel_bias, sinks)
    w = min(WINDOW, T)
    return out.reshape(b, T, N_HEADS * HEAD_DIM), k[:, -w:], v[:, -w:]

def window_attention_sample(q, k, v, k_past, v_past, rel_bias, sinks):
    b, T = q.shape[:2]
    W = k_past.shape[1]
    kk = jnp.concatenate([k_past.astype(k.dtype), k], axis=1)
    vv = jnp.concatenate([v_past.astype(v.dtype), v], axis=1)
    rel = jnp.arange(T)[:, None] + W - jnp.arange(W + T)[None, :]
    valid = ((rel >= 0) & (rel < WINDOW))[None]
    out = attn_core(q.reshape(b, 1, T, N_KV, GROUP, HEAD_DIM), kk[:, None], vv[:, None], rel, valid, rel_bias, sinks)
    return out.reshape(b, T, N_HEADS * HEAD_DIM), kk[:, -W:], vv[:, -W:]

def moe_ffn(h, w_router, b_router, w_up, b_up, w_down, b_down):
    T, D = h.shape
    logits = jnp.einsum('td,de->te', h, w_router).astype(jnp.float32) + b_router.astype(jnp.float32)
    top_vals, top_idx = lax.top_k(logits, TOP_K)
    gates = jax.nn.softmax(top_vals, axis=-1)
    TK = T * TOP_K
    n_blocks = -(-TK // MOE_BLOCK) + N_EXPERTS
    n_rows = n_blocks * MOE_BLOCK
    flat_e = top_idx.reshape(TK)
    flat_tok = jnp.repeat(jnp.arange(T, dtype=jnp.int32), TOP_K)
    flat_g = gates.reshape(TK)
    order = jnp.argsort(flat_e)
    sorted_e = flat_e[order]
    counts = jnp.bincount(flat_e, length=N_EXPERTS)
    padded = (counts + MOE_BLOCK - 1) // MOE_BLOCK * MOE_BLOCK
    pad_end = jnp.cumsum(padded)
    pad_start = pad_end - padded
    start = jnp.cumsum(counts) - counts
    dest = pad_start[sorted_e] + jnp.arange(TK) - start[sorted_e]
    row_tok = jnp.full((n_rows,), T, jnp.int32).at[dest].set(flat_tok[order])
    row_gate = jnp.zeros((n_rows,), jnp.float32).at[dest].set(flat_g[order])
    block_expert = jnp.minimum(jnp.searchsorted(pad_end, jnp.arange(n_blocks) * MOE_BLOCK, side='right'), N_EXPERTS - 1)
    xs = jnp.concatenate([h, jnp.zeros((1, D), h.dtype)], axis=0)[row_tok].reshape(n_blocks, MOE_BLOCK, D)

    def expert_block(args):
        xb, e = args
        u = xb @ w_up[e] + b_up[e]
        glu = jnp.minimum(u[:, 0::2], SWIGLU_LIMIT)
        lin = jnp.clip(u[:, 1::2], -SWIGLU_LIMIT, SWIGLU_LIMIT)
        a = glu * jax.nn.sigmoid(SWIGLU_ALPHA * glu) * (lin + 1)
        return a @ w_down[e] + b_down[e]

    ys = lax.map(expert_block, (xs, block_expert))
    y = jax.ops.segment_sum(ys.reshape(n_rows, D).astype(jnp.float32) * row_gate[:, None], row_tok, num_segments=T + 1)[:T]
    return y.astype(h.dtype)

def trunk_layer(x, conv_prefix, k_past, v_past, rel_bias, attn_norm_w, w_in, conv_w, q_norm_w, k_norm_w, sinks,
                w_out, ffn_norm_w, w_router, b_router, w_up, b_up, w_down, b_down):
    b, T, _ = x.shape
    h = rmsnorm(x, attn_norm_w)
    proj = jnp.einsum('btd,de->bte', h, w_in)
    xin, bg, cg, q, k, v, g_conv, g_attn = jnp.split(proj, list(np.cumsum(IN_SPLITS)[:-1]), axis=-1)
    conv_out, conv_state = causal_short_conv(cg * xin, conv_prefix, conv_w)
    y_conv = bg * conv_out
    q = rmsnorm(q.reshape(b, T, N_HEADS, HEAD_DIM), q_norm_w)
    k = rmsnorm(k.reshape(b, T, N_KV, HEAD_DIM), k_norm_w)
    v = v.reshape(b, T, N_KV, HEAD_DIM)
    if k_past is None:
        y_attn, k_new, v_new = window_attention_prompt(q, k, v, rel_bias, sinks)
    else:
        y_attn, k_new, v_new = window_attention_sample(q, k, v, k_past, v_past, rel_bias, sinks)
    merged = jax.nn.sigmoid(g_conv) * y_conv + jax.nn.sigmoid(g_attn) * y_attn
    x = x + jnp.einsum('bte,ed->btd', merged, w_out)
    h2 = rmsnorm(x, ffn_norm_w)
    x = x + moe_ffn(h2.reshape(b * T, D_MODEL), w_router, b_router, w_up, b_up, w_down, b_down).reshape(b, T, D_MODEL)
    return x, conv_state, k_new, v_new

def setup_inputs(seed: int = 0) -> dict:
    key = jax.random.key(seed)
    ks = jax.random.split(key, 24)

    def nrm(k, shape, s):
        return jax.random.normal(k, shape, jnp.float32) * s

    win_buf = min(WINDOW, PAST_LEN)
    return {
        'x_prompt': nrm(ks[0], (BATCH, SEQ, D_MODEL), 1.0),
        'x_sample': nrm(ks[1], (DEC_BATCH, DEC_SEQ, D_MODEL), 1.0),
        'state_conv': nrm(ks[2], (DEPTH, DEC_BATCH, CONV_W - 1, CONV_DIM), 1.0),
        'cache_k_win': nrm(ks[3], (DEPTH, DEC_BATCH, win_buf, N_KV, HEAD_DIM), 1.0),
        'cache_v_win': nrm(ks[4], (DEPTH, DEC_BATCH, win_buf, N_KV, HEAD_DIM), 1.0),
        'rel_bias': nrm(ks[5], (N_BUCKETS, N_HEADS), 0.5),
        'attn_norm_w': 1.0 + nrm(ks[6], (DEPTH, D_MODEL), 0.01),
        'w_in': nrm(ks[7], (DEPTH, D_MODEL, IN_DIM), D_MODEL ** -0.5),
        'conv_w': nrm(ks[8], (DEPTH, CONV_W, CONV_DIM), CONV_W ** -0.5),
        'q_norm_w': 1.0 + nrm(ks[9], (DEPTH, HEAD_DIM), 0.01),
        'k_norm_w': 1.0 + nrm(ks[10], (DEPTH, HEAD_DIM), 0.01),
        'sinks': nrm(ks[11], (DEPTH, N_HEADS), 0.5),
        'w_out': nrm(ks[12], (DEPTH, D_MODEL, D_MODEL), D_MODEL ** -0.5),
        'ffn_norm_w': 1.0 + nrm(ks[13], (DEPTH, D_MODEL), 0.01),
        'w_router': nrm(ks[14], (DEPTH, D_MODEL, N_EXPERTS), D_MODEL ** -0.5),
        'b_router': nrm(ks[15], (DEPTH, N_EXPERTS), 0.01),
        'w_up': nrm(ks[16], (DEPTH, N_EXPERTS, D_MODEL, 2 * D_EXPERT), D_MODEL ** -0.5),
        'b_up': nrm(ks[17], (DEPTH, N_EXPERTS, 2 * D_EXPERT), 0.01),
        'w_down': nrm(ks[18], (DEPTH, N_EXPERTS, D_EXPERT, D_MODEL), D_EXPERT ** -0.5),
        'b_down': nrm(ks[19], (DEPTH, N_EXPERTS, D_MODEL), 0.01),
    }

def reference(x_prompt, x_sample, state_conv, cache_k_win, cache_v_win, rel_bias, attn_norm_w, w_in, conv_w,
              q_norm_w, k_norm_w, sinks, w_out, ffn_norm_w, w_router, b_router, w_up, b_up, w_down, b_down):
    xp, xs = x_prompt, x_sample
    p_conv, p_k, p_v, s_conv, s_k, s_v = [], [], [], [], [], []
    for l in range(DEPTH):
        lw = (attn_norm_w[l], w_in[l], conv_w[l], q_norm_w[l], k_norm_w[l], sinks[l], w_out[l],
              ffn_norm_w[l], w_router[l], b_router[l], w_up[l], b_up[l], w_down[l], b_down[l])
        zero_prefix = jnp.zeros((xp.shape[0], CONV_W - 1, CONV_DIM), xp.dtype)
        xp, c1, k1, v1 = trunk_layer(xp, zero_prefix, None, None, rel_bias, *lw)
        xs, c2, k2, v2 = trunk_layer(xs, state_conv[l], cache_k_win[l], cache_v_win[l], rel_bias, *lw)
        p_conv.append(c1); p_k.append(k1); p_v.append(v1)
        s_conv.append(c2); s_k.append(k2); s_v.append(v2)
    return (xp, xs, jnp.stack(p_conv), jnp.stack(p_k), jnp.stack(p_v), jnp.stack(s_conv), jnp.stack(s_k), jnp.stack(s_v))


_drawn_inputs = setup_inputs


def setup_inputs(seed=0):
    import zlib

    import numpy as np

    out = dict(_drawn_inputs(seed))
    spreads = {}
    factors = {'q_norm_w': 8.0,
     'k_norm_w': 4.485,
     'sinks': 41.36,
     'b_up': 8.0,
     'b_down': 8.0,
     'b_router': 2.928}
    for name, (base, spread) in spreads.items():
        noise = np.random.default_rng([zlib.crc32(name.encode()), seed]).standard_normal(out[name].shape)
        drawn = base * np.exp(spread * noise) if base else spread * noise
        out[name] = __import__('jax').numpy.asarray(drawn.astype(out[name].dtype))
    for name, factor in factors.items():
        out[name] = (out[name] * factor).astype(out[name].dtype)
    return out
```

```python
from contextlib import ExitStack

import numpy as np

import concourse.bass as bass
from concourse import mybir
from concourse.alu_op_type import AluOpType as ALU

F32 = mybir.dt.float32
BF16 = mybir.dt.bfloat16
I32 = mybir.dt.int32
ACT = mybir.ActivationFunctionType
AX = mybir.AxisListType

D = 1024
SEQ, DEC = 256, 8
NT = SEQ + DEC
KT = D // 128
HD, NKV, GROUP = 64, 2, 8
NH = NKV * GROUP
WIN = 128
NBUCKET, MAXDIST = 32, 128
NE, TOPK = 32, 4
FF = 1024
EPS = 1e-5
NEG = -1e30
ALPHA, LIMIT = 1.702, 7.0

TOK = [(0, 128), (128, 128), (256, DEC)]
CAP = 64
PASSES = -(-NT // CAP)
PAIRS = NE // 2

SLOTS = 6
SLOT = 4096
W_IN_CHUNKS, W_OUT_CHUNKS = 13, 2
FIRST_CHUNKS = W_IN_CHUNKS + W_OUT_CHUNKS
UP_CHUNKS, DOWN_CHUNKS = KT, KT // 2
PAIR_CHUNKS = UP_CHUNKS + DOWN_CHUNKS

XIN, BG, CG, QC, KC_, VC_, GC, GA = 0, 1024, 2048, 3072, 4096, 4224, 4352, 5376

C_ID, C_BLK, C_TRI, C_ONE, C_IOTA, C_BUCKET, C_SEL, C_VALID, C_EPS, C_N = 0, 128, 256, 384, 512, 576, 704, 736, 739, 740

V_ANORM, V_FNORM, V_CONV, V_QN, V_KN, V_N = 0, 8, 16, 40, 41, 42


def constants():
    c = np.zeros((128, C_N), np.float32)
    p = np.arange(128)
    c[:, C_ID:C_ID + 128] = np.eye(128)
    c[:, C_BLK:C_BLK + 128] = (p[:, None] // HD) == (p[None, :] // HD)
    c[:, C_TRI:C_TRI + 128] = p[:, None] < p[None, :]
    c[:, C_ONE:C_ONE + 128] = 1.0
    c[:, C_IOTA:C_IOTA + CAP] = np.arange(CAP)
    rel = 127 - np.arange(128)
    exact = NBUCKET // 2
    far = exact + (np.log(np.maximum(rel, 1).astype(np.float32) / np.float32(exact))
                   / np.float32(np.log(MAXDIST / exact)) * np.float32(NBUCKET - exact)).astype(np.int32)
    bucket = np.where(rel < exact, rel, np.minimum(far, NBUCKET - 1))
    c[0:NBUCKET, C_BUCKET:C_BUCKET + 128] = bucket[None, :] == np.arange(NBUCKET)[:, None]
    c[0:96, C_SEL:C_SEL + NE] = (p[0:96, None] % NE) == np.arange(NE)[None, :]
    for m, (_, n) in enumerate(TOK):
        c[0:n, C_VALID + m] = 1.0
    c[:, C_EPS] = EPS
    return c


def tile_list():
    tiles = [("k", 0, 0, 0), ("v", 0, 1, 0)]
    groups = [("q", 0), ("q", 1), ("cg", 0), ("xin", 0), ("bg", 0), ("gc", 0),
              ("cg", 1), ("xin", 1), ("bg", 1), ("gc", 1), ("ga", 0), ("ga", 1)]
    for c, (kind, half) in enumerate(groups):
        tiles += [(kind, c + 1, j, 4 * half + j) for j in range(4)]
    return tiles


TILES = tile_list()
CHUNK_COL = {"q": QC, "cg": CG, "xin": XIN, "bg": BG, "gc": GC, "ga": GA}
UNITS = [(0, 0), (1, 0), (0, 4), (1, 4)]


def plan():
    after = {n: [] for n in range(len(TILES))}
    for j in range(9):
        n = 0 if j == 0 else j + 1
        after[n + 1].append(("square", j))
        after[n + 2].append(("qknorm", j))
    after[3].append(("v_rows", 0))
    after[4].append(("k_rows", 0))
    after[5].append(("state_cols", 0))
    after[7].append(("cache_cols", 0))
    after[8].append(("cache_cols", 1))
    for u in range(len(UNITS)):
        n = 11 + 7 * u
        for d, what in ((0, "scores"), (1, "bias"), (2, "exp"), (3, "norm"), (5, "turn"), (6, "values")):
            after[n + d].append((what, u))
    for n, what in ((12, "s_scores"), (14, "s_bias"), (16, "s_norm"), (19, "s_turn"), (21, "s_values")):
        after[n].append((what, 0))
    after[34].append(("conv_rows", 0))
    after[36].append(("conv_rows", 1))
    steps = [("vectors", 0), ("bias_table", 0)] + [("h_cols", k) for k in range(KT)]
    for n in range(len(TILES)):
        steps.append(("tile", n))
        steps += after[n]
    return steps


STEPS = plan()

FILLS_OF = {"tile": 0, "qknorm": 0, "scores": 0, "bias": 0, "exp": 0, "norm": 0, "turn": 0, "s_norm": 0, "s_scores": 2}
FILL, _n = {}, 0
for _s in STEPS + [("h2_cols", k) for k in range(KT)] + [("logits", 0), ("route", 0), ("gather", 0), ("gather", 1)]:
    _n += FILLS_OF.get(_s[0], 1)
    FILL[_s] = _n
PRE_FILLS = _n
PAIR_FILLS = 11

BY_ACT = ("cg", "gc", "ga")
ACT_TILES = [sum(t[0] in BY_ACT for t in TILES[:n]) for n in range(len(TILES) + 1)]
DVE_TILES = [sum(t[0] not in BY_ACT for t in TILES[:n]) for n in range(len(TILES) + 1)]
XIN_END = [18, 34]
BIAS_STEPS = 2 * (1 + 2 * 3)
VECS = 2 + 3 + 4 + 2 + 2 * DEC


class Count:

    def __init__(self, sem, base=0):
        self.sem, self.n = sem, base

    def next(self):
        self.n = self.n + 1
        return self.n


def build(nc, x_prompt, x_sample, state_conv, cache_k, cache_v, rel_bias, attn_norm_w, w_in, conv_w, q_norm_w,
          k_norm_w, sinks, w_out, ffn_norm_w, w_router, b_router, w_up, b_up, w_down, b_down, consts,
          y_prompt, y_sample, conv_prompt, k_prompt, v_prompt, conv_sample, k_sample, v_sample):
    with ExitStack() as ctx:
        def sb(name, shape, dt=F32):
            return ctx.enter_context(nc.sbuf_tensor(name, shape, dt))

        def sem(name):
            return ctx.enter_context(nc.semaphore(name))

        ring = sb("ring", [128, SLOTS, SLOT])
        x = sb("x", [128, 3, D])
        hn = sb("hn", [128, 3, D])
        cst = sb("cst", [128, C_N])
        rows = sb("rows", [128, 128])
        cols = sb("cols", [128, V_N])
        rb = sb("rb", [NBUCKET, NH])
        brouter = sb("brouter", [NE, 1])
        sink = sb("sink", [128, NKV, GROUP])
        ssink = sb("ssink", [128, 1])
        conv_row = sb("conv_row", [128, D])
        state_c = sb("state_c", [128, KT, DEC, 2])
        v_row = sb("v_row", [128, 3, 128])
        k_row = sb("k_row", [128, 2, 128])
        tmp = sb("tmp", [128, 2, NT])
        rt = sb("rt", [128, NT])
        stat = sb("stat", [128, 64])
        flag = sb("flag", [1, 4], I32)

        AREA = 8 * NT * 4 + KT * (NT + 2) + 2 * NT + 3 * 2048
        area = sb("area", [128, AREA])

        class Area:
            def __init__(self, at):
                self.at = at

            def take(self, n):
                self.at += n
                assert self.at <= AREA
                return area[:, self.at - n:self.at]

        one = Area(0)
        hT = one.take(KT * NT).rearrange("p (k n) -> p k n", k=KT)
        yc = one.take(KT * NT).rearrange("p (k n) -> p k n", k=KT)
        ya = one.take(KT * NT).rearrange("p (k n) -> p k n", k=KT)
        cx = one.take(KT * (NT + 2)).rearrange("p (k n) -> p k n", k=KT)
        kT = one.take(NT)
        vT = one.take(NT)
        qT = one.take(KT * NT).rearrange("p (k n) -> p k n", k=KT)
        table = one.take(2048).rearrange("p (h s) -> p h s", h=8)
        prob = one.take(2048).rearrange("p (h s) -> p h s", h=8)
        probT = one.take(2048).rearrange("p (b h q) -> p b h q", b=2, h=8)
        hn_flat = hn[:].rearrange("p m d -> p (m d)")
        k_cache = hn_flat[:, 0:1024].rearrange("p (b f) -> p b f", b=DEC)
        v_cache = hn_flat[:, 1024:2048].rearrange("p (b f) -> p b f", b=DEC)
        k_cacheT = hn_flat[:, 2048:3072].rearrange("p (b s) -> p b s", b=DEC)
        stab = sb("stab", [128, WIN])
        sprob = sb("sprob", [128, WIN])
        sprobT = sb("sprobT", [128, 128])

        two = Area(2 * KT * NT)
        xsT = two.take(1024).rearrange("p (k s) -> p k s", k=KT)
        act_out = two.take(FF)
        aT = two.take(1024).rearrange("p (k s) -> p k s", k=KT)
        y_pair = two.take(D)
        glu = two.take(FF)
        lin = two.take(FF)
        pick = two.take(3 * 128).rearrange("p (m e s) -> p m e s", m=3, e=2)
        gateT = two.take(NT)
        two.at = 3 * KT * NT + KT * (NT + 2) + 2 * NT + KT * NT
        sig = two.take(FF)
        gpick = two.take(3 * 128).rearrange("p (m e s) -> p m e s", m=3, e=2)
        NPOS = PASSES * NE + 2
        pos = two.take(3 * NPOS).rearrange("p (m e) -> p m e", m=3)
        sel = two.take(64).bitcast(BF16).rearrange("p (e s) -> p e s", e=2)
        bias_up = two.take(FF).bitcast(BF16)
        bias_down = two.take(D // 2).bitcast(BF16)
        bias_raw = two.take(2 * FF)

        lg = sb("lg", [128, 3, NE])
        mask = sb("mask", [128, 3, NE])
        t32 = sb("t32", [128, 3, NE])
        gate = sb("gate", [128, 3, NE])
        top8 = sb("top8", [128, 3, 8])
        lgT = rt
        flag_f32 = sb("flag_f32", [1, 1])
        rev_sb = prob.rearrange("p h s -> p (h s)")[0:NH, 0:3 * WIN]

        ident = cst[:, C_ID:C_ID + 128]

        pA = ctx.enter_context(nc.psum_tensor("pA", [128, 2048], F32))
        pB = ctx.enter_context(nc.psum_tensor("pB", [128, 2, 512], F32))
        pM = ctx.enter_context(nc.psum_tensor("pM", [128, 2, 512], F32))

        rev_dram = nc.dram_tensor("rev_scratch", (128, NH * 3 * WIN), F32, kind="Internal")

        x_loaded = sem("x_loaded")
        consts_loaded = sem("consts_loaded")
        vecs_loaded = sem("vecs_loaded")
        ring_full = [sem(f"ring_full{s}") for s in range(SLOTS)]
        ring_free = sem("ring_free")
        dve_step = sem("dve_step")
        bias_split = sem("bias_split")
        misc_full = sem("misc_full")
        misc_free = sem("misc_free")
        tile_full = sem("tile_full")
        tile_free_dve = sem("tile_free_dve")
        tile_free_act = sem("tile_free_act")
        norm_sq = sem("norm_sq")
        norm_in = sem("norm_in")
        norm_rt = sem("norm_rt")
        h_ready = sem("h_ready")
        sq_ready = sem("sq_ready")
        qk_normed = sem("qk_normed")
        rt_out = sem("rt_out")
        rev_stored = sem("rev_stored")
        table_loaded = sem("table_loaded")
        stab_loaded = sem("stab_loaded")
        cache_loaded = sem("cache_loaded")
        vnew_loaded = sem("vnew_loaded")
        state_loaded = sem("state_loaded")
        scores_full = sem("scores_full")
        prob_biased = sem("prob_biased")
        exp_done = sem("exp_done")
        prob_ready = sem("prob_ready")
        turned = sem("turned")
        probT_ready = sem("probT_ready")
        sexp_in = sem("sexp_in")
        sexp_done = sem("sexp_done")
        sprob_ready = sem("sprob_ready")
        cg_ready = sem("cg_ready")
        sig_gate = sem("sig_gate")
        sig_used = sem("sig_used")
        merged = sem("merged")
        out_full = sem("out_full")
        router_full = sem("router_full")
        router_ready = sem("router_ready")
        wr_loaded = sem("wr_loaded")
        ex_in = sem("ex_in")
        ex_out = sem("ex_out")
        route_ready = sem("route_ready")
        bias_loaded = sem("bias_loaded")
        pick_ready = sem("pick_ready")
        gpick_ready = sem("gpick_ready")
        sel_ready = sem("sel_ready")
        up_done = sem("up_done")
        glu_ready = sem("glu_ready")
        sig_ready = sem("sig_ready")
        a_ready = sem("a_ready")
        down_done = sem("down_done")
        y_ready = sem("y_ready")
        moe_done = sem("moe_done")
        stored = sem("stored")
        final_stored = sem("final_stored")

        w_router_sb = sb("w_router_sb", [128, KT, NE])
        block = ctx.enter_context(nc.Block())

        def w_in_chunk(c):
            w = w_in.rearrange("(k p) n -> p k n", p=128)
            if c == 0:
                return [(ring[:, 0, 0:2048].rearrange("p (k h n) -> p k h n", k=KT, h=2)[:, :, h],
                         w[:, :, KC_ + 128 * h:KC_ + 128 * h + 128]) for h in range(2)]
            kind, _, _, t = TILES[2 + 4 * (c - 1)]
            col = CHUNK_COL[kind] + t * HD
            dst = ring[:, c % SLOTS, :].rearrange("p (k h n) -> p k h n", k=KT, h=2)
            return [(dst[:, :, h], w[:, :, col + 512 * h:col + 512 * h + 256]) for h in range(2)]

        def filled(c):
            return 32 * (c // SLOTS + 1)

        @block.sync
        def _(sp):
            for c in range(FIRST_CHUNKS):
                if c >= SLOTS:
                    sp.wait_ge(ring_free, c - SLOTS + 1)
                if c < W_IN_CHUNKS:
                    parts = w_in_chunk(c)
                else:
                    k0 = 4 * (c - W_IN_CHUNKS)
                    wo = w_out.rearrange("(h t c) n -> h c t n", h=2, c=HD)
                    dst = ring[:, c % SLOTS, :].rearrange("p (t n) -> p t n", t=4)
                    parts = [(dst[HD * h:HD * h + HD], wo[h, :, k0:k0 + 4, :]) for h in range(2)]
                for dst, src in parts:
                    sp.dma_start(dst, src).then_inc(ring_full[c % SLOTS], 16)

            up = w_up.rearrange("(i e) (k p) n -> e k i p n", e=2, p=128)
            down = w_down.rearrange("(i e) (k t p) n -> e k i p t n", e=2, t=2, p=128)

            def pair(g, i):
                for j in range(PAIR_CHUNKS):
                    c = FIRST_CHUNKS + j
                    sp.wait_ge(ring_free, PAIR_CHUNKS * g + (c - SLOTS + 1))
                    for e in range(2):
                        if j < UP_CHUNKS:
                            dst = ring[:, c % SLOTS, e * 2048:(e + 1) * 2048]
                            src = up[e, j, bass.ds(i, 1)].rearrange("a p n -> (a p) n")
                        else:
                            dst = ring[:, c % SLOTS, e * 2048:(e + 1) * 2048].rearrange("p (t n) -> p t n", t=2)
                            src = down[e, j - UP_CHUNKS, bass.ds(i, 1)].rearrange("a p t n -> (a p) t n")
                        sp.dma_start(dst, src).then_inc(ring_full[c % SLOTS], 16)

            with sp.Fori(0, PAIRS) as i:
                pair(i, i)
            sp.wait_ge(misc_free, FILL["route", 0])
            over = sp.value_load(flag[0:1, 0:1], min_val=0, max_val=1)
            with sp.If(over > 0):
                with sp.Fori(1, PASSES) as q:
                    with sp.Fori(0, PAIRS) as i:
                        pair(q * PAIRS + i, i)
            sp.wait_ge(moe_done, 1)
            for m in range(2):
                sp.dma_start(y_prompt[0, 128 * m:128 * m + 128, :], x[:, m, :]).then_inc(final_stored, 16)
            sp.dma_start(y_sample.rearrange("b t d -> (b t) d"), x[0:DEC, 2, :]).then_inc(final_stored, 16)
            sp.wait_ge(final_stored, 48)

        @block.gpsimd
        def _(pool):
            step = Count(bias_split)

            def link(ins):
                ins.then_inc(bias_split, 1)
                pool.wait_ge(bias_split, step.next())

            for h in range(2):
                pool.dma_start(conv_row[0:2 * DEC, :].rearrange("r (t h c) -> r t h c", t=KT, h=2)[:, :, h, :],
                               state_conv.rearrange("b j (h t c) -> h (b j) t c", h=2, c=HD)[h]).then_inc(state_loaded, 16)
            pool.dma_start(conv_sample[0, :, 0, :], state_conv[:, 1, :]).then_inc(stored, 16)
            pool.dma_start(k_sample[0, :, 0:WIN - 1].rearrange("b s h d -> b (s h d)"),
                           cache_k[:, 1:WIN].rearrange("b s h d -> b (s h d)")).then_inc(stored, 16)
            pool.dma_start(v_sample[0, :, 0:WIN - 1].rearrange("b s h d -> b (s h d)"),
                           cache_v[:, 1:WIN].rearrange("b s h d -> b (s h d)")).then_inc(stored, 16)
            pool.dma_start(w_router_sb[:], w_router.rearrange("(k p) e -> p k e", p=128)).then_inc(wr_loaded, 16)
            pool.dma_start(brouter[:], b_router.rearrange("(e a) -> e a", a=1)).then_inc(wr_loaded, 16)
            pool.wait_ge(misc_free, FILL["bias_table", 0])
            pool.dma_start(rev_dram[:, :].rearrange("r (h m) -> h r m", h=NH),
                           rev_sb.unsqueeze(1).to_broadcast([NH, 128, 3 * WIN])).then_inc(rev_stored, 16)
            pool.wait_ge(rev_stored, 16)

            def load_table(t0):
                for kv in range(NKV):
                    h0 = kv * GROUP + t0
                    src = bass.AP(rev_dram, h0 * 3 * WIN + WIN - 1, [[NH * 3 * WIN - 1, 128], [3 * WIN, 4], [1, 2 * WIN]])
                    pool.dma_start(table[:, 4 * kv:4 * kv + 4, :], src).then_inc(table_loaded, 16)

            load_table(0)
            for kv in range(NKV):
                for b in range(DEC):
                    p = kv * 64 + b * 8
                    pool.dma_start(stab[p:p + 8, :],
                                   rev_dram[0:1, :].rearrange("r (h m) -> (r h) m", h=NH)[
                                       kv * GROUP:(kv + 1) * GROUP, WIN:2 * WIN]).then_inc(stab_loaded, 16)
            pool.wait_ge(misc_free, FILL["h_cols", KT - 1])
            pool.dma_start(k_cache[0:WIN - 1], cache_k[:, 1:WIN].rearrange("b s h d -> s b (h d)")).then_inc(cache_loaded, 16)
            pool.dma_start(v_cache[0:WIN - 1], cache_v[:, 1:WIN].rearrange("b s h d -> s b (h d)")).then_inc(cache_loaded, 16)
            pool.wait_ge(misc_free, FILL["v_rows", 0])
            pool.dma_start(v_cache[WIN - 1:WIN], v_row[0:DEC, 2, :]).then_inc(vnew_loaded, 16)
            pool.dma_start(v_prompt[0, 0].rearrange("s h d -> s (h d)"), v_row[:, 1, :]).then_inc(stored, 16)
            pool.dma_start(v_sample[0, :, WIN - 1].rearrange("b h d -> b (h d)"), v_row[0:DEC, 2, :]).then_inc(stored, 16)
            pool.wait_ge(misc_free, FILL["k_rows", 0])
            pool.dma_start(k_prompt[0, 0].rearrange("s h d -> s (h d)"), k_row[:, 0, :]).then_inc(stored, 16)
            pool.dma_start(k_sample[0, :, WIN - 1].rearrange("b h d -> b (h d)"), k_row[0:DEC, 1, :]).then_inc(stored, 16)
            pool.wait_ge(prob_biased, 2)
            load_table(4)
            pool.wait_ge(misc_free, FILL["conv_rows", 1])
            pool.dma_start(conv_prompt[0, 0], conv_row[0:2, :]).then_inc(stored, 16)
            pool.dma_start(conv_sample[0, :, 1, :], conv_row[2:2 + DEC, :]).then_inc(stored, 16)

            pool.wait_ge(misc_free, FILL["values", 3])
            loads = 0
            for src, parts, n in ((b_up, bias_up, 2 * FF), (b_down, bias_down, D)):
                raw = bias_raw[:, 0:n]
                for j in range(3):
                    pool.dma_start(raw[32 * j:32 * j + 32], src).then_inc(bias_loaded, 16)
                    loads += 16
                pool.wait_ge(bias_loaded, loads)
                link(pool.tensor_copy(parts[0:96, :], raw[0:96]))
                for j in (1, 2):
                    for r in range(j, 3):
                        s = slice(32 * r, 32 * r + 32)
                        link(pool.tensor_tensor(raw[s], raw[s], parts[s, :], ALU.subtract))
                        link(pool.tensor_copy(parts[s, :], raw[s]))
            pool.wait_ge(stored, 16 * 9)

        @block.scalar
        def _(act):
            act.dma_start(x[:, 0:2, :], x_prompt[0].rearrange("(m p) d -> p m d", p=128)).then_inc(x_loaded, 16)
            act.dma_start(x[0:DEC, 2, :], x_sample.rearrange("b t d -> (b t) d")).then_inc(x_loaded, 16)
            act.dma_start(cst[:], consts).then_inc(consts_loaded, 16)
            act.dma_start(rows[V_ANORM:V_ANORM + KT, :], attn_norm_w.rearrange("(k p) -> k p", p=128)).then_inc(vecs_loaded, 16)
            act.dma_start(rows[V_FNORM:V_FNORM + KT, :], ffn_norm_w.rearrange("(k p) -> k p", p=128)).then_inc(vecs_loaded, 16)
            for j in range(3):
                act.dma_start(rows[V_CONV + 8 * j:V_CONV + 8 * j + 8, :].rearrange("t (h c) -> t h c", h=2),
                              conv_w[j].rearrange("(h t c) -> t h c", h=2, c=HD)).then_inc(vecs_loaded, 16)
            for h in range(2):
                act.dma_start(rows[V_QN:V_QN + 1, HD * h:HD * h + HD], q_norm_w.rearrange("(a d) -> a d", a=1)).then_inc(vecs_loaded, 16)
                act.dma_start(rows[V_KN:V_KN + 1, HD * h:HD * h + HD], k_norm_w.rearrange("(a d) -> a d", a=1)).then_inc(vecs_loaded, 16)
            act.dma_start(rb[:], rel_bias).then_inc(vecs_loaded, 16)
            act.dma_start(sink[:].rearrange("p a b -> p (a b)"),
                          bass.AP(sinks.tensor, sinks.offset, [[0, 128], [1, NH]])).then_inc(vecs_loaded, 16)
            for kv in range(NKV):
                for b in range(DEC):
                    p = kv * 64 + b * 8
                    act.dma_start(ssink[p:p + 8, :],
                                  sinks[kv * GROUP:(kv + 1) * GROUP].rearrange("(e a) -> e a", a=1)).then_inc(vecs_loaded, 16)

            act.wait_ge(x_loaded, 32)
            act.wait_ge(norm_in, 1)
            for m, (_, r) in enumerate(TOK):
                ins = nc.scalar.activation(hn[0:r, m, :], x[0:r, m, :], ACT.Square, accum_out=stat[0:r, m:m + 1])
            ins.then_inc(norm_sq, 1)
            act.wait_ge(norm_in, 2)
            nc.scalar.activation(stat[:, 4:7], stat[:, 4:7], ACT.Sqrt).then_inc(norm_rt, 1)

            sigs = 0
            for what, a in STEPS:
                if what == "square":
                    act.wait_ge(tile_free_dve, 1 if a == 0 else a + 2)
                    if a >= 2:
                        act.wait_ge(misc_free, FILL["square", a - 2])
                    src = kT if a == 0 else qT[:, a - 1, :]
                    nc.scalar.activation(tmp[:, a % 2, :], src, ACT.Square).then_inc(sq_ready, 1)
                elif what == "qknorm":
                    act.wait_ge(misc_free, FILL["square", a])
                    nc.scalar.activation(rt[:], rt[:], ACT.Sqrt).then_inc(rt_out, 1)
                elif what == "tile":
                    kind, _, _, t = TILES[a]
                    if kind == "cg":
                        act.wait_ge(tile_full, a + 1)
                        nc.scalar.activation(cx[:, t, 2:], pB[:, a % 2, 0:NT], ACT.Copy).then_inc(tile_free_act, 1)
                    elif kind in ("gc", "ga"):
                        act.wait_ge(tile_full, a + 1)
                        if sigs >= 2:
                            act.wait_ge(sig_used, sigs - 1)
                        else:
                            act.wait_ge(misc_free, FILL["square", 8])
                        nc.scalar.activation(tmp[:, sigs % 2, :], pB[:, a % 2, 0:NT],
                                             ACT.Sigmoid).then_inc(tile_free_act, 1)
                        sigs += 1
                elif what == "exp":
                    keys = WIN * (UNITS[a][0] + 1)
                    act.wait_ge(prob_biased, a + 1)
                    for h in range(8):
                        nc.scalar.activation(prob[:, h, 0:keys], prob[:, h, 0:keys], ACT.Exp,
                                             bias=stat[:, 16 + h:17 + h], accum_out=stat[:, 24 + h:25 + h])
                    nc.scalar.activation(stat[:, 32:40], stat[:, 32:40], ACT.Exp).then_inc(exp_done, 1)
                elif what == "turn":
                    blocks = UNITS[a][0] + 1
                    act.wait_ge(turned, a + 1)
                    if a:
                        act.wait_ge(misc_free, FILL["values", a - 1])
                    for b in range(blocks):
                        ins = nc.scalar.activation(probT[:, b].rearrange("p h q -> p (h q)"),
                                                   pA[:, b * 1024:(b + 1) * 1024], ACT.Copy)
                    ins.then_inc(probT_ready, 1)
                elif what == "s_bias":
                    act.wait_ge(sexp_in, 1)
                    nc.scalar.activation(sprob[:], sprob[:], ACT.Exp, bias=stat[:, 48:49], accum_out=stat[:, 49:50])
                    nc.scalar.activation(stat[:, 50:51], stat[:, 50:51], ACT.Exp).then_inc(sexp_done, 1)

            act.wait_ge(norm_in, 3)
            for m, (_, r) in enumerate(TOK):
                ins = nc.scalar.activation(hn[0:r, m, :], x[0:r, m, :], ACT.Square, accum_out=stat[0:r, m:m + 1])
            ins.then_inc(norm_sq, 1)
            act.wait_ge(norm_in, 4)
            nc.scalar.activation(stat[:, 4:7], stat[:, 4:7], ACT.Sqrt).then_inc(norm_rt, 1)
            act.wait_ge(ex_in, 1)
            nc.scalar.activation(gate[:], gate[:], ACT.Exp).then_inc(ex_out, 1)

            def pair(g, i):
                act.wait_ge(glu_ready, g + 1)
                nc.scalar.activation(sig, glu, ACT.Sigmoid, scale=ALPHA).then_inc(sig_ready, 1)
                act.wait_ge(down_done, g + 1)
                nc.scalar.activation(y_pair[:, 0:512], pB[:, 0, :], ACT.Copy)
                nc.scalar.activation(y_pair[:, 512:1024], pB[:, 1, :], ACT.Copy).then_inc(y_ready, 1)

            with act.Fori(0, PAIRS) as i:
                pair(i, i)
            act.wait_ge(misc_free, FILL["route", 0])
            over = act.value_load(flag[0:1, 0:1], min_val=0, max_val=1)
            with act.If(over > 0):
                with act.Fori(1, PASSES) as q:
                    with act.Fori(0, PAIRS) as i:
                        pair(q * PAIRS + i, i)

        @block.vector
        def _(dve):
            V = nc.vector
            step = Count(dve_step)

            def link(ins):
                ins.then_inc(dve_step, 1)
                dve.wait_ge(dve_step, step.next())

            misc = Count(misc_full)

            def misc_bank():
                n = misc.next()
                dve.wait_ge(misc_full, n)
                return pM[:, (n - 1) % 2, :]

            def normalise(n):
                dve.wait_ge(norm_sq, n + 1)
                V.tensor_scalar(stat[:, 4:7], stat[:, 0:3], 1.0 / D, EPS, ALU.mult, ALU.add).then_inc(norm_in, 1)
                dve.wait_ge(norm_rt, n + 1)
                link(V.reciprocal(stat[:, 8:11], stat[:, 4:7]))
                for m, (_, r) in enumerate(TOK):
                    V.tensor_scalar(hn[0:r, m, :], x[0:r, m, :], stat[0:r, 8 + m:9 + m], None,
                                    ALU.mult).then_inc(h_ready, 1)

            V.memset(stat[:], 0.0).then_inc(norm_in, 1)
            V.memset(cx[:, :, 0:2], 0.0)
            V.memset(lg[:], 0.0)
            link(V.memset(rev_sb, NEG))
            normalise(0)

            freed = 0
            for what, a in STEPS:
                if what == "vectors":
                    V.tensor_copy(cols[:], misc_bank()[:, 0:V_N]).then_inc(misc_free, 1)
                elif what == "bias_table":
                    b = misc_bank()
                    V.tensor_copy(rev_sb[:, WIN:2 * WIN], b[0:NH, 0:128]).then_inc(misc_free, 1)
                elif what == "h_cols":
                    if a == 0:
                        dve.wait_ge(misc_free, 1)
                    V.tensor_scalar(hT[:, a, :], misc_bank()[:, 0:NT], cols[:, V_ANORM + a:V_ANORM + a + 1], None,
                                    ALU.mult).then_inc(misc_free, 1)
                elif what == "tile":
                    kind, _, _, t = TILES[a]
                    src = pB[:, a % 2, 0:NT]
                    if kind in ("k", "q", "v"):
                        dve.wait_ge(tile_full, a + 1)
                        dst = {"k": kT, "v": vT, "q": qT[:, t, :]}[kind]
                        V.tensor_copy(dst, src).then_inc(tile_free_dve, 1)
                    elif kind == "xin":
                        dve.wait_ge(tile_full, a + 1)
                        dve.wait_ge(tile_free_act, ACT_TILES[a])
                        V.tensor_tensor(cx[:, t, 2:], src, cx[:, t, 2:], ALU.mult).then_inc(tile_free_dve, 1)
                        dve.wait_ge(tile_free_dve, DVE_TILES[a] + 1)
                        w = [cols[:, V_CONV + 8 * j + t:V_CONV + 8 * j + t + 1] for j in range(3)]
                        taps = [cx[:, t, j:j + SEQ] for j in range(3)]
                        s_taps = [state_c[:, t, :, 0], state_c[:, t, :, 1], cx[:, t, 2 + SEQ:]]
                        V.tensor_scalar(yc[:, t, 0:SEQ], taps[0], w[0], None, ALU.mult)
                        link(V.tensor_scalar(yc[:, t, SEQ:], s_taps[0], w[0], None, ALU.mult))
                        for j in (1, 2):
                            V.scalar_tensor_tensor(out=yc[:, t, 0:SEQ], in0=taps[j], scalar=w[j],
                                                   in1=yc[:, t, 0:SEQ], op0=ALU.mult, op1=ALU.add)
                            link(V.scalar_tensor_tensor(out=yc[:, t, SEQ:], in0=s_taps[j], scalar=w[j],
                                                        in1=yc[:, t, SEQ:], op0=ALU.mult, op1=ALU.add))
                    elif kind == "bg":
                        dve.wait_ge(tile_full, a + 1)
                        V.tensor_tensor(yc[:, t, :], src, yc[:, t, :], ALU.mult).then_inc(tile_free_dve, 1)
                    elif kind == "gc":
                        dve.wait_ge(tile_free_act, ACT_TILES[a] + 1)
                        dve.wait_ge(tile_free_dve, DVE_TILES[a])
                        V.tensor_tensor(yc[:, t, :], tmp[:, freed % 2, :], yc[:, t, :], ALU.mult).then_inc(sig_used, 1)
                        freed += 1
                    elif kind == "ga":
                        dve.wait_ge(tile_free_act, ACT_TILES[a] + 1)
                        dve.wait_ge(sig_used, freed)
                        dve.wait_ge(misc_free, misc.n)
                        g = tmp[:, freed % 2, :]
                        link(V.tensor_tensor(g, g, ya[:, t, :], ALU.mult))
                        V.tensor_tensor(yc[:, t, :], g, yc[:, t, :], ALU.add).then_inc(sig_used, 1)
                        freed += 1
                elif what == "square":
                    b = misc_bank()
                    if a:
                        dve.wait_ge(qk_normed, a)
                    V.tensor_scalar(rt[:], b[:, 0:NT], 1.0 / HD, EPS, ALU.mult, ALU.add).then_inc(misc_free, 1)
                elif what == "qknorm":
                    dve.wait_ge(rt_out, a + 1)
                    link(V.reciprocal(rt[:], rt[:]))
                    dst, w = (kT, V_KN) if a == 0 else (qT[:, a - 1, :], V_QN)
                    V.scalar_tensor_tensor(out=dst, in0=dst, scalar=cols[:, w:w + 1], in1=rt[:],
                                           op0=ALU.mult, op1=ALU.mult).then_inc(qk_normed, 1)
                elif what == "v_rows":
                    b = misc_bank()
                    V.tensor_copy(v_row[0:DEC, 2, :], b[0:DEC, 256:384])
                    V.tensor_copy(v_row[:, 0:2, :].rearrange("p m f -> p (m f)"), b[:, 0:256]).then_inc(misc_free, 1)
                elif what == "k_rows":
                    b = misc_bank()
                    V.tensor_copy(k_row[0:DEC, 1, :], b[0:DEC, 128:256])
                    V.tensor_copy(k_row[:, 0, :], b[:, 0:128]).then_inc(misc_free, 1)
                elif what == "state_cols":
                    V.tensor_copy(state_c[:].rearrange("p k b j -> p (k b j)"),
                                  misc_bank()[:, 0:KT * 2 * DEC]).then_inc(misc_free, 1)
                elif what == "cache_cols":
                    b = misc_bank()
                    dve.wait_ge(qk_normed, 1)
                    V.tensor_copy(k_cacheT[:, 4 * a:4 * a + 4, 0:WIN - 1],
                                  b.rearrange("p (b s) -> p b s", b=4)[:, :, 0:WIN - 1])
                    V.tensor_copy(k_cacheT[:, 4 * a:4 * a + 4, WIN - 1],
                                  kT[:, SEQ + 4 * a:SEQ + 4 * a + 4]).then_inc(misc_free, 1)
                elif what == "bias":
                    q, t0 = UNITS[a]
                    keys = WIN * (q + 1)
                    dve.wait_ge(scores_full, a + 1)
                    dve.wait_ge(table_loaded, 32 * (a // 2 + 1))
                    if a:
                        dve.wait_ge(turned, a)
                    for kv in range(NKV):
                        ins = V.scalar_tensor_tensor(
                            out=prob[:, 4 * kv:4 * kv + 4, 0:keys],
                            in0=pA[:, 1024 * kv:1024 * kv + 4 * keys].rearrange("p (t s) -> p t s", t=4),
                            scalar=HD ** -0.5, in1=table[:, 4 * kv:4 * kv + 4, 2 * WIN - keys:],
                            op0=ALU.mult, op1=ALU.add)
                    link(ins)
                    link(V.tensor_reduce(stat[:, 16:24], prob[:, :, 0:keys], AX.X, ALU.max))
                    s = sink[:, :, t0:t0 + 4]
                    m = stat[:, 16:24].rearrange("p (a b) -> p a b", a=2)
                    link(V.tensor_tensor(m, m, s, ALU.max))
                    link(V.tensor_scalar(stat[:, 16:24], stat[:, 16:24], -1.0, None, ALU.mult))
                    V.tensor_tensor(stat[:, 32:40].rearrange("p (a b) -> p a b", a=2), m, s,
                                    ALU.add).then_inc(prob_biased, 1)
                elif what == "norm":
                    keys = WIN * (UNITS[a][0] + 1)
                    dve.wait_ge(exp_done, a + 1)
                    link(V.tensor_tensor(stat[:, 24:32], stat[:, 24:32], stat[:, 32:40], ALU.add))
                    link(V.reciprocal(stat[:, 40:48], stat[:, 24:32]))
                    for h in range(8):
                        ins = V.tensor_scalar(prob[:, h, 0:keys], prob[:, h, 0:keys], stat[:, 40 + h:41 + h], None,
                                              ALU.mult)
                    ins.then_inc(prob_ready, 1)
                elif what == "values":
                    q, t0 = UNITS[a]
                    b = misc_bank()
                    V.tensor_copy(ya[:, t0:t0 + 4, 128 * q:128 * q + 128],
                                  b.rearrange("p (t n) -> p t n", t=4)).then_inc(misc_free, 1)
                elif what == "s_scores":
                    for kv in range(NKV):
                        V.tensor_copy(sprobT[:, 64 * kv:64 * kv + 64], misc_bank()[:, 0:64]).then_inc(misc_free, 1)
                elif what == "s_bias":
                    b = misc_bank()
                    dve.wait_ge(stab_loaded, 16 * 16)
                    V.scalar_tensor_tensor(out=sprob[:], in0=b[:, 0:128], scalar=HD ** -0.5, in1=stab[:],
                                           op0=ALU.mult, op1=ALU.add).then_inc(misc_free, 1)
                    dve.wait_ge(misc_free, misc.n)
                    link(V.tensor_reduce(stat[:, 48:49], sprob[:], AX.X, ALU.max))
                    link(V.tensor_tensor(stat[:, 48:49], stat[:, 48:49], ssink[:], ALU.max))
                    link(V.tensor_scalar(stat[:, 48:49], stat[:, 48:49], -1.0, None, ALU.mult))
                    V.tensor_tensor(stat[:, 50:51], stat[:, 48:49], ssink[:], ALU.add).then_inc(sexp_in, 1)
                elif what == "s_norm":
                    dve.wait_ge(sexp_done, 1)
                    link(V.tensor_tensor(stat[:, 49:50], stat[:, 49:50], stat[:, 50:51], ALU.add))
                    link(V.reciprocal(stat[:, 51:52], stat[:, 49:50]))
                    V.tensor_scalar(sprob[:], sprob[:], stat[:, 51:52], None, ALU.mult).then_inc(sprob_ready, 1)
                elif what == "s_turn":
                    V.tensor_copy(sprobT[:], misc_bank()[:, 0:128]).then_inc(misc_free, 1)
                elif what == "s_values":
                    b = misc_bank()
                    V.tensor_copy(ya[:, :, SEQ:].rearrange("p t b -> p b t"),
                                  b[:, 0:64].rearrange("p (b t) -> p b t", b=DEC)).then_inc(misc_free, 1)
                elif what == "conv_rows":
                    b = misc_bank()
                    dst = conv_row[0:2 + DEC, :].rearrange("r (h t c) -> r h t c", h=2, c=HD)
                    V.tensor_copy(dst[:, :, 4 * a:4 * a + 4, :],
                                  b[0:2 + DEC, :].rearrange("r (t h c) -> r h t c", t=4, h=2)).then_inc(misc_free, 1)

            dve.wait_ge(out_full, 1)
            V.tensor_tensor(x[:, 0, :], pA[:, 0:1024], x[:, 0, :], ALU.add)
            V.tensor_tensor(x[:, 1, :], pA[:, 1024:2048], x[:, 1, :], ALU.add)
            V.tensor_tensor(x[0:DEC, 2, :], pB[0:DEC].rearrange("p a n -> p (a n)"), x[0:DEC, 2, :],
                            ALU.add).then_inc(norm_in, 1)
            normalise(1)
            for k in range(KT):
                V.tensor_scalar(hT[:, k, :], misc_bank()[:, 0:NT], cols[:, V_FNORM + k:V_FNORM + k + 1], None,
                                ALU.mult).then_inc(misc_free, 1)
            dve.wait_ge(router_full, 1)
            V.tensor_scalar(lgT[0:NE, :], pB[0:NE, 0, 0:NT], brouter[:, 0:1], None, ALU.add).then_inc(router_ready, 1)
            b = misc_bank()
            V.tensor_copy(lg[:, 0:2, :].rearrange("p m e -> p (m e)"), b[:, 0:64])
            V.tensor_copy(lg[0:DEC, 2, :], b[0:DEC, 64:96]).then_inc(misc_free, 1)
            dve.wait_ge(misc_free, misc.n)

            def wide(ap):
                return ap.to_broadcast([128, 3, NE])

            for m in range(3):
                ins = V.max(top8[:, m, :], lg[:, m, :])
            link(ins)
            link(V.tensor_tensor(mask[:], lg[:], wide(top8[:, :, TOPK - 1:TOPK]), ALU.is_gt))
            link(V.tensor_reduce(stat[:, 52:55], mask[:], AX.X, ALU.add))
            link(V.tensor_scalar(stat[:, 52:55], stat[:, 52:55], -1.0, float(TOPK), ALU.mult, ALU.add))
            link(V.tensor_tensor(t32[:], lg[:], wide(top8[:, :, TOPK - 1:TOPK]), ALU.is_equal))
            for m in range(3):
                ins = V.tensor_tensor_scan(gate[:, m, :], cst[:, C_ONE:C_ONE + NE], t32[:, m, :], 0.0,
                                           ALU.mult, ALU.add)
            link(ins)
            for m in range(3):
                ins = V.scalar_tensor_tensor(out=t32[:, m, :], in0=gate[:, m, :], scalar=stat[:, 52 + m:53 + m],
                                             in1=t32[:, m, :], op0=ALU.is_le, op1=ALU.mult)
            link(ins)
            link(V.tensor_tensor(mask[:], mask[:], t32[:], ALU.add))
            link(V.tensor_tensor(mask[:], mask[:], cst[:, C_VALID:C_VALID + 3].unsqueeze(2).to_broadcast([128, 3, NE]),
                                 ALU.mult))
            V.tensor_tensor(gate[:], lg[:], wide(top8[:, :, 0:1]), ALU.subtract).then_inc(ex_in, 1)
            dve.wait_ge(ex_out, 1)
            link(V.tensor_tensor(gate[:], gate[:], mask[:], ALU.mult))
            link(V.tensor_reduce(stat[:, 52:55], gate[:], AX.X, ALU.add))
            link(V.tensor_scalar(stat[:, 52:55], stat[:, 52:55], 1e-30, None, ALU.max))
            link(V.reciprocal(stat[:, 56:59], stat[:, 52:55]))
            link(V.tensor_tensor(gate[:], gate[:], stat[:, 56:59].unsqueeze(2).to_broadcast([128, 3, NE]), ALU.mult))
            b = misc_bank()
            link(V.tensor_reduce(stat[:, 60:61], b[:, 96:128], AX.X, ALU.max))
            link(V.tensor_scalar(flag_f32[:], stat[0:1, 60:61], float(CAP), None, ALU.is_gt))
            link(V.scalar_tensor_tensor(out=t32[:].rearrange("p m e -> p (m e)"), in0=b[:, 0:96], scalar=1.0,
                                        in1=mask[:].rearrange("p m e -> p (m e)"), op0=ALU.add, op1=ALU.mult))
            V.memset(pos[:, :, PASSES * NE:], -1.0)
            for q in range(PASSES):
                V.tensor_scalar(pos[:, :, q * NE:(q + 1) * NE], t32[:], -1.0 - CAP * q, None, ALU.add)
            V.tensor_copy(flag[0:1, 0:1], flag_f32[:]).then_inc(misc_free, 1)
            dve.wait_ge(misc_free, misc.n)

            iota = cst[:, C_IOTA:C_IOTA + CAP].unsqueeze(1).unsqueeze(1).to_broadcast([128, 3, 2, CAP])

            def picks(g1):
                return V.tensor_tensor(pick, iota, pos[:, :, bass.ds(g1 * 2, 2)].unsqueeze(3).to_broadcast([128, 3, 2, CAP]),
                                       ALU.is_equal)

            picks(0).then_inc(pick_ready, 1)
            fw = cols[:, V_FNORM:V_FNORM + KT].unsqueeze(2).to_broadcast([128, KT, 128])

            def gathered(half, b):
                return V.tensor_tensor(xsT[:, 4 * half:4 * half + 4, :], b.rearrange("p (k s) -> p k s", k=4),
                                       fw[:, 4 * half:4 * half + 4, :], ALU.mult)

            for half in range(2):
                gathered(half, misc_bank()).then_inc(misc_free, 1)
            misc0 = misc.n
            assert misc0 == PRE_FILLS, misc0
            step0 = step.n
            LINKS = 2

            def pair(g, i):
                n = 0
                base = step0 + LINKS * g

                def link(ins):
                    nonlocal n
                    n += 1
                    ins.then_inc(dve_step, 1)
                    dve.wait_ge(dve_step, base + n)

                def bank(k):
                    dve.wait_ge(misc_full, PAIR_FILLS * g + (misc0 + k + 1))
                    return pM[:, (misc0 + k) % 2, :]

                V.tensor_copy(sel[0:96], cst[0:96, C_SEL:C_SEL + NE][:, bass.ds(i * 2, 2)].unsqueeze(2)
                              .to_broadcast([96, 2, CAP])).then_inc(sel_ready, 1)
                dve.wait_ge(pick_ready, g + 1)
                V.tensor_tensor(gpick, pick, gate[:, :, bass.ds(i * 2, 2)].unsqueeze(3)
                                .to_broadcast([128, 3, 2, CAP]), ALU.mult).then_inc(gpick_ready, 1)
                dve.wait_ge(gpick_ready, g + 1)
                picks(g + 1).then_inc(pick_ready, 1)
                dve.wait_ge(up_done, g + 1)
                u = pA[:].rearrange("p (f two) -> p two f", two=2)
                V.tensor_scalar(glu, u[:, 0], LIMIT, None, ALU.min).then_inc(glu_ready, 1)
                dve.wait_ge(glu_ready, g + 1)
                link(V.tensor_scalar(lin, u[:, 1], -LIMIT, LIMIT, ALU.max, ALU.min))
                link(V.scalar_tensor_tensor(out=lin, in0=lin, scalar=1.0, in1=glu, op0=ALU.add, op1=ALU.mult))
                dve.wait_ge(sig_ready, g + 1)
                V.tensor_tensor(act_out, lin, sig, ALU.mult).then_inc(a_ready, 1)
                for half in range(2):
                    gathered(half, bank(half)).then_inc(misc_free, 1)
                V.tensor_copy(gateT, bank(2)[:, 0:NT]).then_inc(misc_free, 1)
                for half in range(2):
                    V.tensor_copy(aT[:, 4 * half:4 * half + 4, :].rearrange("p k s -> p (k s)"),
                                  bank(3 + half)).then_inc(misc_free, 1)
                for k in range(6):
                    m, h = k // 2, k % 2
                    r = TOK[m][1]
                    xs = x[0:r, m, 512 * h:512 * h + 512]
                    V.tensor_tensor(xs, bank(5 + k)[0:r], xs, ALU.add).then_inc(misc_free, 1)
                dve.wait_ge(misc_free, PAIR_FILLS * g + (misc0 + PAIR_FILLS))
                assert n == LINKS

            with dve.Fori(0, PAIRS) as i:
                pair(i, i)
            dve.wait_ge(misc_free, FILL["route", 0])
            over = dve.value_load(flag[0:1, 0:1], min_val=0, max_val=1)
            with dve.If(over > 0):
                with dve.Fori(1, PASSES) as q:
                    with dve.Fori(0, PAIRS) as i:
                        pair(q * PAIRS + i, i)
            V.memset(stat[:, 0:1], 0.0).then_inc(moe_done, 1)

        @block.tensor
        def _(pe):
            fills = Count(misc_full)

            def misc_bank():
                if fills.n >= 2:
                    pe.wait_ge(misc_free, fills.n - 1)
                return pM[:, (fills.next() - 1) % 2, :]

            def matmul(out, w, m, start=True, stop=True):
                return pe.matmul(out, w, m, start=start, stop=stop, skip_group_check=True)

            def tr(out, src):
                return pe.transpose(out, src, ident[0:src.shape[0], 0:src.shape[0]])

            pe.wait_ge(consts_loaded, 16)
            pe.wait_ge(vecs_loaded, 16 * VECS)
            for what, a in STEPS:
                if what == "vectors":
                    tr(misc_bank()[:, 0:V_N], rows[0:V_N, :]).then_inc(misc_full, 1)
                elif what == "bias_table":
                    matmul(misc_bank()[0:NH, 0:128], rb[:], cst[0:NBUCKET, C_BUCKET:C_BUCKET + 128]).then_inc(misc_full, 1)
                elif what == "h_cols":
                    if a == 0:
                        pe.wait_ge(h_ready, 3)
                    b = misc_bank()
                    for m, (t0, r) in enumerate(TOK):
                        mm = tr(b[:, t0:t0 + r], hn[0:r, m, 128 * a:128 * a + 128])
                    mm.then_inc(misc_full, 1)
                elif what == "tile":
                    kind, c, j, t = TILES[a]
                    if j == 0:
                        pe.wait_ge(ring_full[c % SLOTS], filled(c))
                    if a == 0:
                        pe.wait_ge(misc_free, FILL["h_cols", KT - 1])
                    if a >= 2:
                        if TILES[a - 2][0] in ("cg", "gc", "ga"):
                            pe.wait_ge(tile_free_act, ACT_TILES[a - 2] + 1)
                        else:
                            pe.wait_ge(tile_free_dve, DVE_TILES[a - 2] + 1)
                    for k in range(KT):
                        if c == 0:
                            w = ring[:, 0, 0:2048].rearrange("p (k n) -> p k n", k=KT)[:, k, 128 * j:128 * j + 128]
                            mm = matmul(pB[:, a % 2, 0:NT], w, hT[:, k, :], start=(k == 0), stop=(k == KT - 1))
                            continue
                        w = ring[:, c % SLOTS, :].rearrange("p (k h n) -> p k h n", k=KT, h=2)
                        for h in range(2):
                            mm = matmul(pB[HD * h:HD * h + HD, a % 2, 0:NT], w[:, k, h, HD * j:HD * j + HD],
                                        hT[:, k, :], start=(k == 0), stop=(k == KT - 1))
                            if k == 0 and j == 0 and h == 0:
                                mm.then_inc(ring_free, 1)
                    mm.then_inc(tile_full, 1)
                elif what == "square":
                    b = misc_bank()
                    pe.wait_ge(sq_ready, a + 1)
                    matmul(b[:, 0:NT], cst[:, C_BLK:C_BLK + 128], tmp[:, a % 2, :]).then_inc(misc_full, 1)
                elif what == "v_rows":
                    b = misc_bank()
                    pe.wait_ge(tile_free_dve, 2)
                    for m, (t0, r) in enumerate(TOK):
                        mm = tr(b[0:r, 128 * m:128 * m + 128], vT[:, t0:t0 + r])
                    mm.then_inc(misc_full, 1)
                elif what == "k_rows":
                    b = misc_bank()
                    pe.wait_ge(qk_normed, 1)
                    tr(b[:, 0:128], kT[:, 128:256])
                    tr(b[0:DEC, 128:256], kT[:, 256:NT]).then_inc(misc_full, 1)
                elif what == "state_cols":
                    b = misc_bank()
                    pe.wait_ge(state_loaded, 32)
                    for t in range(KT):
                        mm = tr(b[:, 16 * t:16 * t + 16], conv_row[0:2 * DEC, 128 * t:128 * t + 128])
                    mm.then_inc(misc_full, 1)
                elif what == "cache_cols":
                    b = misc_bank()
                    pe.wait_ge(cache_loaded, 32)
                    for n in range(4):
                        mm = tr(b[:, 128 * n:128 * n + 127], k_cache[0:WIN - 1, 4 * a + n, :])
                    mm.then_inc(misc_full, 1)
                elif what == "scores":
                    q, t0 = UNITS[a]
                    keys = WIN * (q + 1)
                    pe.wait_ge(qk_normed, 9)
                    if a:
                        pe.wait_ge(probT_ready, a)
                    for t in range(4):
                        for kv in range(NKV):
                            s = slice(HD * kv, HD * kv + HD)
                            o = 1024 * kv + t * keys
                            mm = matmul(pA[:, o:o + keys], qT[s, t0 + t, 128 * q:128 * q + 128],
                                        kT[s, 0:keys])
                    mm.then_inc(scores_full, 1)
                elif what == "turn":
                    q, t0 = UNITS[a]
                    pe.wait_ge(prob_ready, a + 1)
                    for b in range(q + 1):
                        for h in range(8):
                            o = (8 * b + h) * 128
                            mm = tr(pA[:, o:o + 128], prob[:, h, 128 * b:128 * b + 128])
                    mm.then_inc(turned, 1)
                elif what == "values":
                    q, t0 = UNITS[a]
                    o = misc_bank()
                    pe.wait_ge(probT_ready, a + 1)
                    for b in range(q + 1):
                        for kv in range(NKV):
                            mm = matmul(o[HD * kv:HD * kv + HD, :], v_row[:, b, HD * kv:HD * kv + HD],
                                        probT[:, b, 4 * kv:4 * kv + 4, :].rearrange("p h q -> p (h q)"),
                                        start=(b == 0), stop=(b == q))
                    mm.then_inc(misc_full, 1)
                elif what == "s_scores":
                    for kv in range(NKV):
                        b = misc_bank()
                        s = slice(HD * kv, HD * kv + HD)
                        for n in range(DEC):
                            mm = matmul(b[:, 8 * n:8 * n + 8], k_cacheT[s, n, :], qT[s, :, SEQ + n])
                        mm.then_inc(misc_full, 1)
                elif what == "s_bias":
                    b = misc_bank()
                    pe.wait_ge(misc_free, fills.n - 1)
                    tr(b[:, 0:128], sprobT[:]).then_inc(misc_full, 1)
                elif what == "s_turn":
                    b = misc_bank()
                    pe.wait_ge(sprob_ready, 1)
                    tr(b[:, 0:128], sprob[:]).then_inc(misc_full, 1)
                elif what == "s_values":
                    b = misc_bank()
                    pe.wait_ge(misc_free, fills.n - 1)
                    pe.wait_ge(vnew_loaded, 16)
                    pe.wait_ge(cache_loaded, 32)
                    for n in range(DEC):
                        for kv in range(NKV):
                            s = slice(HD * kv, HD * kv + HD)
                            mm = matmul(b[s, 8 * n:8 * n + 8], v_cache[:, n, s],
                                        sprobT[:, 64 * kv + 8 * n:64 * kv + 8 * n + 8])
                    mm.then_inc(misc_full, 1)
                elif what == "conv_rows":
                    b = misc_bank()
                    pe.wait_ge(tile_free_dve, DVE_TILES[XIN_END[a]])
                    for t in range(4):
                        mm = tr(b[0:2 + DEC, 128 * t:128 * t + 128], cx[:, 4 * a + t, SEQ:])
                    mm.then_inc(misc_full, 1)

            pe.wait_ge(probT_ready, len(UNITS))
            pe.wait_ge(tile_free_act, ACT_TILES[len(TILES)])
            for c in range(W_OUT_CHUNKS):
                ch = W_IN_CHUNKS + c
                pe.wait_ge(ring_full[ch % SLOTS], filled(ch))
                for k in range(4):
                    t = 4 * c + k
                    pe.wait_ge(sig_used, KT + t + 1)
                    for n in range(2):
                        w = ring[:, ch % SLOTS, 1024 * k + 512 * n:1024 * k + 512 * n + 512]
                        for m, (t0, r) in enumerate(TOK):
                            out = pA[:, 1024 * m + 512 * n:1024 * m + 512 * n + 512] if m < 2 else pB[0:DEC, n, :]
                            mm = matmul(out, yc[:, t, t0:t0 + r], w, start=(t == 0), stop=(t == KT - 1))
                            if k == 0 and n == 0 and m == 0:
                                mm.then_inc(ring_free, 1)
            mm.then_inc(out_full, 1)

            for k in range(KT):
                b = misc_bank()
                if k == 0:
                    pe.wait_ge(h_ready, 6)
                for m, (t0, r) in enumerate(TOK):
                    mm = tr(b[:, t0:t0 + r], hn[0:r, m, 128 * k:128 * k + 128])
                    if k == 0 and m == 0:
                        mm.then_inc(ring_free, 1)
                mm.then_inc(misc_full, 1)
            pe.wait_ge(wr_loaded, 32)
            pe.wait_ge(misc_free, fills.n)
            for k in range(KT):
                mm = matmul(pB[0:NE, 0, 0:NT], w_router_sb[:, k, :], hT[:, k, :], start=(k == 0), stop=(k == KT - 1))
            mm.then_inc(router_full, 1)
            b = misc_bank()
            pe.wait_ge(router_ready, 1)
            for m, (t0, r) in enumerate(TOK):
                mm = tr(b[0:r, NE * m:NE * m + NE], lgT[0:NE, t0:t0 + r])
            mm.then_inc(misc_full, 1)
            b = misc_bank()
            pe.wait_ge(ex_in, 1)
            tri, ones = cst[:, C_TRI:C_TRI + 128], cst[:, C_ONE:C_ONE + 128]
            for m in range(4):
                for s in range(min(m, 2) + 1):
                    mm = matmul(b[:, NE * m:NE * m + NE], tri if s == m else ones, mask[:, s, :],
                                start=(s == 0), stop=(s == min(m, 2)))
            mm.then_inc(misc_full, 1)

            def gather(bank):
                for half in range(2):
                    b = bank(half)
                    for k in range(4):
                        f = 128 * (4 * half + k)
                        for m, (_, r) in enumerate(TOK):
                            mm = matmul(b[:, 128 * k:128 * k + 128], hn[0:r, m, f:f + 128],
                                        pick[0:r, m].rearrange("p e s -> p (e s)"), start=(m == 0), stop=(m == 2))
                    mm.then_inc(misc_full, 1)

            pe.wait_ge(pick_ready, 1)
            gather(lambda half: misc_bank())
            misc0 = fills.n
            assert misc0 == PRE_FILLS, misc0
            pe.wait_ge(bias_split, BIAS_STEPS)

            def pair(g, i):
                def bank(k):
                    pe.wait_ge(misc_free, PAIR_FILLS * g + (misc0 + k - 1))
                    return pM[:, (misc0 + k) % 2, :]

                pe.wait_ge(misc_free, PAIR_FILLS * g + misc0)
                for k in range(UP_CHUNKS):
                    c = FIRST_CHUNKS + k
                    pe.wait_ge(ring_full[c % SLOTS], 64 * g + filled(c))
                    for n in range(4):
                        for e in range(2):
                            mm = matmul(pA[64 * e:64 * e + 64, 512 * n:512 * n + 512], xsT[:, k, 64 * e:64 * e + 64],
                                        ring[:, c % SLOTS, 2048 * e + 512 * n:2048 * e + 512 * n + 512],
                                        start=(k == 0), stop=False)
                    mm.then_inc(ring_free, 1)
                pe.wait_ge(sel_ready, g + 1)
                for n in range(4):
                    mm = pe.matmul(pA[:, 512 * n:512 * n + 512], sel[0:96].rearrange("p e s -> p (e s)"),
                                   bias_up[0:96, 512 * n:512 * n + 512], start=False, stop=True, skip_group_check=True)
                mm.then_inc(up_done, 1)
                pe.wait_ge(pick_ready, g + 2)
                gather(bank)
                b = bank(2)
                pe.wait_ge(gpick_ready, g + 1)
                for m, (t0, r) in enumerate(TOK):
                    mm = tr(b[:, t0:t0 + r], gpick[0:r, m].rearrange("p e s -> p (e s)"))
                mm.then_inc(misc_full, 1)
                for half in range(2):
                    b = bank(3 + half)
                    if half == 0:
                        pe.wait_ge(a_ready, g + 1)
                    for k in range(4):
                        f = 128 * (4 * half + k)
                        mm = tr(b[:, 128 * k:128 * k + 128], act_out[:, f:f + 128])
                    mm.then_inc(misc_full, 1)
                pe.wait_ge(misc_free, PAIR_FILLS * g + (misc0 + 5))
                for k in range(KT):
                    c = FIRST_CHUNKS + UP_CHUNKS + k // 2
                    if k % 2 == 0:
                        pe.wait_ge(ring_full[c % SLOTS], 64 * g + filled(c))
                    for n in range(2):
                        for e in range(2):
                            o = 2048 * e + 1024 * (k % 2) + 512 * n
                            mm = matmul(pB[64 * e:64 * e + 64, n, :], aT[:, k, 64 * e:64 * e + 64],
                                        ring[:, c % SLOTS, o:o + 512], start=(k == 0), stop=False)
                    if k % 2:
                        mm.then_inc(ring_free, 1)
                for n in range(2):
                    mm = pe.matmul(pB[:, n, :], sel[0:96].rearrange("p e s -> p (e s)"),
                                   bias_down[0:96, 512 * n:512 * n + 512], start=False, stop=True, skip_group_check=True)
                mm.then_inc(down_done, 1)
                for k in range(6):
                    m, h = k // 2, k % 2
                    t0, r = TOK[m]
                    b = bank(5 + k)
                    if k == 0:
                        pe.wait_ge(y_ready, g + 1)
                    matmul(b[0:r, :], gateT[:, t0:t0 + r], y_pair[:, 512 * h:512 * h + 512]).then_inc(misc_full, 1)

            with pe.Fori(0, PAIRS) as i:
                pair(i, i)
            pe.wait_ge(misc_free, FILL["route", 0])
            over = pe.value_load(flag[0:1, 0:1], min_val=0, max_val=1)
            with pe.If(over > 0):
                with pe.Fori(1, PASSES) as q:
                    with pe.Fori(0, PAIRS) as i:
                        pair(q * PAIRS + i, i)


_INS = ["x_prompt", "x_sample", "state_conv", "cache_k_win", "cache_v_win", "rel_bias", "attn_norm_w", "w_in",
        "conv_w", "q_norm_w", "k_norm_w", "sinks", "w_out", "ffn_norm_w", "w_router", "b_router", "w_up", "b_up",
        "w_down", "b_down"]
_BY_LAYER = set(_INS) - {"x_prompt", "x_sample", "rel_bias"}
_OUTS = [(1, SEQ, D), (DEC, 1, D), (1, 1, 2, D), (1, 1, WIN, NKV, HD), (1, 1, WIN, NKV, HD),
         (1, DEC, 2, D), (1, DEC, WIN, NKV, HD), (1, DEC, WIN, NKV, HD)]


def kernel(**inputs):
    import concourse.bacc as bacc
    from concourse.bass_utils import run_bass_kernel_spmd

    nc = bacc.Bacc("TRN2", target_bir_lowering=False, num_devices=1)
    arrays, args = {}, []
    for name in _INS:
        a = np.ascontiguousarray(inputs[name])
        arrays["in_" + name] = a
        ap = nc.dram_tensor("in_" + name, a.shape, F32, kind="ExternalInput").ap()
        args.append(ap[0] if name in _BY_LAYER else ap)
    arrays["in_consts"] = constants()
    args.append(nc.dram_tensor("in_consts", (128, C_N), F32, kind="ExternalInput").ap())
    for n, shape in enumerate(_OUTS):
        args.append(nc.dram_tensor(f"out_{n}", shape, F32, kind="ExternalOutput").ap())
    build(nc, *args)
    r = run_bass_kernel_spmd(nc, [arrays], core_ids=[0])
    return tuple(r.results[0][f"out_{n}"] for n in range(len(_OUTS)))
```

```python
from contextlib import ExitStack

import numpy as np

import concourse.bass as bass
from concourse import mybir
from concourse.alu_op_type import AluOpType as ALU

F32 = mybir.dt.float32
BF16 = mybir.dt.bfloat16
I32 = mybir.dt.int32
ACT = mybir.ActivationFunctionType
AX = mybir.AxisListType

D = 1024
SEQ, DEC = 256, 8
NT = SEQ + DEC
KT = D // 128
HD, NKV, GROUP = 64, 2, 8
NH = NKV * GROUP
WIN = 128
NBUCKET, MAXDIST = 32, 128
NE, TOPK = 32, 4
FF = 1024
EPS = 1e-5
NEG = -1e30
ALPHA, LIMIT = 1.702, 7.0

TOK = [(0, 128), (128, 128), (256, DEC)]
CAP = 64
PASSES = -(-NT // CAP)
PAIRS = NE // 2

SLOTS = 6
SLOT = 4096
W_IN_CHUNKS, W_OUT_CHUNKS = 13, 2
FIRST_CHUNKS = W_IN_CHUNKS + W_OUT_CHUNKS
UP_CHUNKS, DOWN_CHUNKS = KT, KT // 2
PAIR_CHUNKS = UP_CHUNKS + DOWN_CHUNKS
EXTRA = {4: 0, 5: 1, 8: 2}
FIRST_PAIR = {}
for _j in range(PAIR_CHUNKS):
    if _j not in EXTRA:
        FIRST_PAIR[_j] = FIRST_CHUNKS + len(FIRST_PAIR)
LOOP_CHUNK = FIRST_CHUNKS - len(EXTRA)

XIN, BG, CG, QC, KC_, VC_, GC, GA = 0, 1024, 2048, 3072, 4096, 4224, 4352, 5376

C_ID, C_BLK, C_TRI, C_ONE, C_IOTA, C_BUCKET, C_SEL, C_VALID, C_EPS, C_N = 0, 128, 256, 384, 512, 576, 704, 736, 739, 740

V_ANORM, V_FNORM, V_CONV, V_QN, V_KN, V_N = 0, 8, 16, 40, 41, 42


def constants():
    c = np.zeros((128, C_N), np.float32)
    p = np.arange(128)
    c[:, C_ID:C_ID + 128] = np.eye(128)
    c[:, C_BLK:C_BLK + 128] = (p[:, None] // HD) == (p[None, :] // HD)
    c[:, C_TRI:C_TRI + 128] = p[:, None] < p[None, :]
    c[:, C_ONE:C_ONE + 128] = 1.0
    c[:, C_IOTA:C_IOTA + CAP] = np.arange(CAP)
    rel = 127 - np.arange(128)
    exact = NBUCKET // 2
    far = exact + (np.log(np.maximum(rel, 1).astype(np.float32) / np.float32(exact))
                   / np.float32(np.log(MAXDIST / exact)) * np.float32(NBUCKET - exact)).astype(np.int32)
    bucket = np.where(rel < exact, rel, np.minimum(far, NBUCKET - 1))
    c[0:NBUCKET, C_BUCKET:C_BUCKET + 128] = bucket[None, :] == np.arange(NBUCKET)[:, None]
    c[0:96, C_SEL:C_SEL + NE] = (p[0:96, None] % NE) == np.arange(NE)[None, :]
    for m, (_, n) in enumerate(TOK):
        c[0:n, C_VALID + m] = 1.0
    c[:, C_EPS] = EPS
    return c


def tile_list():
    tiles = [("k", 0, 0, 0), ("v", 0, 1, 0)]
    groups = [("q", 0), ("q", 1), ("cg", 0), ("xin", 0), ("bg", 0), ("gc", 0),
              ("cg", 1), ("xin", 1), ("bg", 1), ("gc", 1), ("ga", 0), ("ga", 1)]
    for c, (kind, half) in enumerate(groups):
        tiles += [(kind, c + 1, j, 4 * half + j) for j in range(4)]
    return tiles


TILES = tile_list()
CHUNK_COL = {"q": QC, "cg": CG, "xin": XIN, "bg": BG, "gc": GC, "ga": GA}
UNITS = [(0, 0), (1, 0), (0, 4), (1, 4)]


def plan():
    after = {n: [] for n in range(len(TILES))}
    for j in range(9):
        n = 0 if j == 0 else j + 1 + (j == 8)
        after[n + 1].append(("square", j))
        after[n + 2].append(("qknorm", j))
    after[3].append(("v_rows", 0))
    after[4].append(("k_rows", 0))
    after[5].append(("state_cols", 0))
    after[7].append(("cache_cols", 0))
    after[8].append(("cache_cols", 1))
    for u in range(len(UNITS)):
        n = 13 + 7 * u
        for d, what in ((0, "scores"), (1, "bias"), (2, "exp"), (3, "norm"), (5, "turn"), (6, "values")):
            after[n + d].append((what, u))
    for n, what in ((14, "s_scores"), (16, "s_bias"), (18, "s_norm"), (21, "s_turn"), (23, "s_values")):
        after[n].append((what, 0))
    after[34].append(("conv_rows", 0))
    after[36].append(("conv_rows", 1))
    steps = [("vectors", 0), ("bias_table", 0)] + [("h_cols", n) for n in (1, 2, 3, 4, 0)]
    for n in range(len(TILES)):
        steps.append(("tile", n))
        steps += after[n]
    return steps


STEPS = plan()

COLS_FIRST = next(a for what, a in STEPS if what == "h_cols")
COLS = [(2, 0, 8), (0, 0, 4), (0, 4, 4), (1, 0, 4), (1, 4, 4)]
BRANCH = [("out", (2, 0)), ("out", (0, 0)), ("x_cols", 0), ("out", (0, 1)), ("x_cols", 1), ("logits", 2),
          ("out", (1, 0)), ("x_cols", 2), ("logits", 0), ("out", (1, 1)), ("x_cols", 3), ("x_cols", 4), ("logits", 1)]

FILLS_OF = {"tile": 0, "qknorm": 0, "scores": 0, "bias": 0, "exp": 0, "norm": 0, "turn": 0, "s_norm": 0, "s_scores": 2, "out": 0}
FILL, _n = {}, 0
for _s in STEPS + BRANCH + [("route", 0), ("gather", 0), ("gather", 1)]:
    _n += FILLS_OF.get(_s[0], 1)
    FILL[_s] = _n
PRE_FILLS = _n
PAIR_FILLS = 11

BY_ACT = ("cg", "gc", "ga")
ACT_TILES = [sum(t[0] in BY_ACT for t in TILES[:n]) for n in range(len(TILES) + 1)]
DVE_TILES = [sum(t[0] not in BY_ACT for t in TILES[:n]) for n in range(len(TILES) + 1)]
XIN_END = [18, 34]
BIAS_STEPS = 2 * (1 + 2 * 3)
VECS = 6


class Count:

    def __init__(self, sem, base=0):
        self.sem, self.n = sem, base

    def next(self):
        self.n = self.n + 1
        return self.n


def build(nc, x_prompt, x_sample, state_conv, cache_k, cache_v, rel_bias, attn_norm_w, w_in, conv_w, q_norm_w,
          k_norm_w, sinks, w_out, ffn_norm_w, w_router, b_router, w_up, b_up, w_down, b_down, consts,
          y_prompt, y_sample, conv_prompt, k_prompt, v_prompt, conv_sample, k_sample, v_sample):
    with ExitStack() as ctx:
        def sb(name, shape, dt=F32):
            return ctx.enter_context(nc.sbuf_tensor(name, shape, dt))

        def sem(name):
            return ctx.enter_context(nc.semaphore(name))

        ring = sb("ring", [128, SLOTS, SLOT])
        x = sb("x", [128, 3, D])
        hn = sb("hn", [128, 3, D])
        cst = sb("cst", [128, C_N])
        rows = sb("rows", [128, 128])
        cols = sb("cols", [128, V_N])
        rb = sb("rb", [NBUCKET, NH])
        brouter = sb("brouter", [128, NE])
        sink = sb("sink", [128, NKV, GROUP])
        ssink = sb("ssink", [128, 1])
        conv_row = sb("conv_row", [128, D])
        state_c = sb("state_c", [128, KT, DEC, 2])
        v_row = sb("v_row", [128, 3, 128])
        k_row = sb("k_row", [128, 2, 128])
        tmp = sb("tmp", [128, 2, NT])
        rt = sb("rt", [128, NT])
        stat = sb("stat", [128, 64])
        flag = sb("flag", [1, 4], I32)

        AREA = 8 * NT * 4 + KT * (NT + 2) + 2 * NT + 3 * 2048
        area = sb("area", [128, AREA])

        class Area:
            def __init__(self, at):
                self.at = at

            def take(self, n):
                self.at += n
                assert self.at <= AREA
                return area[:, self.at - n:self.at]

        one = Area(0)
        hT = one.take(KT * NT).rearrange("p (k n) -> p k n", k=KT)
        yc = one.take(KT * NT).rearrange("p (k n) -> p k n", k=KT)
        ya = one.take(KT * NT).rearrange("p (k n) -> p k n", k=KT)
        cx = one.take(KT * (NT + 2)).rearrange("p (k n) -> p k n", k=KT)
        kT = one.take(NT)
        vT = one.take(NT)
        qT = one.take(KT * NT).rearrange("p (k n) -> p k n", k=KT)
        table = one.take(2048).rearrange("p (h s) -> p h s", h=8)
        prob = one.take(2048).rearrange("p (h s) -> p h s", h=8)
        probT = one.take(2048).rearrange("p (b h q) -> p b h q", b=2, h=8)
        hn_flat = hn[:].rearrange("p m d -> p (m d)")
        k_cache = hn_flat[:, 0:1024].rearrange("p (b f) -> p b f", b=DEC)
        v_cache = hn_flat[:, 1024:2048].rearrange("p (b f) -> p b f", b=DEC)
        k_cacheT = hn_flat[:, 2048:3072].rearrange("p (b s) -> p b s", b=DEC)
        stab = sb("stab", [128, WIN])
        sprob = sb("sprob", [128, WIN])
        sprobT = sb("sprobT", [128, 128])

        two = Area(2 * KT * NT)
        xsT = two.take(1024).rearrange("p (k s) -> p k s", k=KT)
        extra0 = area[:, two.at:two.at + SLOT]
        act_out = two.take(FF)
        aT = two.take(1024).rearrange("p (k s) -> p k s", k=KT)
        y_pair = two.take(D)
        glu = two.take(FF)
        pick = two.take(3 * 128).rearrange("p (m e s) -> p m e s", m=3, e=2)
        gateT = two.take(NT)
        gpick = two.take(3 * 128).rearrange("p (m e s) -> p m e s", m=3, e=2)
        bias_down = two.take(D // 2).bitcast(BF16)
        assert two.at <= 3 * KT * NT + KT * (NT + 2) + 2 * NT + KT * NT
        two.at = 3 * KT * NT + KT * (NT + 2) + 2 * NT + KT * NT
        extra1 = area[:, two.at:two.at + SLOT]
        bias_raw = two.take(2 * FF)
        lin = two.take(FF)
        sig = two.take(FF)
        NPOS = PASSES * NE + 2
        pos = two.take(3 * NPOS).rearrange("p (m e) -> p m e", m=3)
        sel = two.take(64).bitcast(BF16).rearrange("p (e s) -> p e s", e=2)
        bias_up = two.take(FF).bitcast(BF16)
        extra = [extra0, extra1, area[:, 0:SLOT]]

        lg = sb("lg", [128, 3, NE])
        mask = sb("mask", [128, 3, NE])
        t32 = sb("t32", [128, 3, NE])
        gate = sb("gate", [128, 3, NE])
        rank = sb("rank", [128, NE])
        top8 = sb("top8", [128, 3, 8])
        flag_f32 = sb("flag_f32", [1, 1])
        rev_sb = prob.rearrange("p h s -> p (h s)")[0:NH, 0:3 * WIN]

        ident = cst[:, C_ID:C_ID + 128]

        pA = ctx.enter_context(nc.psum_tensor("pA", [128, 2048], F32))
        pB = ctx.enter_context(nc.psum_tensor("pB", [128, 2, 512], F32))
        pM = ctx.enter_context(nc.psum_tensor("pM", [128, 2, 512], F32))

        rev_dram = nc.dram_tensor("rev_scratch", (128, NH * 3 * WIN), F32, kind="Internal")

        x_loaded = [sem(f"x_loaded{m}") for m in range(3)]
        consts_loaded = sem("consts_loaded")
        vecs_loaded = sem("vecs_loaded")
        sink_loaded = sem("sink_loaded")
        ring_full = [sem(f"ring_full{s}") for s in range(SLOTS)]
        ring_free = sem("ring_free")
        extra_full = [sem(f"extra_full{n}") for n in range(len(EXTRA))]
        dve_step = sem("dve_step")
        bias_split = sem("bias_split")
        misc_full = sem("misc_full")
        misc_free = sem("misc_free")
        tile_full = sem("tile_full")
        tile_free_dve = sem("tile_free_dve")
        tile_free_act = sem("tile_free_act")
        cleared = sem("cleared")
        norm_sq = sem("norm_sq")
        norm_in = sem("norm_in")
        norm_rt = sem("norm_rt")
        h_ready = sem("h_ready")
        x_added = sem("x_added")
        rms_ready = sem("rms_ready")
        hn_ready = sem("hn_ready")
        ssink_loaded = sem("ssink_loaded")
        sq_ready = sem("sq_ready")
        qk_normed = sem("qk_normed")
        rt_out = sem("rt_out")
        rev_stored = sem("rev_stored")
        table_loaded = sem("table_loaded")
        stab_loaded = sem("stab_loaded")
        cache_loaded = sem("cache_loaded")
        vnew_loaded = sem("vnew_loaded")
        state_loaded = sem("state_loaded")
        scores_full = sem("scores_full")
        prob_biased = sem("prob_biased")
        exp_done = sem("exp_done")
        prob_ready = sem("prob_ready")
        turned = sem("turned")
        probT_ready = sem("probT_ready")
        sexp_in = sem("sexp_in")
        sexp_done = sem("sexp_done")
        sprob_ready = sem("sprob_ready")
        cg_ready = sem("cg_ready")
        sig_gate = sem("sig_gate")
        sig_used = sem("sig_used")
        out_full = sem("out_full")
        wr_loaded = sem("wr_loaded")
        wr_ready = sem("wr_ready")
        mask_ready = sem("mask_ready")
        ex_in = sem("ex_in")
        ex_out = sem("ex_out")
        route_ready = sem("route_ready")
        bias_loaded = sem("bias_loaded")
        pick_ready = sem("pick_ready")
        gpick_ready = sem("gpick_ready")
        sel_ready = sem("sel_ready")
        up_done = sem("up_done")
        glu_ready = sem("glu_ready")
        sig_ready = sem("sig_ready")
        a_ready = sem("a_ready")
        down_done = sem("down_done")
        y_ready = sem("y_ready")
        y_ready_dve = sem("y_ready_dve")
        stored = sem("stored")
        final_stored = sem("final_stored")

        w_router_sb = sb("w_router_sb", [128, KT, NE])
        block = ctx.enter_context(nc.Block())

        def w_in_chunk(c):
            w = w_in.rearrange("(k p) n -> p k n", p=128)
            if c == 0:
                return [(ring[:, 0, 0:2048].rearrange("p (k h n) -> p k h n", k=KT, h=2)[:, :, h],
                         w[:, :, KC_ + 128 * h:KC_ + 128 * h + 128]) for h in range(2)]
            kind, _, _, t = TILES[2 + 4 * (c - 1)]
            if kind == "q":
                col = QC + t * HD
                dst = ring[:, c % SLOTS, :].rearrange("p (k h n) -> p k h n", k=KT, h=2)
                return [(dst[:, :, h], w[:, :, col + 512 * h:col + 512 * h + 256]) for h in range(2)]
            col = CHUNK_COL[kind] + t * 128
            dst = ring[:, c % SLOTS, :].rearrange("p (k n) -> p k n", k=KT)
            return [(dst[:, k:k + 4], w[:, k:k + 4, col:col + 512]) for k in (0, 4)]

        def filled(c):
            return 32 * (c // SLOTS + 1)

        @block.sync
        def _(sp):
            for m in range(2):
                sp.dma_start(x[:, m, :], x_prompt[0, 128 * m:128 * m + 128, :]).then_inc(x_loaded[m], 16)
            sp.dma_start(x[0:DEC, 2, :], x_sample.rearrange("b t d -> (b t) d")).then_inc(x_loaded[2], 16)
            for row, src in ((V_QN, q_norm_w), (V_KN, k_norm_w)):
                sp.dma_start(rows[row:row + 1, :].rearrange("a (h d) -> a h d", h=2),
                             bass.AP(src.tensor, src.offset, [[0, 1], [0, 2], [1, HD]])).then_inc(vecs_loaded, 16)
            sp.dma_start(rb[:], rel_bias).then_inc(vecs_loaded, 16)
            for c in range(FIRST_CHUNKS):
                if c == 1:
                    sp.wait_ge(consts_loaded, 16)
                    sp.wait_ge(vecs_loaded, 16 * VECS)
                if c >= SLOTS:
                    sp.wait_ge(ring_free, c - SLOTS + 1)
                if c < W_IN_CHUNKS:
                    parts = w_in_chunk(c)
                else:
                    k0 = 4 * (c - W_IN_CHUNKS)
                    wo = w_out.rearrange("(t p) n -> p t n", p=128)
                    dst = ring[:, c % SLOTS, :].rearrange("p (t n) -> p t n", t=4)
                    parts = [(dst[:, t:t + 2], wo[:, k0 + t:k0 + t + 2]) for t in (0, 2)]
                for dst, src in parts:
                    sp.dma_start(dst, src).then_inc(ring_full[c % SLOTS], 16)

            up = w_up.rearrange("(i e) (k p) n -> e k i p n", e=2, p=128)
            down = w_down.rearrange("(i e) (k t p) n -> e k i p t n", e=2, t=2, p=128)

            def load(dst, full, j, i):
                for e in range(2):
                    d = dst[:, e * 2048:(e + 1) * 2048]
                    if j < UP_CHUNKS:
                        src = up[e, j, bass.ds(i, 1)].rearrange("a p n -> (a p) n")
                    else:
                        d = d.rearrange("p (t n) -> p t n", t=2)
                        src = down[e, j - UP_CHUNKS, bass.ds(i, 1)].rearrange("a p t n -> (a p) t n")
                    sp.dma_start(d, src).then_inc(full, 16)

            def pair(g, i):
                for j in range(PAIR_CHUNKS):
                    c = LOOP_CHUNK + j
                    sp.wait_ge(ring_free, PAIR_CHUNKS * g + (c - SLOTS + 1))
                    load(ring[:, c % SLOTS, :], ring_full[c % SLOTS], j, i)

            for j in range(PAIR_CHUNKS):
                if j in EXTRA:
                    if EXTRA[j] == 0:
                        sp.wait_ge(sig_used, 2 * KT)
                        sp.wait_ge(misc_free, FILL["values", 3])
                    elif EXTRA[j] == 1:
                        sp.wait_ge(bias_split, BIAS_STEPS)
                    else:
                        sp.wait_ge(misc_free, FILL["logits", 1])
                    load(extra[EXTRA[j]], extra_full[EXTRA[j]], j, 0)
                else:
                    c = FIRST_PAIR[j]
                    sp.wait_ge(ring_free, c - SLOTS + 1)
                    load(ring[:, c % SLOTS, :], ring_full[c % SLOTS], j, 0)
            with sp.Fori(1, PAIRS) as i:
                pair(i, i)

            def store(fills):
                for m in range(2):
                    sp.wait_ge(misc_free, fills - 4 + 2 * m)
                    sp.dma_start(y_prompt[0, 128 * m:128 * m + 128, :], x[:, m, :]).then_inc(final_stored, 16)
                sp.wait_ge(misc_free, fills)
                sp.dma_start(y_sample.rearrange("b t d -> (b t) d"), x[0:DEC, 2, :]).then_inc(final_stored, 16)

            store(PRE_FILLS + PAIR_FILLS * PAIRS)
            over = sp.value_load(flag[0:1, 0:1], min_val=0, max_val=1)
            sp.wait_ge(final_stored, 48)
            with sp.If(over > 0):
                with sp.Fori(1, PASSES) as q:
                    with sp.Fori(0, PAIRS) as i:
                        pair(q * PAIRS + i, i)
                store(PRE_FILLS + PAIR_FILLS * PAIRS * PASSES)
                sp.wait_ge(final_stored, 96)

        @block.gpsimd
        def _(pool):
            step = Count(bias_split)

            def link(ins):
                ins.then_inc(bias_split, 1)
                pool.wait_ge(bias_split, step.next())

            pool.dma_start(conv_row[0:2 * DEC, :],
                           state_conv.rearrange("b j d -> (b j) d")).then_inc(state_loaded, 16)
            pool.dma_start(w_router_sb[:], w_router.rearrange("(k p) e -> p k e", p=128)).then_inc(wr_loaded, 16)
            pool.dma_start(brouter[:], bass.AP(b_router.tensor, b_router.offset, [[0, 128], [1, NE]])).then_inc(wr_loaded, 16)
            pool.wait_ge(misc_free, FILL["bias_table", 0])
            pool.dma_start(rev_dram[:, :].rearrange("r (h m) -> h r m", h=NH),
                           rev_sb.unsqueeze(1).to_broadcast([NH, 128, 3 * WIN])).then_inc(rev_stored, 16)
            pool.wait_ge(misc_free, FILL["h_cols", 0])
            pool.dma_start(k_cache[0:WIN - 1], cache_k[:, 1:WIN].rearrange("b s h d -> s b (h d)")).then_inc(cache_loaded, 16)
            pool.dma_start(v_cache[0:WIN - 1], cache_v[:, 1:WIN].rearrange("b s h d -> s b (h d)")).then_inc(cache_loaded, 16)
            for kv in range(NKV):
                for b in range(DEC):
                    p = kv * 64 + b * 8
                    pool.dma_start(ssink[p:p + 8, :],
                                   sinks[kv * GROUP:(kv + 1) * GROUP].rearrange("(e a) -> e a", a=1)).then_inc(ssink_loaded, 16)
            pool.wait_ge(rev_stored, 16)

            def load_table(t0):
                for kv in range(NKV):
                    h0 = kv * GROUP + t0
                    src = bass.AP(rev_dram, h0 * 3 * WIN + WIN - 1, [[NH * 3 * WIN - 1, 128], [3 * WIN, 4], [1, 2 * WIN]])
                    pool.dma_start(table[:, 4 * kv:4 * kv + 4, :], src).then_inc(table_loaded, 16)

            load_table(0)
            for kv in range(NKV):
                for b in range(DEC):
                    p = kv * 64 + b * 8
                    pool.dma_start(stab[p:p + 8, :],
                                   rev_dram[0:1, :].rearrange("r (h m) -> (r h) m", h=NH)[
                                       kv * GROUP:(kv + 1) * GROUP, WIN:2 * WIN]).then_inc(stab_loaded, 16)
            pool.dma_start(conv_sample[0, :, 0, :], state_conv[:, 1, :]).then_inc(stored, 16)
            pool.dma_start(k_sample[0, :, 0:WIN - 1].rearrange("b s h d -> b (s h d)"),
                           cache_k[:, 1:WIN].rearrange("b s h d -> b (s h d)")).then_inc(stored, 16)
            pool.dma_start(v_sample[0, :, 0:WIN - 1].rearrange("b s h d -> b (s h d)"),
                           cache_v[:, 1:WIN].rearrange("b s h d -> b (s h d)")).then_inc(stored, 16)
            pool.wait_ge(misc_free, FILL["v_rows", 0])
            pool.dma_start(v_cache[WIN - 1:WIN], v_row[0:DEC, 2, :]).then_inc(vnew_loaded, 16)
            pool.dma_start(v_prompt[0, 0].rearrange("s h d -> s (h d)"), v_row[:, 1, :]).then_inc(stored, 16)
            pool.dma_start(v_sample[0, :, WIN - 1].rearrange("b h d -> b (h d)"), v_row[0:DEC, 2, :]).then_inc(stored, 16)
            pool.wait_ge(misc_free, FILL["k_rows", 0])
            pool.dma_start(k_prompt[0, 0].rearrange("s h d -> s (h d)"), k_row[:, 0, :]).then_inc(stored, 16)
            pool.dma_start(k_sample[0, :, WIN - 1].rearrange("b h d -> b (h d)"), k_row[0:DEC, 1, :]).then_inc(stored, 16)
            pool.wait_ge(prob_biased, 2)
            load_table(4)
            pool.wait_ge(misc_free, FILL["conv_rows", 1])
            pool.dma_start(conv_prompt[0, 0], conv_row[0:2, :]).then_inc(stored, 16)
            pool.dma_start(conv_sample[0, :, 1, :], conv_row[2:2 + DEC, :]).then_inc(stored, 16)

            pool.wait_ge(misc_free, FILL["values", 3])
            loads = 0
            for src, parts, n in ((b_up, bias_up, 2 * FF), (b_down, bias_down, D)):
                raw = bias_raw[:, 0:n]
                for j in range(3):
                    pool.dma_start(raw[32 * j:32 * j + 32], src).then_inc(bias_loaded, 16)
                    loads += 16
                pool.wait_ge(bias_loaded, loads)
                link(pool.tensor_copy(parts[0:96, :], raw[0:96]))
                for j in (1, 2):
                    for r in range(j, 3):
                        s = slice(32 * r, 32 * r + 32)
                        link(pool.tensor_tensor(raw[s], raw[s], parts[s, :], ALU.subtract))
                        link(pool.tensor_copy(parts[s, :], raw[s]))
            pool.wait_ge(stored, 16 * 9)

        @block.scalar
        def _(act):
            act.dma_start(cst[:], consts).then_inc(consts_loaded, 16)
            act.dma_start(rows[V_ANORM:V_ANORM + KT, :], attn_norm_w.rearrange("(k p) -> k p", p=128)).then_inc(vecs_loaded, 16)
            act.dma_start(rows[V_FNORM:V_FNORM + KT, :], ffn_norm_w.rearrange("(k p) -> k p", p=128)).then_inc(vecs_loaded, 16)
            act.dma_start(rows[V_CONV:V_CONV + 3 * KT, :], conv_w.rearrange("j (k p) -> (j k) p", p=128)).then_inc(vecs_loaded, 16)
            for kv in range(NKV):
                act.dma_start(sink[:, kv, :],
                              bass.AP(sinks.tensor, sinks.offset + kv * GROUP, [[0, 128], [1, GROUP]])).then_inc(sink_loaded, 16)

            act.wait_ge(cleared, 1)
            nc.scalar.activation(stat[:, 63:64], stat[:, 62:63], ACT.Sqrt)
            for m in range(3):
                r = TOK[m][1]
                act.wait_ge(x_loaded[m], 16)
                nc.scalar.activation(hn[0:r, m, :], x[0:r, m, :], ACT.Square,
                                     accum_out=stat[0:r, m:m + 1]).then_inc(norm_sq, 1)
                act.wait_ge(norm_in, m + 1)
                nc.scalar.activation(stat[:, 4 + m:5 + m], stat[:, 4 + m:5 + m], ACT.Sqrt).then_inc(norm_rt, 1)

            sigs = 0
            for what, a in STEPS:
                if what == "square":
                    act.wait_ge(tile_free_dve, 1 if a == 0 else a + 2)
                    if a >= 2:
                        act.wait_ge(misc_free, FILL["square", a - 2])
                    src = kT if a == 0 else qT[:, a - 1, :]
                    nc.scalar.activation(tmp[:, a % 2, :], src, ACT.Square).then_inc(sq_ready, 1)
                elif what == "qknorm":
                    act.wait_ge(misc_free, FILL["square", a])
                    nc.scalar.activation(rt[:], rt[:], ACT.Sqrt).then_inc(rt_out, 1)
                elif what == "tile":
                    kind, _, _, t = TILES[a]
                    if kind == "cg":
                        act.wait_ge(tile_full, a + 1)
                        nc.scalar.activation(cx[:, t, 2:], pB[:, a % 2, 0:NT], ACT.Copy).then_inc(tile_free_act, 1)
                    elif kind in ("gc", "ga"):
                        act.wait_ge(tile_full, a + 1)
                        if sigs >= 2:
                            act.wait_ge(sig_used, sigs - 1)
                        else:
                            act.wait_ge(misc_free, FILL["square", 8])
                        nc.scalar.activation(tmp[:, sigs % 2, :], pB[:, a % 2, 0:NT],
                                             ACT.Sigmoid).then_inc(tile_free_act, 1)
                        sigs += 1
                elif what == "exp":
                    keys = WIN * (UNITS[a][0] + 1)
                    act.wait_ge(prob_biased, a + 1)
                    for h in range(8):
                        nc.scalar.activation(prob[:, h, 0:keys], prob[:, h, 0:keys], ACT.Exp,
                                             bias=stat[:, 16 + h:17 + h], accum_out=stat[:, 24 + h:25 + h])
                    nc.scalar.activation(stat[:, 32:40], stat[:, 32:40], ACT.Exp).then_inc(exp_done, 1)
                elif what == "turn":
                    blocks = UNITS[a][0] + 1
                    act.wait_ge(turned, a + 1)
                    if a:
                        act.wait_ge(misc_free, FILL["values", a - 1])
                    for b in range(blocks):
                        ins = nc.scalar.activation(probT[:, b].rearrange("p h q -> p (h q)"),
                                                   pA[:, b * 1024:(b + 1) * 1024], ACT.Copy)
                    ins.then_inc(probT_ready, 1)
                elif what == "s_bias":
                    act.wait_ge(sexp_in, 1)
                    nc.scalar.activation(sprob[:], sprob[:], ACT.Exp, bias=stat[:, 48:49], accum_out=stat[:, 49:50])
                    nc.scalar.activation(stat[:, 50:51], stat[:, 50:51], ACT.Exp).then_inc(sexp_done, 1)

            halves = norms = 0
            for what, a in BRANCH:
                if what == "out":
                    a, half = a
                    r = TOK[a][1]
                    for h in ((0, 1) if a == 2 else (half,)):
                        halves += 1
                        act.wait_ge(x_added, halves)
                        f = slice(512 * h, 512 * h + 512)
                        ins = nc.scalar.activation(hn[0:r, a, f], x[0:r, a, f], ACT.Square,
                                                   accum_out=stat[0:r, 2 * a + h:2 * a + h + 1])
                    if a < 2 and half == 0:
                        continue
                    ins.then_inc(norm_sq, 1)
                    norms += 1
                    act.wait_ge(norm_in, 3 + norms)
                    nc.scalar.activation(stat[0:r, 8 + a:9 + a], stat[0:r, 8 + a:9 + a], ACT.Sqrt).then_inc(norm_rt, 1)
                    act.wait_ge(rms_ready, norms)
                    nc.scalar.activation(hn[0:r, a, :], x[0:r, a, :], ACT.Copy,
                                         scale=stat[0:r, 12 + a:13 + a]).then_inc(hn_ready, 1)
            for n, a in enumerate((2, 0, 1)):
                r = TOK[a][1]
                act.wait_ge(ex_in, n + 1)
                nc.scalar.activation(gate[0:r, a, :], lg[0:r, a, :], ACT.Exp,
                                     bias=stat[0:r, 52 + a:53 + a]).then_inc(ex_out, 1)

            def pair(g, i):
                act.wait_ge(glu_ready, g + 1)
                nc.scalar.activation(sig, glu, ACT.Sigmoid, scale=ALPHA).then_inc(sig_ready, 1)
                act.wait_ge(down_done, g + 1)
                nc.scalar.activation(y_pair[:, 0:512], pB[:, 0, :], ACT.Copy).then_inc(y_ready, 1)

            with act.Fori(0, PAIRS) as i:
                pair(i, i)
            act.wait_ge(misc_free, FILL["route", 0])
            over = act.value_load(flag[0:1, 0:1], min_val=0, max_val=1)
            with act.If(over > 0):
                with act.Fori(1, PASSES) as q:
                    with act.Fori(0, PAIRS) as i:
                        pair(q * PAIRS + i, i)

        @block.vector
        def _(dve):
            V = nc.vector
            step = Count(dve_step)

            def link(ins):
                ins.then_inc(dve_step, 1)
                dve.wait_ge(dve_step, step.next())

            misc = Count(misc_full)

            def misc_bank():
                n = misc.next()
                dve.wait_ge(misc_full, n)
                return pM[:, (n - 1) % 2, :]

            V.memset(stat[:], 0.0)
            V.memset(cx[:, :, 0:2], 0.0)
            for t in (lg, mask, t32, gate):
                V.memset(t[:], 0.0)
            link(V.memset(rev_sb, NEG))
            V.memset(flag_f32[:], 0.0).then_inc(cleared, 1)
            for m, (_, r) in enumerate(TOK):
                dve.wait_ge(norm_sq, m + 1)
                V.tensor_scalar(stat[:, 4 + m:5 + m], stat[:, m:m + 1], 1.0 / D, EPS,
                                ALU.mult, ALU.add).then_inc(norm_in, 1)
                dve.wait_ge(norm_rt, m + 1)
                link(V.reciprocal(stat[:, 8 + m:9 + m], stat[:, 4 + m:5 + m]))
                V.tensor_scalar(hn[0:r, m, :], x[0:r, m, :], stat[0:r, 8 + m:9 + m], None,
                                ALU.mult).then_inc(h_ready, 1)

            def columns(n, scale):
                m, k0, nk = COLS[n]
                t0, r = TOK[m]
                src = misc_bank()[:, 0:nk * r].rearrange("p (k n) -> p k n", k=nk)
                dst = hT[:, k0:k0 + nk, t0:t0 + r]
                if scale is None:
                    return V.tensor_copy(dst, src)
                return V.tensor_tensor(dst, src, cols[:, scale + k0:scale + k0 + nk].unsqueeze(2)
                                       .to_broadcast([128, nk, r]), ALU.mult)

            freed = 0
            for what, a in STEPS:
                if what == "vectors":
                    V.tensor_copy(cols[:], misc_bank()[:, 0:V_N]).then_inc(misc_free, 1)
                elif what == "bias_table":
                    b = misc_bank()
                    V.tensor_copy(rev_sb[:, WIN:2 * WIN], b[0:NH, 0:128]).then_inc(misc_free, 1)
                elif what == "h_cols":
                    if a == COLS_FIRST:
                        dve.wait_ge(misc_free, 1)
                    columns(a, V_ANORM).then_inc(misc_free, 1)
                elif what == "tile":
                    kind, _, _, t = TILES[a]
                    src = pB[:, a % 2, 0:NT]
                    if kind in ("k", "q", "v"):
                        dve.wait_ge(tile_full, a + 1)
                        dst = {"k": kT, "v": vT, "q": qT[:, t, :]}[kind]
                        V.tensor_copy(dst, src).then_inc(tile_free_dve, 1)
                    elif kind == "xin":
                        dve.wait_ge(tile_full, a + 1)
                        dve.wait_ge(tile_free_act, ACT_TILES[a])
                        V.tensor_tensor(cx[:, t, 2:], src, cx[:, t, 2:], ALU.mult).then_inc(tile_free_dve, 1)
                        dve.wait_ge(tile_free_dve, DVE_TILES[a] + 1)
                        w = [cols[:, V_CONV + 8 * j + t:V_CONV + 8 * j + t + 1] for j in range(3)]
                        taps = [cx[:, t, j:j + SEQ] for j in range(3)]
                        s_taps = [state_c[:, t, :, 0], state_c[:, t, :, 1], cx[:, t, 2 + SEQ:]]
                        V.tensor_scalar(yc[:, t, 0:SEQ], taps[0], w[0], None, ALU.mult)
                        link(V.tensor_scalar(yc[:, t, SEQ:], s_taps[0], w[0], None, ALU.mult))
                        for j in (1, 2):
                            V.scalar_tensor_tensor(out=yc[:, t, 0:SEQ], in0=taps[j], scalar=w[j],
                                                   in1=yc[:, t, 0:SEQ], op0=ALU.mult, op1=ALU.add)
                            link(V.scalar_tensor_tensor(out=yc[:, t, SEQ:], in0=s_taps[j], scalar=w[j],
                                                        in1=yc[:, t, SEQ:], op0=ALU.mult, op1=ALU.add))
                    elif kind == "bg":
                        dve.wait_ge(tile_full, a + 1)
                        V.tensor_tensor(yc[:, t, :], src, yc[:, t, :], ALU.mult).then_inc(tile_free_dve, 1)
                    elif kind == "gc":
                        dve.wait_ge(tile_free_act, ACT_TILES[a] + 1)
                        dve.wait_ge(tile_free_dve, DVE_TILES[a])
                        V.tensor_tensor(yc[:, t, :], tmp[:, freed % 2, :], yc[:, t, :], ALU.mult).then_inc(sig_used, 1)
                        freed += 1
                    elif kind == "ga":
                        dve.wait_ge(tile_free_act, ACT_TILES[a] + 1)
                        dve.wait_ge(sig_used, freed)
                        dve.wait_ge(misc_free, misc.n)
                        g = tmp[:, freed % 2, :]
                        link(V.tensor_tensor(g, g, ya[:, t, :], ALU.mult))
                        V.tensor_tensor(yc[:, t, :], g, yc[:, t, :], ALU.add).then_inc(sig_used, 1)
                        freed += 1
                elif what == "square":
                    b = misc_bank()
                    if a:
                        dve.wait_ge(qk_normed, a)
                    V.tensor_scalar(rt[:], b[:, 0:NT], 1.0 / HD, EPS, ALU.mult, ALU.add).then_inc(misc_free, 1)
                elif what == "qknorm":
                    dve.wait_ge(rt_out, a + 1)
                    link(V.reciprocal(rt[:], rt[:]))
                    dst, w = (kT, V_KN) if a == 0 else (qT[:, a - 1, :], V_QN)
                    V.scalar_tensor_tensor(out=dst, in0=dst, scalar=cols[:, w:w + 1], in1=rt[:],
                                           op0=ALU.mult, op1=ALU.mult).then_inc(qk_normed, 1)
                elif what == "v_rows":
                    b = misc_bank()
                    V.tensor_copy(v_row[0:DEC, 2, :], b[0:DEC, 256:384])
                    V.tensor_copy(v_row[:, 0:2, :].rearrange("p m f -> p (m f)"), b[:, 0:256]).then_inc(misc_free, 1)
                elif what == "k_rows":
                    b = misc_bank()
                    V.tensor_copy(k_row[0:DEC, 1, :], b[0:DEC, 128:256])
                    V.tensor_copy(k_row[:, 0, :], b[:, 0:128]).then_inc(misc_free, 1)
                elif what == "state_cols":
                    V.tensor_copy(state_c[:].rearrange("p k b j -> p (k b j)"),
                                  misc_bank()[:, 0:KT * 2 * DEC]).then_inc(misc_free, 1)
                elif what == "cache_cols":
                    b = misc_bank()
                    dve.wait_ge(qk_normed, 1)
                    V.tensor_copy(k_cacheT[:, 4 * a:4 * a + 4, 0:WIN - 1],
                                  b.rearrange("p (b s) -> p b s", b=4)[:, :, 0:WIN - 1])
                    V.tensor_copy(k_cacheT[:, 4 * a:4 * a + 4, WIN - 1],
                                  kT[:, SEQ + 4 * a:SEQ + 4 * a + 4]).then_inc(misc_free, 1)
                elif what == "bias":
                    q, t0 = UNITS[a]
                    keys = WIN * (q + 1)
                    dve.wait_ge(scores_full, a + 1)
                    dve.wait_ge(table_loaded, 32 * (a // 2 + 1))
                    if a:
                        dve.wait_ge(turned, a)
                    for kv in range(NKV):
                        ins = V.scalar_tensor_tensor(
                            out=prob[:, 4 * kv:4 * kv + 4, 0:keys],
                            in0=pA[:, 1024 * kv:1024 * kv + 4 * keys].rearrange("p (t s) -> p t s", t=4),
                            scalar=HD ** -0.5, in1=table[:, 4 * kv:4 * kv + 4, 2 * WIN - keys:],
                            op0=ALU.mult, op1=ALU.add)
                    link(ins)
                    link(V.tensor_reduce(stat[:, 16:24], prob[:, :, 0:keys], AX.X, ALU.max))
                    if a == 0:
                        dve.wait_ge(sink_loaded, 32)
                    s = sink[:, :, t0:t0 + 4]
                    m = stat[:, 16:24].rearrange("p (a b) -> p a b", a=2)
                    link(V.tensor_tensor(m, m, s, ALU.max))
                    link(V.tensor_scalar(stat[:, 16:24], stat[:, 16:24], -1.0, None, ALU.mult))
                    V.tensor_tensor(stat[:, 32:40].rearrange("p (a b) -> p a b", a=2), m, s,
                                    ALU.add).then_inc(prob_biased, 1)
                elif what == "norm":
                    keys = WIN * (UNITS[a][0] + 1)
                    dve.wait_ge(exp_done, a + 1)
                    link(V.tensor_tensor(stat[:, 24:32], stat[:, 24:32], stat[:, 32:40], ALU.add))
                    link(V.reciprocal(stat[:, 40:48], stat[:, 24:32]))
                    for h in range(8):
                        ins = V.tensor_scalar(prob[:, h, 0:keys], prob[:, h, 0:keys], stat[:, 40 + h:41 + h], None,
                                              ALU.mult)
                    ins.then_inc(prob_ready, 1)
                elif what == "values":
                    q, t0 = UNITS[a]
                    b = misc_bank()
                    dst = ya[:].rearrange("p (kv j) n -> p kv j n", kv=NKV)
                    V.tensor_copy(dst[:, :, t0 // 2:t0 // 2 + 2, 128 * q:128 * q + 128],
                                  b.rearrange("p (kv j n) -> p kv j n", kv=NKV, j=2)).then_inc(misc_free, 1)
                elif what == "s_scores":
                    for kv in range(NKV):
                        V.tensor_copy(sprobT[:, 64 * kv:64 * kv + 64], misc_bank()[:, 0:64]).then_inc(misc_free, 1)
                elif what == "s_bias":
                    b = misc_bank()
                    dve.wait_ge(stab_loaded, 16 * 16)
                    V.scalar_tensor_tensor(out=sprob[:], in0=b[:, 0:128], scalar=HD ** -0.5, in1=stab[:],
                                           op0=ALU.mult, op1=ALU.add).then_inc(misc_free, 1)
                    dve.wait_ge(misc_free, misc.n)
                    link(V.tensor_reduce(stat[:, 48:49], sprob[:], AX.X, ALU.max))
                    dve.wait_ge(ssink_loaded, 16 * 2 * DEC)
                    link(V.tensor_tensor(stat[:, 48:49], stat[:, 48:49], ssink[:], ALU.max))
                    link(V.tensor_scalar(stat[:, 48:49], stat[:, 48:49], -1.0, None, ALU.mult))
                    V.tensor_tensor(stat[:, 50:51], stat[:, 48:49], ssink[:], ALU.add).then_inc(sexp_in, 1)
                elif what == "s_norm":
                    dve.wait_ge(sexp_done, 1)
                    link(V.tensor_tensor(stat[:, 49:50], stat[:, 49:50], stat[:, 50:51], ALU.add))
                    link(V.reciprocal(stat[:, 51:52], stat[:, 49:50]))
                    V.tensor_scalar(sprob[:], sprob[:], stat[:, 51:52], None, ALU.mult).then_inc(sprob_ready, 1)
                elif what == "s_turn":
                    V.tensor_copy(sprobT[:], misc_bank()[:, 0:128]).then_inc(misc_free, 1)
                elif what == "s_values":
                    b = misc_bank()
                    V.tensor_copy(ya[:, :, SEQ:].rearrange("p t b -> p b t"),
                                  b[:, 0:64].rearrange("p (b t) -> p b t", b=DEC)).then_inc(misc_free, 1)
                elif what == "conv_rows":
                    b = misc_bank()
                    V.tensor_copy(conv_row[0:2 + DEC, 512 * a:512 * a + 512], b[0:2 + DEC, :]).then_inc(misc_free, 1)

            dve.wait_ge(wr_loaded, 32)
            for k in range(KT):
                ins = V.tensor_scalar(w_router_sb[:, k, :], w_router_sb[:, k, :],
                                      cols[:, V_FNORM + k:V_FNORM + k + 1], None, ALU.mult)
            ins.then_inc(wr_ready, 1)

            fulls = norms = 0
            for what, a in BRANCH:
                if what == "out":
                    a, half = a
                    r = TOK[a][1]
                    for h in ((0, 1) if a == 2 else (half,)):
                        xs = x[0:r, a, 512 * h:512 * h + 512]
                        if a < 2:
                            fulls += 1
                            dve.wait_ge(out_full, fulls)
                            o = 1024 * a + 512 * h
                            V.tensor_tensor(xs, pA[:, o:o + 512], xs, ALU.add).then_inc(x_added, 1)
                            continue
                        if h == 0:
                            fulls += 1
                            dve.wait_ge(out_full, fulls)
                        for j in range(4):
                            ins = V.tensor_tensor(xs, pB[32 * j:32 * j + DEC, h, :], xs, ALU.add)
                            if j < 3:
                                link(ins)
                        ins.then_inc(x_added, 1)
                    if a < 2 and half == 0:
                        continue
                    norms += 1
                    dve.wait_ge(norm_sq, 3 + norms)
                    s1 = stat[0:r, 2 * a + 1:2 * a + 2]
                    link(V.tensor_tensor(s1, s1, stat[0:r, 2 * a:2 * a + 1], ALU.add))
                    V.tensor_scalar(stat[0:r, 8 + a:9 + a], s1, 1.0 / D, EPS, ALU.mult, ALU.add).then_inc(norm_in, 1)
                    dve.wait_ge(norm_rt, 3 + norms)
                    V.reciprocal(stat[0:r, 12 + a:13 + a], stat[0:r, 8 + a:9 + a]).then_inc(rms_ready, 1)
                elif what == "x_cols":
                    columns(a, None).then_inc(misc_free, 1)
                elif what == "logits":
                    r = TOK[a][1]
                    rows_ = slice(0, r)
                    l, e, c, g = lg[rows_, a, :], t32[rows_, a, :], mask[rows_, a, :], gate[rows_, a, :]
                    b = misc_bank()
                    dve.wait_ge(rms_ready, norms)
                    V.scalar_tensor_tensor(out=l, in0=b[rows_, 0:NE], scalar=stat[rows_, 12 + a:13 + a],
                                           in1=brouter[rows_, :], op0=ALU.mult, op1=ALU.add).then_inc(misc_free, 1)
                    dve.wait_ge(misc_free, misc.n)
                    link(V.max(top8[rows_, a, :], l))
                    V.tensor_scalar(stat[rows_, 52 + a:53 + a], top8[rows_, a, 0:1], -1.0, None,
                                    ALU.mult).then_inc(ex_in, 1)
                    least = top8[rows_, a, TOPK - 1:TOPK]
                    V.tensor_scalar(c, l, least, None, ALU.is_gt, ALU.add, accum_out=stat[rows_, 56 + a:57 + a])
                    link(V.tensor_scalar(e, l, least, None, ALU.is_equal))
                    V.tensor_scalar(stat[rows_, 56 + a:57 + a], stat[rows_, 56 + a:57 + a], -1.0, float(TOPK),
                                    ALU.mult, ALU.add)
                    link(V.tensor_tensor_scan(rank[rows_, :], cst[rows_, C_ONE:C_ONE + NE], e, 0.0,
                                              ALU.mult, ALU.add))
                    link(V.scalar_tensor_tensor(out=e, in0=rank[rows_, :], scalar=stat[rows_, 56 + a:57 + a],
                                                in1=e, op0=ALU.is_le, op1=ALU.mult))
                    V.tensor_tensor(c, c, e, ALU.add).then_inc(mask_ready, 1)

            b = misc_bank()
            V.scalar_tensor_tensor(out=t32[:, 0:2, :].rearrange("p m e -> p (m e)"), in0=b[:, 0:2 * NE], scalar=1.0,
                                   in1=mask[:, 0:2, :].rearrange("p m e -> p (m e)"), op0=ALU.add, op1=ALU.mult)
            link(V.scalar_tensor_tensor(out=t32[0:DEC, 2, :], in0=b[0:DEC, 2 * NE:3 * NE], scalar=1.0,
                                        in1=mask[0:DEC, 2, :], op0=ALU.add, op1=ALU.mult))
            V.memset(pos[:, :, PASSES * NE:], -1.0)
            link(V.tensor_scalar(pos[:, :, 0:NE], t32[:], -1.0, None, ALU.add))

            iota = cst[:, C_IOTA:C_IOTA + CAP].unsqueeze(1).unsqueeze(1).to_broadcast([128, 3, 2, CAP])

            def picks(g1):
                return V.tensor_tensor(pick, iota, pos[:, :, bass.ds(g1 * 2, 2)].unsqueeze(3).to_broadcast([128, 3, 2, CAP]),
                                       ALU.is_equal)

            picks(0).then_inc(pick_ready, 1)
            for n, a in enumerate((2, 0, 1)):
                rows_ = slice(0, TOK[a][1])
                g = gate[rows_, a, :]
                dve.wait_ge(ex_out, n + 1)
                dve.wait_ge(mask_ready, n + 1)
                link(V.scalar_tensor_tensor(out=g, in0=g, scalar=1.0, in1=mask[rows_, a, :], op0=ALU.mult,
                                            op1=ALU.mult, accum_out=stat[rows_, 60:61]))
                link(V.reciprocal(stat[rows_, 61:62], stat[rows_, 60:61]))
                link(V.tensor_scalar(g, g, stat[rows_, 61:62], None, ALU.mult))
            for q in range(1, PASSES):
                V.tensor_scalar(pos[:, :, q * NE:(q + 1) * NE], t32[:], -1.0 - CAP * q, None, ALU.add)
            link(V.tensor_reduce(stat[:, 60:61], b[:, 3 * NE:4 * NE], AX.X, ALU.max))
            link(V.tensor_scalar(flag_f32[:], stat[0:1, 60:61], float(CAP), None, ALU.is_gt))
            V.tensor_copy(flag[0:1, 0:1], flag_f32[:]).then_inc(misc_free, 1)
            fw = cols[:, V_FNORM:V_FNORM + KT].unsqueeze(2).to_broadcast([128, KT, 128])

            def gathered(half, b):
                return V.tensor_tensor(xsT[:, 4 * half:4 * half + 4, :], b.rearrange("p (k s) -> p k s", k=4),
                                       fw[:, 4 * half:4 * half + 4, :], ALU.mult)

            for half in range(2):
                gathered(half, misc_bank()).then_inc(misc_free, 1)
            misc0 = misc.n
            assert misc0 == PRE_FILLS, misc0
            step0 = step.n
            LINKS = 2

            def pair(g, i):
                n = 0
                base = step0 + LINKS * g

                def link(ins):
                    nonlocal n
                    n += 1
                    ins.then_inc(dve_step, 1)
                    dve.wait_ge(dve_step, base + n)

                def bank(k):
                    dve.wait_ge(misc_full, PAIR_FILLS * g + (misc0 + k + 1))
                    return pM[:, (misc0 + k) % 2, :]

                V.tensor_copy(sel[0:96], cst[0:96, C_SEL:C_SEL + NE][:, bass.ds(i * 2, 2)].unsqueeze(2)
                              .to_broadcast([96, 2, CAP])).then_inc(sel_ready, 1)
                dve.wait_ge(pick_ready, g + 1)
                V.tensor_tensor(gpick, pick, gate[:, :, bass.ds(i * 2, 2)].unsqueeze(3)
                                .to_broadcast([128, 3, 2, CAP]), ALU.mult).then_inc(gpick_ready, 1)
                dve.wait_ge(gpick_ready, g + 1)
                picks(g + 1).then_inc(pick_ready, 1)
                dve.wait_ge(up_done, g + 1)
                u = pA[:].rearrange("p (f two) -> p two f", two=2)
                V.tensor_scalar(glu, u[:, 0], LIMIT, None, ALU.min).then_inc(glu_ready, 1)
                dve.wait_ge(glu_ready, g + 1)
                link(V.tensor_scalar(lin, u[:, 1], -LIMIT, LIMIT, ALU.max, ALU.min))
                link(V.scalar_tensor_tensor(out=lin, in0=lin, scalar=1.0, in1=glu, op0=ALU.add, op1=ALU.mult))
                dve.wait_ge(sig_ready, g + 1)
                V.tensor_tensor(act_out, lin, sig, ALU.mult).then_inc(a_ready, 1)
                for half in range(2):
                    gathered(half, bank(half)).then_inc(misc_free, 1)
                V.tensor_copy(gateT, bank(2)[:, 0:NT]).then_inc(misc_free, 1)
                for half in range(2):
                    V.tensor_copy(aT[:, 4 * half:4 * half + 4, :].rearrange("p k s -> p (k s)"),
                                  bank(3 + half)).then_inc(misc_free, 1)
                dve.wait_ge(down_done, g + 1)
                V.tensor_copy(y_pair[:, 512:1024], pB[:, 1, :]).then_inc(y_ready_dve, 1)
                for k in range(6):
                    m, h = k // 2, k % 2
                    r = TOK[m][1]
                    xs = x[0:r, m, 512 * h:512 * h + 512]
                    V.tensor_tensor(xs, bank(5 + k)[0:r], xs, ALU.add).then_inc(misc_free, 1)
                dve.wait_ge(misc_free, PAIR_FILLS * g + (misc0 + PAIR_FILLS))
                assert n == LINKS

            with dve.Fori(0, PAIRS) as i:
                pair(i, i)
            dve.wait_ge(misc_free, FILL["route", 0])
            over = dve.value_load(flag[0:1, 0:1], min_val=0, max_val=1)
            with dve.If(over > 0):
                dve.wait_ge(final_stored, 48)
                with dve.Fori(1, PASSES) as q:
                    with dve.Fori(0, PAIRS) as i:
                        pair(q * PAIRS + i, i)

        @block.tensor
        def _(pe):
            fills = Count(misc_full)

            def misc_bank():
                if fills.n >= 2:
                    pe.wait_ge(misc_free, fills.n - 1)
                return pM[:, (fills.next() - 1) % 2, :]

            def matmul(out, w, m, start=True, stop=True):
                return pe.matmul(out, w, m, start=start, stop=stop, skip_group_check=True)

            def tr(out, src):
                return pe.transpose(out, src, ident[0:src.shape[0], 0:src.shape[0]])

            def columns(n, src, b):
                m, k0, nk = COLS[n]
                r = TOK[m][1]
                mms = [tr(b[:, r * k:r * k + r], src[0:r, m, 128 * (k0 + k):128 * (k0 + k) + 128]) for k in range(nk)]
                mms[-1].then_inc(misc_full, 1)
                return mms[0]

            pe.wait_ge(consts_loaded, 16)
            pe.wait_ge(vecs_loaded, 16 * VECS)
            for what, a in STEPS:
                if what == "vectors":
                    tr(misc_bank()[:, 0:V_N], rows[0:V_N, :]).then_inc(misc_full, 1)
                elif what == "bias_table":
                    matmul(misc_bank()[0:NH, 0:128], rb[:], cst[0:NBUCKET, C_BUCKET:C_BUCKET + 128]).then_inc(misc_full, 1)
                elif what == "h_cols":
                    b = misc_bank()
                    pe.wait_ge(h_ready, (3, 1, 1, 2, 2)[a])
                    columns(a, hn, b)
                elif what == "tile":
                    kind, c, j, t = TILES[a]
                    if j == 0:
                        pe.wait_ge(ring_full[c % SLOTS], filled(c))
                    if a == 0:
                        pe.wait_ge(misc_free, FILL["h_cols", 0])
                    if a >= 2:
                        if TILES[a - 2][0] in ("cg", "gc", "ga"):
                            pe.wait_ge(tile_free_act, ACT_TILES[a - 2] + 1)
                        else:
                            pe.wait_ge(tile_free_dve, DVE_TILES[a - 2] + 1)
                    for k in range(KT):
                        if c == 0:
                            w = ring[:, 0, 0:2048].rearrange("p (k n) -> p k n", k=KT)[:, k, 128 * j:128 * j + 128]
                            mm = matmul(pB[:, a % 2, 0:NT], w, hT[:, k, :], start=(k == 0), stop=(k == KT - 1))
                            continue
                        if kind != "q":
                            w = ring[:, c % SLOTS, :].rearrange("p (k n) -> p k n", k=KT)[:, k, 128 * j:128 * j + 128]
                            mm = matmul(pB[:, a % 2, 0:NT], w, hT[:, k, :], start=(k == 0), stop=(k == KT - 1))
                            if k == 0 and j == 0:
                                mm.then_inc(ring_free, 1)
                            continue
                        w = ring[:, c % SLOTS, :].rearrange("p (k h n) -> p k h n", k=KT, h=2)
                        for h in range(2):
                            mm = matmul(pB[HD * h:HD * h + HD, a % 2, 0:NT], w[:, k, h, HD * j:HD * j + HD],
                                        hT[:, k, :], start=(k == 0), stop=(k == KT - 1))
                            if k == 0 and j == 0 and h == 0:
                                mm.then_inc(ring_free, 1)
                    mm.then_inc(tile_full, 1)
                elif what == "square":
                    b = misc_bank()
                    pe.wait_ge(sq_ready, a + 1)
                    matmul(b[:, 0:NT], cst[:, C_BLK:C_BLK + 128], tmp[:, a % 2, :]).then_inc(misc_full, 1)
                elif what == "v_rows":
                    b = misc_bank()
                    pe.wait_ge(tile_free_dve, 2)
                    for m, (t0, r) in enumerate(TOK):
                        mm = tr(b[0:r, 128 * m:128 * m + 128], vT[:, t0:t0 + r])
                    mm.then_inc(misc_full, 1)
                elif what == "k_rows":
                    b = misc_bank()
                    pe.wait_ge(qk_normed, 1)
                    tr(b[:, 0:128], kT[:, 128:256])
                    tr(b[0:DEC, 128:256], kT[:, 256:NT]).then_inc(misc_full, 1)
                elif what == "state_cols":
                    b = misc_bank()
                    pe.wait_ge(state_loaded, 16)
                    for t in range(KT):
                        mm = tr(b[:, 16 * t:16 * t + 16], conv_row[0:2 * DEC, 128 * t:128 * t + 128])
                    mm.then_inc(misc_full, 1)
                elif what == "cache_cols":
                    b = misc_bank()
                    pe.wait_ge(cache_loaded, 32)
                    for n in range(4):
                        mm = tr(b[:, 128 * n:128 * n + 127], k_cache[0:WIN - 1, 4 * a + n, :])
                    mm.then_inc(misc_full, 1)
                elif what == "scores":
                    q, t0 = UNITS[a]
                    keys = WIN * (q + 1)
                    pe.wait_ge(qk_normed, 9)
                    if a:
                        pe.wait_ge(probT_ready, a)
                    for t in range(4):
                        for kv in range(NKV):
                            s = slice(HD * kv, HD * kv + HD)
                            o = 1024 * kv + t * keys
                            mm = matmul(pA[:, o:o + keys], qT[s, t0 + t, 128 * q:128 * q + 128],
                                        kT[s, 0:keys])
                    mm.then_inc(scores_full, 1)
                elif what == "turn":
                    q, t0 = UNITS[a]
                    pe.wait_ge(prob_ready, a + 1)
                    for b in range(q + 1):
                        for h in range(8):
                            o = (8 * b + h) * 128
                            mm = tr(pA[:, o:o + 128], prob[:, h, 128 * b:128 * b + 128])
                    mm.then_inc(turned, 1)
                elif what == "values":
                    q, t0 = UNITS[a]
                    o = misc_bank()
                    pe.wait_ge(probT_ready, a + 1)
                    for kv in range(NKV):
                        for b in range(q + 1):
                            for odd in range(2):
                                mm = matmul(o[HD * odd:HD * odd + HD, 256 * kv:256 * kv + 256],
                                            v_row[:, b, HD * kv:HD * kv + HD],
                                            probT[:, b, 4 * kv + odd:4 * kv + 4:2, :],
                                            start=(b == 0), stop=(b == q))
                    mm.then_inc(misc_full, 1)
                elif what == "s_scores":
                    for kv in range(NKV):
                        b = misc_bank()
                        s = slice(HD * kv, HD * kv + HD)
                        for n in range(DEC):
                            mm = matmul(b[:, 8 * n:8 * n + 8], k_cacheT[s, n, :], qT[s, :, SEQ + n])
                        mm.then_inc(misc_full, 1)
                elif what == "s_bias":
                    b = misc_bank()
                    pe.wait_ge(misc_free, fills.n - 1)
                    tr(b[:, 0:128], sprobT[:]).then_inc(misc_full, 1)
                elif what == "s_turn":
                    b = misc_bank()
                    pe.wait_ge(sprob_ready, 1)
                    tr(b[:, 0:128], sprob[:]).then_inc(misc_full, 1)
                elif what == "s_values":
                    b = misc_bank()
                    pe.wait_ge(misc_free, fills.n - 1)
                    pe.wait_ge(vnew_loaded, 16)
                    pe.wait_ge(cache_loaded, 32)
                    for n in range(DEC):
                        for kv in range(NKV):
                            for odd in range(2):
                                o = 64 * kv + 8 * n
                                mm = matmul(b[HD * odd:HD * odd + HD, 8 * n + 4 * kv:8 * n + 4 * kv + 4],
                                            v_cache[:, n, HD * kv:HD * kv + HD], sprobT[:, o + odd:o + 8:2])
                    mm.then_inc(misc_full, 1)
                elif what == "conv_rows":
                    b = misc_bank()
                    pe.wait_ge(tile_free_dve, DVE_TILES[XIN_END[a]])
                    for t in range(4):
                        mm = tr(b[0:2 + DEC, 128 * t:128 * t + 128], cx[:, 4 * a + t, SEQ:])
                    mm.then_inc(misc_full, 1)

            pe.wait_ge(probT_ready, len(UNITS))
            pe.wait_ge(tile_free_act, ACT_TILES[len(TILES)])
            norms = 0
            for what, a in BRANCH:
                if what == "out":
                    a, n = a
                    t0, r = TOK[a]
                    w = [ring[:, (W_IN_CHUNKS + k // 4) % SLOTS, 1024 * (k % 4):1024 * (k % 4) + 1024] for k in range(KT)]
                    if a == 2:
                        for k0 in (0, 4):
                            ch = W_IN_CHUNKS + k0 // 4
                            pe.wait_ge(ring_full[ch % SLOTS], filled(ch))
                            pe.wait_ge(sig_used, KT + k0 + 4)
                            for n in range(2):
                                for j in range(4):
                                    mm = matmul(pB[32 * j:32 * j + r, n, :], yc[:, k0 + j, t0:t0 + r],
                                                w[k0 + j][:, 512 * n:512 * n + 512], start=(k0 == 0), stop=(k0 == 4))
                                    if k0 == 0 and n == 0 and j == 0:
                                        mm.then_inc(ring_free, 1)
                        mm.then_inc(out_full, 1)
                        continue
                    for k in range(KT):
                        o = 1024 * a + 512 * n
                        mm = matmul(pA[:, o:o + 512], yc[:, k, t0:t0 + r], w[k][:, 512 * n:512 * n + 512],
                                    start=(k == 0), stop=(k == KT - 1))
                        if a == 1 and n == 1 and k == 4:
                            mm.then_inc(ring_free, 1)
                    mm.then_inc(out_full, 1)
                elif what == "x_cols":
                    b = misc_bank()
                    if a == 0:
                        pe.wait_ge(x_added, 2)
                    else:
                        pe.wait_ge(x_added, a + 2)
                    mm = columns(a, x, b)
                    if a == 3:
                        mm.then_inc(ring_free, 1)
                elif what == "logits":
                    b = misc_bank()
                    t0, r = TOK[a]
                    pe.wait_ge(misc_free, FILL["x_cols", {2: 0, 0: 2, 1: 4}[a]])
                    pe.wait_ge(wr_ready, 1)
                    for k in range(KT):
                        mm = matmul(b[0:r, 0:NE], hT[:, k, t0:t0 + r], w_router_sb[:, k, :],
                                    start=(k == 0), stop=(k == KT - 1))
                    mm.then_inc(misc_full, 1)

            b = misc_bank()
            pe.wait_ge(mask_ready, 2)
            for m in range(4):
                out_rows = TOK[m][1] if m < 3 else 128
                if m == 1:
                    pe.wait_ge(mask_ready, 3)
                for s in range(min(m, 2) + 1):
                    c, rs = (C_TRI if s == m else C_ONE), TOK[s][1]
                    mm = matmul(b[0:out_rows, NE * m:NE * m + NE], cst[0:rs, c:c + out_rows], mask[0:rs, s, :],
                                start=(s == 0), stop=(s == min(m, 2)))
            mm.then_inc(misc_full, 1)

            def gather(bank):
                for half in range(2):
                    b = bank(half)
                    for k in range(4):
                        f = 128 * (4 * half + k)
                        for m, (_, r) in enumerate(TOK):
                            mm = matmul(b[:, 128 * k:128 * k + 128], hn[0:r, m, f:f + 128],
                                        pick[0:r, m].rearrange("p e s -> p (e s)"), start=(m == 0), stop=(m == 2))
                    mm.then_inc(misc_full, 1)

            pe.wait_ge(pick_ready, 1)
            pe.wait_ge(hn_ready, 3)
            gather(lambda half: misc_bank())
            misc0 = fills.n
            assert misc0 == PRE_FILLS, misc0
            pe.wait_ge(bias_split, BIAS_STEPS)

            def pair(g, i, first=False):
                def bank(k):
                    pe.wait_ge(misc_free, PAIR_FILLS * g + (misc0 + k - 1))
                    return pM[:, (misc0 + k) % 2, :]

                def chunk(j):
                    if first and j in EXTRA:
                        pe.wait_ge(extra_full[EXTRA[j]], 32)
                        return extra[EXTRA[j]], False
                    if first:
                        c = FIRST_PAIR[j]
                        pe.wait_ge(ring_full[c % SLOTS], filled(c))
                    else:
                        c = LOOP_CHUNK + j
                        pe.wait_ge(ring_full[c % SLOTS], 64 * g + filled(c))
                    return ring[:, c % SLOTS, :], True

                for k in range(UP_CHUNKS):
                    if k % 4 == 0:
                        pe.wait_ge(misc_free, PAIR_FILLS * g + (misc0 - 1 + k // 4))
                    w, in_ring = chunk(k)
                    for n in range(4):
                        for e in range(2):
                            mm = matmul(pA[64 * e:64 * e + 64, 512 * n:512 * n + 512], xsT[:, k, 64 * e:64 * e + 64],
                                        w[:, 2048 * e + 512 * n:2048 * e + 512 * n + 512],
                                        start=(k == 0), stop=False)
                    if in_ring:
                        mm.then_inc(ring_free, 1)
                pe.wait_ge(sel_ready, g + 1)
                for n in range(4):
                    mm = pe.matmul(pA[:, 512 * n:512 * n + 512], sel[0:96].rearrange("p e s -> p (e s)"),
                                   bias_up[0:96, 512 * n:512 * n + 512], start=False, stop=True, skip_group_check=True)
                mm.then_inc(up_done, 1)
                pe.wait_ge(pick_ready, g + 2)
                gather(bank)
                b = bank(2)
                pe.wait_ge(gpick_ready, g + 1)
                for m, (t0, r) in enumerate(TOK):
                    mm = tr(b[:, t0:t0 + r], gpick[0:r, m].rearrange("p e s -> p (e s)"))
                mm.then_inc(misc_full, 1)
                for half in range(2):
                    b = bank(3 + half)
                    if half == 0:
                        pe.wait_ge(a_ready, g + 1)
                    for k in range(4):
                        f = 128 * (4 * half + k)
                        mm = tr(b[:, 128 * k:128 * k + 128], act_out[:, f:f + 128])
                    mm.then_inc(misc_full, 1)
                pe.wait_ge(misc_free, PAIR_FILLS * g + (misc0 + 5))
                for k in range(KT):
                    if k % 2 == 0:
                        w, in_ring = chunk(UP_CHUNKS + k // 2)
                    for n in range(2):
                        for e in range(2):
                            o = 2048 * e + 1024 * (k % 2) + 512 * n
                            mm = matmul(pB[64 * e:64 * e + 64, n, :], aT[:, k, 64 * e:64 * e + 64],
                                        w[:, o:o + 512], start=(k == 0), stop=False)
                    if k % 2 and in_ring:
                        mm.then_inc(ring_free, 1)
                for n in range(2):
                    mm = pe.matmul(pB[:, n, :], sel[0:96].rearrange("p e s -> p (e s)"),
                                   bias_down[0:96, 512 * n:512 * n + 512], start=False, stop=True, skip_group_check=True)
                mm.then_inc(down_done, 1)
                for k in range(6):
                    m, h = k // 2, k % 2
                    t0, r = TOK[m]
                    b = bank(5 + k)
                    if k < 2:
                        pe.wait_ge((y_ready, y_ready_dve)[k], g + 1)
                    matmul(b[0:r, :], gateT[:, t0:t0 + r], y_pair[:, 512 * h:512 * h + 512]).then_inc(misc_full, 1)

            pair(0, 0, first=True)
            with pe.Fori(1, PAIRS) as i:
                pair(i, i)
            pe.wait_ge(misc_free, FILL["route", 0])
            over = pe.value_load(flag[0:1, 0:1], min_val=0, max_val=1)
            with pe.If(over > 0):
                with pe.Fori(1, PASSES) as q:
                    with pe.Fori(0, PAIRS) as i:
                        pair(q * PAIRS + i, i)


_INS = ["x_prompt", "x_sample", "state_conv", "cache_k_win", "cache_v_win", "rel_bias", "attn_norm_w", "w_in",
        "conv_w", "q_norm_w", "k_norm_w", "sinks", "w_out", "ffn_norm_w", "w_router", "b_router", "w_up", "b_up",
        "w_down", "b_down"]
_BY_LAYER = set(_INS) - {"x_prompt", "x_sample", "rel_bias"}
_OUTS = [(1, SEQ, D), (DEC, 1, D), (1, 1, 2, D), (1, 1, WIN, NKV, HD), (1, 1, WIN, NKV, HD),
         (1, DEC, 2, D), (1, DEC, WIN, NKV, HD), (1, DEC, WIN, NKV, HD)]


def kernel(**inputs):
    import concourse.bacc as bacc
    from concourse.bass_utils import run_bass_kernel_spmd

    nc = bacc.Bacc("TRN2", target_bir_lowering=False, num_devices=1)
    arrays, args = {}, []
    for name in _INS:
        a = np.ascontiguousarray(inputs[name])
        arrays["in_" + name] = a
        ap = nc.dram_tensor("in_" + name, a.shape, F32, kind="ExternalInput").ap()
        args.append(ap[0] if name in _BY_LAYER else ap)
    arrays["in_consts"] = constants()
    args.append(nc.dram_tensor("in_consts", (128, C_N), F32, kind="ExternalInput").ap())
    for n, shape in enumerate(_OUTS):
        args.append(nc.dram_tensor(f"out_{n}", shape, F32, kind="ExternalOutput").ap())
    build(nc, *args)
    r = run_bass_kernel_spmd(nc, [arrays], core_ids=[0])
    return tuple(r.results[0][f"out_{n}"] for n in range(len(_OUTS)))
```

```python
from contextlib import ExitStack

import numpy as np

import concourse.bass as bass
from concourse import mybir
from concourse.alu_op_type import AluOpType as ALU

F32 = mybir.dt.float32
BF16 = mybir.dt.bfloat16
I32 = mybir.dt.int32
ACT = mybir.ActivationFunctionType
AX = mybir.AxisListType

D = 1024
SEQ, DEC = 256, 8
NT = SEQ + DEC
KT = D // 128
HD, NKV, GROUP = 64, 2, 8
NH = NKV * GROUP
WIN = 128
NBUCKET, MAXDIST = 32, 128
NE, TOPK = 32, 4
FF = 1024
EPS = 1e-5
NEG = -1e30
ALPHA, LIMIT = 1.702, 7.0

TOK = [(0, 128), (128, 128), (256, DEC)]
CAP = 64
PASSES = -(-NT // CAP)
PAIRS = NE // 2

SLOTS = 6
SLOT = 4096
W_IN_CHUNKS, W_OUT_CHUNKS = 13, 2
FIRST_CHUNKS = W_IN_CHUNKS + W_OUT_CHUNKS
UP_CHUNKS, DOWN_CHUNKS = KT, KT // 2
PAIR_CHUNKS = UP_CHUNKS + DOWN_CHUNKS
EXTRA = {4: 0, 5: 1, 8: 2}
FIRST_PAIR = {}
for _j in range(PAIR_CHUNKS):
    if _j not in EXTRA:
        FIRST_PAIR[_j] = FIRST_CHUNKS + len(FIRST_PAIR)
LOOP_CHUNK = FIRST_CHUNKS - len(EXTRA)

XIN, BG, CG, QC, KC_, VC_, GC, GA = 0, 1024, 2048, 3072, 4096, 4224, 4352, 5376

C_ID, C_BLK, C_TRI, C_ONE, C_IOTA, C_BUCKET, C_SEL, C_N = 0, 128, 256, 384, 512, 577, 705, 737

V_ANORM, V_FNORM, V_CONV, V_QN, V_KN, V_N = 0, 8, 16, 40, 41, 42


def constants():
    c = np.zeros((128, C_N), np.float32)
    p = np.arange(128)
    c[:, C_ID:C_ID + 128] = np.eye(128)
    c[:, C_BLK:C_BLK + 128] = (p[:, None] // HD) == (p[None, :] // HD)
    c[:, C_TRI:C_TRI + 128] = p[:, None] < p[None, :]
    c[:, C_ONE:C_ONE + 128] = 1.0
    c[:, C_IOTA:C_IOTA + CAP + 1] = np.arange(CAP + 1)
    rel = 127 - np.arange(128)
    exact = NBUCKET // 2
    far = exact + (np.log(np.maximum(rel, 1).astype(np.float32) / np.float32(exact))
                   / np.float32(np.log(MAXDIST / exact)) * np.float32(NBUCKET - exact)).astype(np.int32)
    bucket = np.where(rel < exact, rel, np.minimum(far, NBUCKET - 1))
    c[0:NBUCKET, C_BUCKET:C_BUCKET + 128] = bucket[None, :] == np.arange(NBUCKET)[:, None]
    c[0:96, C_SEL:C_SEL + NE] = (p[0:96, None] % NE) == np.arange(NE)[None, :]
    return c


def tile_list():
    tiles = [("k", 0, 0, 0), ("v", 0, 1, 0)]
    groups = [("q", 0), ("q", 1), ("cg", 0), ("xin", 0), ("bg", 0), ("gc", 0),
              ("cg", 1), ("xin", 1), ("bg", 1), ("gc", 1), ("ga", 0), ("ga", 1)]
    for c, (kind, half) in enumerate(groups):
        tiles += [(kind, c + 1, j, 4 * half + j) for j in range(4)]
    return tiles


TILES = tile_list()
CHUNK_COL = {"q": QC, "cg": CG, "xin": XIN, "bg": BG, "gc": GC, "ga": GA}
UNITS = [(0, 0), (1, 0), (0, 4), (1, 4)]


SPLITS = 6


def plan():
    after = {n: [] for n in range(len(TILES))}
    for j in range(9):
        n = 0 if j == 0 else j + 1
        after[n].append(("square_in", j))
        after[n + 1].append(("square", j))
        after[n + 2].append(("qknorm", j))
    after[3].append(("v_rows", 0))
    after[4].append(("k_rows", 0))
    after[5].append(("state_cols", 0))
    after[8].append(("cache_cols", 0))
    after[9].append(("cache_cols", 1))
    for u in range(len(UNITS)):
        n = 13 + 7 * u
        for d, what in ((0, "scores"), (1, "bias"), (2, "exp"), (3, "norm"), (5, "turn"), (6, "values")):
            after[n + d].append((what, u))
    for n, what, part in ((14, "s_scores", 0), (15, "s_scores", 1), (16, "s_bias", 0), (18, "s_norm", 0),
                          (21, "s_turn", 0), (24, "s_values", 0), (31, "s_values", 1)):
        after[n].append((what, part))
    after[34].append(("conv_rows", 0))
    after[36].append(("conv_rows", 1))
    for n in range(SPLITS):
        after[42 + n].append(("split", n))
    steps = [("vectors", 0), ("bias_table", 0)] + [("h_cols", n) for n in (1, 2, 3, 4, 0)]
    for n in range(len(TILES)):
        steps.append(("tile", n))
        steps += after[n]
    return steps


STEPS = plan()

COLS_FIRST = next(a for what, a in STEPS if what == "h_cols")
COLS = [(2, 0, 8), (0, 0, 4), (0, 4, 4), (1, 0, 4), (1, 4, 4)]
BRANCH = [("out", (2, 0)), ("out", (0, 0)), ("x_cols", 0), ("rms", 2), ("out", (1, 0)), ("x_cols", 1),
          ("logits", 2), ("out", (0, 1)), ("x_cols", 3), ("rms", 0), ("out", (1, 1)), ("x_cols", 2),
          ("x_cols", 4), ("rms", 1), ("logits", 0), ("logits", 1)]

FILLS_OF = {"tile": 0, "square_in": 0, "split": 0, "qknorm": 0, "scores": 0, "bias": 0, "exp": 0, "norm": 0, "turn": 0, "s_norm": 0, "out": 0, "rms": 0}
FILL, _n = {}, 0
for _s in STEPS + BRANCH + [("route", 0), ("gather", 0), ("gather", 1)]:
    _n += FILLS_OF.get(_s[0], 1)
    FILL[_s] = _n
PRE_FILLS = _n
PAIR_FILLS = 9
OUTPUTS = [(0, 0), (1, 0), (0, 1), (1, 1), (2, 0), (2, 1)]

BY_ACT = ("cg", "gc", "ga")
ACT_TILES = [sum(t[0] in BY_ACT for t in TILES[:n]) for n in range(len(TILES) + 1)]
DVE_TILES = [sum(t[0] not in BY_ACT for t in TILES[:n]) for n in range(len(TILES) + 1)]
XIN_END = [18, 34]
VECS = 6


class Count:

    def __init__(self, sem, base=0):
        self.sem, self.n = sem, base

    def next(self):
        self.n = self.n + 1
        return self.n


def build(nc, x_prompt, x_sample, state_conv, cache_k, cache_v, rel_bias, attn_norm_w, w_in, conv_w, q_norm_w,
          k_norm_w, sinks, w_out, ffn_norm_w, w_router, b_router, w_up, b_up, w_down, b_down, consts,
          y_prompt, y_sample, conv_prompt, k_prompt, v_prompt, conv_sample, k_sample, v_sample):
    with ExitStack() as ctx:
        def sb(name, shape, dt=F32):
            return ctx.enter_context(nc.sbuf_tensor(name, shape, dt))

        def sem(name):
            return ctx.enter_context(nc.semaphore(name))

        ring = sb("ring", [128, SLOTS, SLOT])
        x = sb("x", [128, 3, D])
        hn = sb("hn", [128, 3, D])
        cst = sb("cst", [128, C_N])
        rows = sb("rows", [128, 128])
        cols = sb("cols", [128, V_N])
        rb = sb("rb", [NBUCKET, NH])
        brouter = sb("brouter", [128, NE])
        sink = sb("sink", [128, NKV, GROUP])
        ssink = sb("ssink", [128, 1])
        conv_row = sb("conv_row", [128, D])
        state_c = sb("state_c", [128, KT, DEC, 2])
        v_row = sb("v_row", [128, 3, 128])
        k_row = sb("k_row", [128, 2, 128])
        tmp = sb("tmp", [128, 2, NT])
        rt = sb("rt", [128, NT])
        stat = sb("stat", [128, 64])
        flag = sb("flag", [1, 4], I32)

        AREA = 8 * NT * 4 + KT * (NT + 2) + 2 * NT + 3 * 2048
        area = sb("area", [128, AREA])

        class Area:
            def __init__(self, at):
                self.at = at

            def take(self, n):
                self.at += n
                assert self.at <= AREA
                return area[:, self.at - n:self.at]

        one = Area(0)
        hT = one.take(KT * NT).rearrange("p (k n) -> p k n", k=KT)
        yc = one.take(KT * NT).rearrange("p (k n) -> p k n", k=KT)
        ya = one.take(KT * NT).rearrange("p (k n) -> p k n", k=KT)
        cx = one.take(KT * (NT + 2)).rearrange("p (k n) -> p k n", k=KT)
        kT = one.take(NT)
        vT = one.take(NT)
        qT = one.take(KT * NT).rearrange("p (k n) -> p k n", k=KT)
        table = one.take(2048).rearrange("p (h s) -> p h s", h=8)
        prob = one.take(2048).rearrange("p (h s) -> p h s", h=8)
        probT = one.take(2048).rearrange("p (b h q) -> p b h q", b=2, h=8)
        hn_flat = hn[:].rearrange("p m d -> p (m d)")
        k_cache = hn_flat[:, 0:1024].rearrange("p (b f) -> p b f", b=DEC)
        v_cache = hn_flat[:, 1024:2048].rearrange("p (b f) -> p b f", b=DEC)
        k_cacheT = hn_flat[:, 2048:3072].rearrange("p (b s) -> p b s", b=DEC)
        stab = sb("stab", [128, WIN])
        sprob = sb("sprob", [128, WIN])
        sprobT = sb("sprobT", [128, 128])

        two = Area(2 * KT * NT)
        xsT = two.take(1024).rearrange("p (k s) -> p k s", k=KT)
        extra0 = area[:, two.at:two.at + SLOT]
        act_out = two.take(FF)
        aT = two.take(1024).rearrange("p (k s) -> p k s", k=KT)
        y_pair = two.take(D)
        glu = two.take(FF)
        pick = two.take(3 * 128).rearrange("p (m e s) -> p m e s", m=3, e=2)
        gateT = two.take(NT)
        gpick = two.take(3 * 128).rearrange("p (m e s) -> p m e s", m=3, e=2)
        bias_down = two.take(D // 2).bitcast(BF16)
        assert two.at <= 3 * KT * NT + KT * (NT + 2) + 2 * NT + KT * NT
        two.at = 3 * KT * NT + KT * (NT + 2) + 2 * NT + KT * NT
        extra1 = area[:, two.at:two.at + SLOT]
        raw_up = two.take(2 * FF)
        lin = two.take(FF)
        raw_down = lin
        sig = two.take(FF)
        NPOS = PASSES * NE + 2
        pos = two.take(3 * NPOS).rearrange("p (m e) -> p m e", m=3)
        sel = two.take(64).bitcast(BF16).rearrange("p (e s) -> p e s", e=2)
        bias_up = two.take(FF).bitcast(BF16)
        extra = [extra0, extra1, area[:, 0:SLOT]]

        lg = sb("lg", [128, 3, NE])
        mask = sb("mask", [128, 3, NE], BF16)
        count_w = sb("count_w", [128, 2, 128], BF16)
        t32 = sb("t32", [128, 3, NE])
        gate = sb("gate", [128, 3, NE])
        rank = sb("rank", [128, NE])
        top8 = sb("top8", [128, 3, 8])
        flag_f32 = sb("flag_f32", [1, 1])
        zeros = table.rearrange("p h s -> p (h s)")[:, 0:256].bitcast(BF16)
        rev_sb = prob.rearrange("p h s -> p (h s)")[0:NH, 0:3 * WIN]

        ident = cst[:, C_ID:C_ID + 128]

        pA = ctx.enter_context(nc.psum_tensor("pA", [128, 2048], F32))
        pB = ctx.enter_context(nc.psum_tensor("pB", [128, 2, 512], F32))
        pM = ctx.enter_context(nc.psum_tensor("pM", [128, 2, 512], F32))

        rev_dram = nc.dram_tensor("rev_scratch", (128, NH * 3 * WIN), F32, kind="Internal")

        x_loaded = [sem(f"x_loaded{m}") for m in range(3)]
        consts_loaded = sem("consts_loaded")
        vecs_loaded = sem("vecs_loaded")
        sink_loaded = sem("sink_loaded")
        ring_full = [sem(f"ring_full{s}") for s in range(SLOTS)]
        ring_free = sem("ring_free")
        extra_full = [sem(f"extra_full{n}") for n in range(len(EXTRA))]
        dve_step = sem("dve_step")
        bias_cast = sem("bias_cast")
        bias_left = sem("bias_left")
        misc_full = sem("misc_full")
        misc_free = sem("misc_free")
        tile_full = sem("tile_full")
        tile_free_dve = sem("tile_free_dve")
        tile_free_act = sem("tile_free_act")
        warm_ready = sem("warm_ready")
        cleared = sem("cleared")
        norm_sq = sem("norm_sq")
        norm_in = sem("norm_in")
        norm_rt = sem("norm_rt")
        h_ready = sem("h_ready")
        x_added = sem("x_added")
        rms_ready = sem("rms_ready")
        hn_ready = sem("hn_ready")
        ssink_loaded = sem("ssink_loaded")
        sq_ready = sem("sq_ready")
        qk_normed = sem("qk_normed")
        rt_out = sem("rt_out")
        rev_stored = sem("rev_stored")
        table_loaded = sem("table_loaded")
        stab_loaded = sem("stab_loaded")
        cache_loaded = sem("cache_loaded")
        vnew_loaded = sem("vnew_loaded")
        state_loaded = sem("state_loaded")
        scores_full = sem("scores_full")
        prob_biased = sem("prob_biased")
        exp_done = sem("exp_done")
        prob_ready = sem("prob_ready")
        turned = sem("turned")
        probT_ready = sem("probT_ready")
        sexp_in = sem("sexp_in")
        sexp_done = sem("sexp_done")
        sprob_ready = sem("sprob_ready")
        cg_ready = sem("cg_ready")
        sig_gate = sem("sig_gate")
        sig_used = sem("sig_used")
        out_full = sem("out_full")
        wr_loaded = sem("wr_loaded")
        wr_ready = sem("wr_ready")
        mask_ready = sem("mask_ready")
        ex_in = sem("ex_in")
        ex_out = sem("ex_out")
        route_ready = sem("route_ready")
        bias_loaded = [sem("bias_up_loaded"), sem("bias_down_loaded")]
        pick_ready = sem("pick_ready")
        gpick_ready = sem("gpick_ready")
        sel_ready = sem("sel_ready")
        up_done = sem("up_done")
        glu_ready = sem("glu_ready")
        sig_ready = sem("sig_ready")
        a_ready = sem("a_ready")
        aT_full = sem("aT_full")
        aT_ready = sem("aT_ready")
        down_done = sem("down_done")
        y_ready = sem("y_ready")
        y_ready_dve = sem("y_ready_dve")
        stored = sem("stored")
        final_stored = sem("final_stored")

        w_router_sb = sb("w_router_sb", [128, KT, NE])
        block = ctx.enter_context(nc.Block())

        def w_in_chunk(c):
            w = w_in.rearrange("(k p) n -> p k n", p=128)
            if c == 0:
                return [(ring[:, 0, 0:2048].rearrange("p (k h n) -> p k h n", k=KT, h=2)[:, :, h],
                         w[:, :, KC_ + 128 * h:KC_ + 128 * h + 128]) for h in range(2)]
            kind, _, _, t = TILES[2 + 4 * (c - 1)]
            if kind == "q":
                col = QC + t * HD
                dst = ring[:, c % SLOTS, :].rearrange("p (k h n) -> p k h n", k=KT, h=2)
                return [(dst[:, :, h], w[:, :, col + 512 * h:col + 512 * h + 256]) for h in range(2)]
            col = CHUNK_COL[kind] + t * 128
            dst = ring[:, c % SLOTS, :].rearrange("p (k n) -> p k n", k=KT)
            return [(dst[:, k:k + 4], w[:, k:k + 4, col:col + 512]) for k in (0, 4)]

        def filled(c):
            return 32 * (c // SLOTS + 1)

        @block.sync
        def _(sp):
            for m in range(2):
                sp.dma_start(x[:, m, :], x_prompt[0, 128 * m:128 * m + 128, :]).then_inc(x_loaded[m], 16)
            sp.dma_start(x[0:DEC, 2, :], x_sample.rearrange("b t d -> (b t) d")).then_inc(x_loaded[2], 16)
            for row, src in ((V_QN, q_norm_w), (V_KN, k_norm_w)):
                sp.dma_start(rows[row:row + 1, :].rearrange("a (h d) -> a h d", h=2),
                             bass.AP(src.tensor, src.offset, [[0, 1], [0, 2], [1, HD]])).then_inc(vecs_loaded, 16)
            sp.dma_start(rb[:], rel_bias).then_inc(vecs_loaded, 16)
            for c in range(FIRST_CHUNKS):
                if c == 1:
                    sp.wait_ge(consts_loaded, 16)
                    sp.wait_ge(vecs_loaded, 16 * VECS)
                if c >= SLOTS:
                    sp.wait_ge(ring_free, c - SLOTS + 1)
                if c < W_IN_CHUNKS:
                    parts = w_in_chunk(c)
                else:
                    n = c - W_IN_CHUNKS
                    wo = w_out[:, 512 * n:512 * n + 512].rearrange("(t p) n -> p t n", p=128)
                    dst = ring[:, c % SLOTS, :].rearrange("p (t n) -> p t n", t=KT)
                    parts = [(dst[:, t:t + 4], wo[:, t:t + 4]) for t in (0, 4)]
                for dst, src in parts:
                    sp.dma_start(dst, src).then_inc(ring_full[c % SLOTS], 16)

            up = w_up.rearrange("(i e) (k p) n -> e k i p n", e=2, p=128)
            down = w_down.rearrange("(i e) (k t p) n -> e k i p t n", e=2, t=2, p=128)

            def load(dst, full, j, i):
                for e in range(2):
                    d = dst[:, e * 2048:(e + 1) * 2048]
                    if j < UP_CHUNKS:
                        src = up[e, j, bass.ds(i, 1)].rearrange("a p n -> (a p) n")
                    else:
                        d = d.rearrange("p (t n) -> p t n", t=2)
                        src = down[e, j - UP_CHUNKS, bass.ds(i, 1)].rearrange("a p t n -> (a p) t n")
                    sp.dma_start(d, src).then_inc(full, 16)

            def pair(g, i):
                for j in range(PAIR_CHUNKS):
                    c = LOOP_CHUNK + j
                    sp.wait_ge(ring_free, PAIR_CHUNKS * g + (c - SLOTS + 1))
                    load(ring[:, c % SLOTS, :], ring_full[c % SLOTS], j, i)

            for j in range(PAIR_CHUNKS):
                if j in EXTRA:
                    if EXTRA[j] == 0:
                        sp.wait_ge(sig_used, 2 * KT)
                        sp.wait_ge(misc_free, FILL["values", 3])
                    elif EXTRA[j] == 1:
                        sp.wait_ge(bias_cast, SPLITS)
                    else:
                        sp.wait_ge(misc_free, FILL["logits", 1])
                    load(extra[EXTRA[j]], extra_full[EXTRA[j]], j, 0)
                else:
                    c = FIRST_PAIR[j]
                    sp.wait_ge(ring_free, c - SLOTS + 1)
                    load(ring[:, c % SLOTS, :], ring_full[c % SLOTS], j, 0)
            with sp.Fori(1, PAIRS) as i:
                pair(i, i)

            def store(fills):
                for m in range(2):
                    sp.wait_ge(misc_free, fills - len(OUTPUTS) + OUTPUTS.index((m, 1)) + 1)
                    sp.dma_start(y_prompt[0, 128 * m:128 * m + 128, :], x[:, m, :]).then_inc(final_stored, 16)
                sp.wait_ge(misc_free, fills)
                sp.dma_start(y_sample.rearrange("b t d -> (b t) d"), x[0:DEC, 2, :]).then_inc(final_stored, 16)

            store(PRE_FILLS + PAIR_FILLS * PAIRS)
            over = sp.value_load(flag[0:1, 0:1], min_val=0, max_val=1)
            sp.wait_ge(final_stored, 48)
            with sp.If(over > 0):
                with sp.Fori(1, PASSES) as q:
                    with sp.Fori(0, PAIRS) as i:
                        pair(q * PAIRS + i, i)
                store(PRE_FILLS + PAIR_FILLS * PAIRS * PASSES)
                sp.wait_ge(final_stored, 96)

        @block.gpsimd
        def _(pool):
            pool.dma_start(conv_row[0:2 * DEC, :],
                           state_conv.rearrange("b j d -> (b j) d")).then_inc(state_loaded, 16)
            pool.dma_start(w_router_sb[:], w_router.rearrange("(k p) e -> p k e", p=128)).then_inc(wr_loaded, 16)
            pool.dma_start(brouter[:], bass.AP(b_router.tensor, b_router.offset, [[0, 128], [1, NE]])).then_inc(wr_loaded, 16)
            pool.wait_ge(misc_free, FILL["bias_table", 0])
            pool.dma_start(rev_dram[:, :].rearrange("r (h m) -> h r m", h=NH),
                           rev_sb.unsqueeze(1).to_broadcast([NH, 128, 3 * WIN])).then_inc(rev_stored, 16)
            pool.wait_ge(misc_free, FILL["h_cols", 0])
            pool.dma_start(k_cache[0:WIN - 1], cache_k[:, 1:WIN].rearrange("b s h d -> s b (h d)")).then_inc(cache_loaded, 16)
            pool.dma_start(v_cache[0:WIN - 1], cache_v[:, 1:WIN].rearrange("b s h d -> s b (h d)")).then_inc(cache_loaded, 16)
            for kv in range(NKV):
                for b in range(DEC):
                    p = kv * 64 + b * 8
                    pool.dma_start(ssink[p:p + 8, :],
                                   sinks[kv * GROUP:(kv + 1) * GROUP].rearrange("(e a) -> e a", a=1)).then_inc(ssink_loaded, 16)
            pool.wait_ge(rev_stored, 16)

            def load_table(t0):
                for kv in range(NKV):
                    h0 = kv * GROUP + t0
                    src = bass.AP(rev_dram, h0 * 3 * WIN + WIN - 1, [[NH * 3 * WIN - 1, 128], [3 * WIN, 4], [1, 2 * WIN]])
                    pool.dma_start(table[:, 4 * kv:4 * kv + 4, :], src).then_inc(table_loaded, 16)

            load_table(0)
            for kv in range(NKV):
                for b in range(DEC):
                    p = kv * 64 + b * 8
                    pool.dma_start(stab[p:p + 8, :],
                                   rev_dram[0:1, :].rearrange("r (h m) -> (r h) m", h=NH)[
                                       kv * GROUP:(kv + 1) * GROUP, WIN:2 * WIN]).then_inc(stab_loaded, 16)
            pool.dma_start(conv_sample[0, :, 0, :], state_conv[:, 1, :]).then_inc(stored, 16)
            pool.dma_start(k_sample[0, :, 0:WIN - 1].rearrange("b s h d -> b (s h d)"),
                           cache_k[:, 1:WIN].rearrange("b s h d -> b (s h d)")).then_inc(stored, 16)
            pool.dma_start(v_sample[0, :, 0:WIN - 1].rearrange("b s h d -> b (s h d)"),
                           cache_v[:, 1:WIN].rearrange("b s h d -> b (s h d)")).then_inc(stored, 16)
            pool.wait_ge(misc_free, FILL["v_rows", 0])
            pool.dma_start(v_cache[WIN - 1:WIN], v_row[0:DEC, 2, :]).then_inc(vnew_loaded, 16)
            pool.dma_start(v_prompt[0, 0].rearrange("s h d -> s (h d)"), v_row[:, 1, :]).then_inc(stored, 16)
            pool.dma_start(v_sample[0, :, WIN - 1].rearrange("b h d -> b (h d)"), v_row[0:DEC, 2, :]).then_inc(stored, 16)
            pool.wait_ge(misc_free, FILL["k_rows", 0])
            pool.dma_start(k_prompt[0, 0].rearrange("s h d -> s (h d)"), k_row[:, 0, :]).then_inc(stored, 16)
            pool.dma_start(k_sample[0, :, WIN - 1].rearrange("b h d -> b (h d)"), k_row[0:DEC, 1, :]).then_inc(stored, 16)
            pool.wait_ge(prob_biased, 2)
            load_table(4)
            pool.wait_ge(misc_free, FILL["conv_rows", 1])
            pool.dma_start(conv_prompt[0, 0], conv_row[0:2, :]).then_inc(stored, 16)
            pool.dma_start(conv_sample[0, :, 1, :], conv_row[2:2 + DEC, :]).then_inc(stored, 16)

            pool.wait_ge(misc_free, FILL["values", 3])
            for src, raw, loaded in ((b_up, raw_up, bias_loaded[0]), (b_down, raw_down, bias_loaded[1])):
                for j in range(3):
                    pool.dma_start(raw[32 * j:32 * j + 32], src).then_inc(loaded, 16)
            for n in range(SPLITS - 2):
                raw, parts = ((raw_up, bias_up), (raw_down, bias_down))[n % 2]
                pool.wait_ge(bias_cast, n + 1)
                for j in range(n // 2 + 1, 3):
                    rows_ = slice(32 * j, 32 * j + 32)
                    ins = pool.tensor_tensor(raw[rows_], raw[rows_], parts[rows_, :], ALU.subtract)
                ins.then_inc(bias_left, 1)
            pool.wait_ge(stored, 16 * 9)

        @block.scalar
        def _(act):
            act.dma_start(cst[:], consts).then_inc(consts_loaded, 16)
            act.dma_start(rows[V_ANORM:V_ANORM + KT, :], attn_norm_w.rearrange("(k p) -> k p", p=128)).then_inc(vecs_loaded, 16)
            act.dma_start(rows[V_FNORM:V_FNORM + KT, :], ffn_norm_w.rearrange("(k p) -> k p", p=128)).then_inc(vecs_loaded, 16)
            act.dma_start(rows[V_CONV:V_CONV + 3 * KT, :], conv_w.rearrange("j (k p) -> (j k) p", p=128)).then_inc(vecs_loaded, 16)
            act.wait_ge(cleared, 1)
            nc.scalar.activation(stat[:, 63:64], stat[:, 62:63], ACT.Sqrt)
            for m in range(3):
                r = TOK[m][1]
                act.wait_ge(x_loaded[m], 16)
                nc.scalar.activation(hn[0:r, m, :], x[0:r, m, :], ACT.Square,
                                     accum_out=stat[0:r, m:m + 1]).then_inc(norm_sq, 1)
                act.wait_ge(norm_in, m + 1)
                nc.scalar.activation(stat[:, 4 + m:5 + m], stat[:, 4 + m:5 + m], ACT.Sqrt).then_inc(norm_rt, 1)

            for kv in range(NKV):
                act.dma_start(sink[:, kv, :],
                              bass.AP(sinks.tensor, sinks.offset + kv * GROUP, [[0, 128], [1, GROUP]])).then_inc(sink_loaded, 16)

            sigs = 0
            for what, a in STEPS:
                if what == "square_in":
                    act.wait_ge(tile_free_dve, 1 if a == 0 else a + 2)
                    if a >= 2:
                        act.wait_ge(misc_free, FILL["square", a - 2])
                    src = kT if a == 0 else qT[:, a - 1, :]
                    nc.scalar.activation(tmp[:, a % 2, :], src, ACT.Square).then_inc(sq_ready, 1)
                elif what == "qknorm":
                    act.wait_ge(misc_free, FILL["square", a])
                    nc.scalar.activation(rt[:], rt[:], ACT.Sqrt).then_inc(rt_out, 1)
                elif what == "tile":
                    kind, _, _, t = TILES[a]
                    if kind == "cg":
                        act.wait_ge(tile_full, a + 1)
                        nc.scalar.activation(cx[:, t, 2:], pB[:, a % 2, 0:NT], ACT.Copy).then_inc(tile_free_act, 1)
                    elif kind in ("gc", "ga"):
                        act.wait_ge(tile_full, a + 1)
                        if sigs >= 2:
                            act.wait_ge(sig_used, sigs - 1)
                        else:
                            act.wait_ge(misc_free, FILL["square", 8])
                        nc.scalar.activation(tmp[:, sigs % 2, :], pB[:, a % 2, 0:NT],
                                             ACT.Sigmoid).then_inc(tile_free_act, 1)
                        sigs += 1
                elif what == "exp":
                    keys = WIN * (UNITS[a][0] + 1)
                    act.wait_ge(prob_biased, a + 1)
                    for h in range(8):
                        nc.scalar.activation(prob[:, h, 0:keys], prob[:, h, 0:keys], ACT.Exp,
                                             bias=stat[:, 16 + h:17 + h], accum_out=stat[:, 24 + h:25 + h])
                    nc.scalar.activation(stat[:, 32:40], stat[:, 32:40], ACT.Exp).then_inc(exp_done, 1)
                elif what == "turn":
                    blocks = UNITS[a][0] + 1
                    act.wait_ge(turned, a + 1)
                    if a:
                        act.wait_ge(misc_free, FILL["values", a - 1])
                    for b in range(blocks):
                        ins = nc.scalar.activation(probT[:, b].rearrange("p h q -> p (h q)"),
                                                   pA[:, b * 1024:(b + 1) * 1024], ACT.Copy)
                    ins.then_inc(probT_ready, 1)
                elif what == "split":
                    raw, parts = ((raw_up, bias_up), (raw_down, bias_down))[a % 2]
                    if a < 2:
                        act.wait_ge(bias_loaded[a], 48)
                        nc.scalar.activation(parts[0:96, :], raw[0:96], ACT.Copy).then_inc(bias_cast, 1)
                        continue
                    act.wait_ge(bias_left, a - 1)
                    for j in range(a // 2, 3):
                        rows_ = slice(32 * j, 32 * j + 32)
                        ins = nc.scalar.activation(parts[rows_, :], raw[rows_], ACT.Copy)
                    ins.then_inc(bias_cast, 1)
                elif what == "s_bias":
                    act.wait_ge(sexp_in, 1)
                    nc.scalar.activation(sprob[:], sprob[:], ACT.Exp, bias=stat[:, 48:49], accum_out=stat[:, 49:50])
                    nc.scalar.activation(stat[:, 50:51], stat[:, 50:51], ACT.Exp).then_inc(sexp_done, 1)

            halves = norms = 0
            for what, a in BRANCH:
                if what == "out":
                    a, half = a
                    r = TOK[a][1]
                    for h in ((0, 1) if a == 2 else (half,)):
                        halves += 1
                        act.wait_ge(x_added, halves)
                        f = slice(512 * h, 512 * h + 512)
                        ins = nc.scalar.activation(hn[0:r, a, f], x[0:r, a, f], ACT.Square,
                                                   accum_out=stat[0:r, 2 * a + h:2 * a + h + 1])
                    if h == 1:
                        ins.then_inc(norm_sq, 1)
                elif what == "rms":
                    r = TOK[a][1]
                    norms += 1
                    act.wait_ge(norm_in, 3 + norms)
                    nc.scalar.activation(stat[0:r, 8 + a:9 + a], stat[0:r, 8 + a:9 + a], ACT.Sqrt).then_inc(norm_rt, 1)
                    act.wait_ge(rms_ready, norms)
                    nc.scalar.activation(hn[0:r, a, :], x[0:r, a, :], ACT.Copy,
                                         scale=stat[0:r, 12 + a:13 + a]).then_inc(hn_ready, 1)
            for n, a in enumerate((2, 0, 1)):
                r = TOK[a][1]
                act.wait_ge(ex_in, n + 1)
                nc.scalar.activation(gate[0:r, a, :], lg[0:r, a, :], ACT.Exp,
                                     bias=stat[0:r, 52 + a:53 + a]).then_inc(ex_out, 1)

            def pair(g, i):
                for h in range(2):
                    f = slice(512 * h, 512 * h + 512)
                    act.wait_ge(glu_ready, 2 * g + (h + 1))
                    nc.scalar.activation(sig[:, f], glu[:, f], ACT.Sigmoid, scale=ALPHA).then_inc(sig_ready, 1)
                for h in range(2):
                    act.wait_ge(aT_full, 2 * g + (h + 1))
                    nc.scalar.activation(aT[:, 4 * h:4 * h + 4, :].rearrange("p k s -> p (k s)"),
                                         pA[:, 1024 * h:1024 * h + 512], ACT.Copy).then_inc(aT_ready, 1)
                act.wait_ge(down_done, 2 * g + 1)
                nc.scalar.activation(y_pair[:, 0:512], pB[:, 0, :], ACT.Copy).then_inc(y_ready, 1)

            with act.Fori(0, PAIRS) as i:
                pair(i, i)
            act.wait_ge(misc_free, FILL["route", 0])
            over = act.value_load(flag[0:1, 0:1], min_val=0, max_val=1)
            with act.If(over > 0):
                with act.Fori(1, PASSES) as q:
                    with act.Fori(0, PAIRS) as i:
                        pair(q * PAIRS + i, i)

        @block.vector
        def _(dve):
            V = nc.vector
            step = Count(dve_step)

            def link(ins):
                ins.then_inc(dve_step, 1)
                dve.wait_ge(dve_step, step.next())

            misc = Count(misc_full)

            def misc_bank():
                n = misc.next()
                dve.wait_ge(misc_full, n)
                return pM[:, (n - 1) % 2, :]

            V.memset(zeros, 0.0).then_inc(warm_ready, 1)
            V.memset(stat[:], 0.0)
            V.memset(cx[:, :, 0:2], 0.0)
            for t in (lg, mask, t32, gate):
                V.memset(t[:], 0.0)
            link(V.memset(rev_sb, NEG))
            V.memset(flag_f32[:], 0.0).then_inc(cleared, 1)
            for m, (_, r) in enumerate(TOK):
                dve.wait_ge(norm_sq, m + 1)
                V.tensor_scalar(stat[:, 4 + m:5 + m], stat[:, m:m + 1], 1.0 / D, EPS,
                                ALU.mult, ALU.add).then_inc(norm_in, 1)
                dve.wait_ge(norm_rt, m + 1)
                link(V.reciprocal(stat[:, 8 + m:9 + m], stat[:, 4 + m:5 + m]))
                V.tensor_scalar(hn[0:r, m, :], x[0:r, m, :], stat[0:r, 8 + m:9 + m], None,
                                ALU.mult).then_inc(h_ready, 1)

            def columns(n, scale):
                m, k0, nk = COLS[n]
                t0, r = TOK[m]
                src = misc_bank()[:, 0:nk * r].rearrange("p (k n) -> p k n", k=nk)
                dst = hT[:, k0:k0 + nk, t0:t0 + r]
                if scale is None:
                    return V.tensor_copy(dst, src)
                return V.tensor_tensor(dst, src, cols[:, scale + k0:scale + k0 + nk].unsqueeze(2)
                                       .to_broadcast([128, nk, r]), ALU.mult)

            freed = 0
            for what, a in STEPS:
                if what == "vectors":
                    V.tensor_copy(cols[:], misc_bank()[:, 0:V_N]).then_inc(misc_free, 1)
                elif what == "bias_table":
                    b = misc_bank()
                    V.tensor_copy(rev_sb[:, WIN:2 * WIN], b[0:NH, 0:128]).then_inc(misc_free, 1)
                elif what == "h_cols":
                    if a == COLS_FIRST:
                        dve.wait_ge(misc_free, 1)
                    columns(a, V_ANORM).then_inc(misc_free, 1)
                elif what == "tile":
                    kind, _, _, t = TILES[a]
                    src = pB[:, a % 2, 0:NT]
                    if kind in ("k", "q", "v"):
                        dve.wait_ge(tile_full, a + 1)
                        dst = {"k": kT, "v": vT, "q": qT[:, t, :]}[kind]
                        V.tensor_copy(dst, src).then_inc(tile_free_dve, 1)
                    elif kind == "xin":
                        dve.wait_ge(tile_full, a + 1)
                        dve.wait_ge(tile_free_act, ACT_TILES[a])
                        V.tensor_tensor(cx[:, t, 2:], src, cx[:, t, 2:], ALU.mult).then_inc(tile_free_dve, 1)
                        dve.wait_ge(tile_free_dve, DVE_TILES[a] + 1)
                        w = [cols[:, V_CONV + 8 * j + t:V_CONV + 8 * j + t + 1] for j in range(3)]
                        taps = [cx[:, t, j:j + SEQ] for j in range(3)]
                        s_taps = [state_c[:, t, :, 0], state_c[:, t, :, 1], cx[:, t, 2 + SEQ:]]
                        V.tensor_scalar(yc[:, t, 0:SEQ], taps[0], w[0], None, ALU.mult)
                        link(V.tensor_scalar(yc[:, t, SEQ:], s_taps[0], w[0], None, ALU.mult))
                        for j in (1, 2):
                            V.scalar_tensor_tensor(out=yc[:, t, 0:SEQ], in0=taps[j], scalar=w[j],
                                                   in1=yc[:, t, 0:SEQ], op0=ALU.mult, op1=ALU.add)
                            link(V.scalar_tensor_tensor(out=yc[:, t, SEQ:], in0=s_taps[j], scalar=w[j],
                                                        in1=yc[:, t, SEQ:], op0=ALU.mult, op1=ALU.add))
                    elif kind == "bg":
                        dve.wait_ge(tile_full, a + 1)
                        V.tensor_tensor(yc[:, t, :], src, yc[:, t, :], ALU.mult).then_inc(tile_free_dve, 1)
                    elif kind == "gc":
                        dve.wait_ge(tile_free_act, ACT_TILES[a] + 1)
                        dve.wait_ge(tile_free_dve, DVE_TILES[a])
                        V.tensor_tensor(yc[:, t, :], tmp[:, freed % 2, :], yc[:, t, :], ALU.mult).then_inc(sig_used, 1)
                        freed += 1
                    elif kind == "ga":
                        dve.wait_ge(tile_free_act, ACT_TILES[a] + 1)
                        dve.wait_ge(sig_used, freed)
                        dve.wait_ge(misc_free, misc.n)
                        g = tmp[:, freed % 2, :]
                        link(V.tensor_tensor(g, g, ya[:, t, :], ALU.mult))
                        V.tensor_tensor(yc[:, t, :], g, yc[:, t, :], ALU.add).then_inc(sig_used, 1)
                        freed += 1
                elif what == "square":
                    b = misc_bank()
                    if a:
                        dve.wait_ge(qk_normed, a)
                    V.tensor_scalar(rt[:], b[:, 0:NT], 1.0 / HD, EPS, ALU.mult, ALU.add).then_inc(misc_free, 1)
                elif what == "qknorm":
                    dve.wait_ge(rt_out, a + 1)
                    link(V.reciprocal(rt[:], rt[:]))
                    dst, w = (kT, V_KN) if a == 0 else (qT[:, a - 1, :], V_QN)
                    V.scalar_tensor_tensor(out=dst, in0=dst, scalar=cols[:, w:w + 1], in1=rt[:],
                                           op0=ALU.mult, op1=ALU.mult).then_inc(qk_normed, 1)
                elif what == "v_rows":
                    b = misc_bank()
                    V.tensor_copy(v_row[0:DEC, 2, :], b[0:DEC, 256:384])
                    V.tensor_copy(v_row[:, 0:2, :].rearrange("p m f -> p (m f)"), b[:, 0:256]).then_inc(misc_free, 1)
                elif what == "k_rows":
                    b = misc_bank()
                    V.tensor_copy(k_row[0:DEC, 1, :], b[0:DEC, 128:256])
                    V.tensor_copy(k_row[:, 0, :], b[:, 0:128]).then_inc(misc_free, 1)
                elif what == "state_cols":
                    V.tensor_copy(state_c[:].rearrange("p k b j -> p (k b j)"),
                                  misc_bank()[:, 0:KT * 2 * DEC]).then_inc(misc_free, 1)
                elif what == "cache_cols":
                    b = misc_bank()
                    dve.wait_ge(qk_normed, 1)
                    V.tensor_copy(k_cacheT[:, 4 * a:4 * a + 4, 0:WIN - 1],
                                  b.rearrange("p (b s) -> p b s", b=4)[:, :, 0:WIN - 1])
                    V.tensor_copy(k_cacheT[:, 4 * a:4 * a + 4, WIN - 1],
                                  kT[:, SEQ + 4 * a:SEQ + 4 * a + 4]).then_inc(misc_free, 1)
                elif what == "bias":
                    q, t0 = UNITS[a]
                    keys = WIN * (q + 1)
                    dve.wait_ge(scores_full, a + 1)
                    dve.wait_ge(table_loaded, 32 * (a // 2 + 1))
                    if a:
                        dve.wait_ge(turned, a)
                    for kv in range(NKV):
                        ins = V.scalar_tensor_tensor(
                            out=prob[:, 4 * kv:4 * kv + 4, 0:keys],
                            in0=pA[:, 1024 * kv:1024 * kv + 4 * keys].rearrange("p (t s) -> p t s", t=4),
                            scalar=HD ** -0.5, in1=table[:, 4 * kv:4 * kv + 4, 2 * WIN - keys:],
                            op0=ALU.mult, op1=ALU.add)
                    link(ins)
                    link(V.tensor_reduce(stat[:, 16:24], prob[:, :, 0:keys], AX.X, ALU.max))
                    if a == 0:
                        dve.wait_ge(sink_loaded, 32)
                    s = sink[:, :, t0:t0 + 4]
                    m = stat[:, 16:24].rearrange("p (a b) -> p a b", a=2)
                    link(V.tensor_tensor(m, m, s, ALU.max))
                    link(V.tensor_scalar(stat[:, 16:24], stat[:, 16:24], -1.0, None, ALU.mult))
                    V.tensor_tensor(stat[:, 32:40].rearrange("p (a b) -> p a b", a=2), m, s,
                                    ALU.add).then_inc(prob_biased, 1)
                elif what == "norm":
                    keys = WIN * (UNITS[a][0] + 1)
                    dve.wait_ge(exp_done, a + 1)
                    link(V.tensor_tensor(stat[:, 24:32], stat[:, 24:32], stat[:, 32:40], ALU.add))
                    link(V.reciprocal(stat[:, 40:48], stat[:, 24:32]))
                    for h in range(8):
                        ins = V.tensor_scalar(prob[:, h, 0:keys], prob[:, h, 0:keys], stat[:, 40 + h:41 + h], None,
                                              ALU.mult)
                    ins.then_inc(prob_ready, 1)
                elif what == "values":
                    q, t0 = UNITS[a]
                    b = misc_bank()
                    dst = ya[:].rearrange("p (kv j) n -> p kv j n", kv=NKV)
                    V.tensor_copy(dst[:, :, t0 // 2:t0 // 2 + 2, 128 * q:128 * q + 128],
                                  b.rearrange("p (kv j n) -> p kv j n", kv=NKV, j=2)).then_inc(misc_free, 1)
                elif what == "s_scores":
                    V.tensor_copy(sprobT[:, 64 * a:64 * a + 64], misc_bank()[:, 0:64]).then_inc(misc_free, 1)
                elif what == "s_bias":
                    b = misc_bank()
                    dve.wait_ge(stab_loaded, 16 * 16)
                    V.scalar_tensor_tensor(out=sprob[:], in0=b[:, 0:128], scalar=HD ** -0.5, in1=stab[:],
                                           op0=ALU.mult, op1=ALU.add).then_inc(misc_free, 1)
                    dve.wait_ge(misc_free, misc.n)
                    link(V.tensor_reduce(stat[:, 48:49], sprob[:], AX.X, ALU.max))
                    dve.wait_ge(ssink_loaded, 16 * 2 * DEC)
                    link(V.tensor_tensor(stat[:, 48:49], stat[:, 48:49], ssink[:], ALU.max))
                    link(V.tensor_scalar(stat[:, 48:49], stat[:, 48:49], -1.0, None, ALU.mult))
                    V.tensor_tensor(stat[:, 50:51], stat[:, 48:49], ssink[:], ALU.add).then_inc(sexp_in, 1)
                elif what == "s_norm":
                    dve.wait_ge(sexp_done, 1)
                    link(V.tensor_tensor(stat[:, 49:50], stat[:, 49:50], stat[:, 50:51], ALU.add))
                    link(V.reciprocal(stat[:, 51:52], stat[:, 49:50]))
                    V.tensor_scalar(sprob[:], sprob[:], stat[:, 51:52], None, ALU.mult).then_inc(sprob_ready, 1)
                elif what == "s_turn":
                    V.tensor_copy(sprobT[:], misc_bank()[:, 0:128]).then_inc(misc_free, 1)
                elif what == "s_values":
                    b = misc_bank()
                    V.tensor_copy(ya[:, :, SEQ + 4 * a:SEQ + 4 * a + 4].rearrange("p t b -> p b t"),
                                  b[:, 0:32].rearrange("p (b t) -> p b t", b=4)).then_inc(misc_free, 1)
                elif what == "conv_rows":
                    b = misc_bank()
                    V.tensor_copy(conv_row[0:2 + DEC, 512 * a:512 * a + 512], b[0:2 + DEC, :]).then_inc(misc_free, 1)

            V.tensor_copy(count_w[:].rearrange("p a n -> p (a n)"), cst[:, C_TRI:C_TRI + 256])
            dve.wait_ge(wr_loaded, 32)
            for k in range(KT):
                ins = V.tensor_scalar(w_router_sb[:, k, :], w_router_sb[:, k, :],
                                      cols[:, V_FNORM + k:V_FNORM + k + 1], None, ALU.mult)
            ins.then_inc(wr_ready, 1)

            fulls = norms = 0
            for what, a in BRANCH:
                if what == "out":
                    a, half = a
                    r = TOK[a][1]
                    for h in ((0, 1) if a == 2 else (half,)):
                        xs = x[0:r, a, 512 * h:512 * h + 512]
                        if a < 2:
                            fulls += 1
                            dve.wait_ge(out_full, fulls)
                            o = 1024 * a + 512 * h
                            V.tensor_tensor(xs, pA[:, o:o + 512], xs, ALU.add).then_inc(x_added, 1)
                            continue
                        if h == 0:
                            fulls += 1
                            dve.wait_ge(out_full, fulls)
                        for j in range(4):
                            ins = V.tensor_tensor(xs, pB[32 * j:32 * j + DEC, h, :], xs, ALU.add)
                            if j < 3:
                                link(ins)
                        ins.then_inc(x_added, 1)
                elif what == "rms":
                    r = TOK[a][1]
                    norms += 1
                    dve.wait_ge(norm_sq, 3 + norms)
                    s1 = stat[0:r, 2 * a + 1:2 * a + 2]
                    link(V.tensor_tensor(s1, s1, stat[0:r, 2 * a:2 * a + 1], ALU.add))
                    V.tensor_scalar(stat[0:r, 8 + a:9 + a], s1, 1.0 / D, EPS, ALU.mult, ALU.add).then_inc(norm_in, 1)
                    dve.wait_ge(norm_rt, 3 + norms)
                    V.reciprocal(stat[0:r, 12 + a:13 + a], stat[0:r, 8 + a:9 + a]).then_inc(rms_ready, 1)
                elif what == "x_cols":
                    columns(a, None).then_inc(misc_free, 1)
                elif what == "logits":
                    r = TOK[a][1]
                    rows_ = slice(0, r)
                    l, e, c, g = lg[rows_, a, :], t32[rows_, a, :], mask[rows_, a, :], gate[rows_, a, :]
                    b = misc_bank()
                    dve.wait_ge(rms_ready, norms)
                    V.scalar_tensor_tensor(out=l, in0=b[rows_, 0:NE], scalar=stat[rows_, 12 + a:13 + a],
                                           in1=brouter[rows_, :], op0=ALU.mult, op1=ALU.add).then_inc(misc_free, 1)
                    dve.wait_ge(misc_free, misc.n)
                    link(V.max(top8[rows_, a, :], l))
                    least = top8[rows_, a, TOPK - 1:TOPK]
                    V.tensor_scalar(c, l, least, None, ALU.is_gt, ALU.add, accum_out=stat[rows_, 56 + a:57 + a])
                    link(V.tensor_scalar(e, l, least, None, ALU.is_equal))
                    V.tensor_scalar(stat[rows_, 56 + a:57 + a], stat[rows_, 56 + a:57 + a], -1.0, float(TOPK),
                                    ALU.mult, ALU.add)
                    link(V.tensor_tensor_scan(rank[rows_, :], cst[rows_, C_ONE:C_ONE + NE], e, 0.0,
                                              ALU.mult, ALU.add))
                    link(V.scalar_tensor_tensor(out=e, in0=rank[rows_, :], scalar=stat[rows_, 56 + a:57 + a],
                                                in1=e, op0=ALU.is_le, op1=ALU.mult))
                    V.tensor_tensor(c, c, e, ALU.add).then_inc(mask_ready, 1)
                    V.tensor_scalar(stat[rows_, 52 + a:53 + a], top8[rows_, a, 0:1], -1.0, None,
                                    ALU.mult).then_inc(ex_in, 1)

            b = misc_bank()
            V.scalar_tensor_tensor(out=t32[:, 0:2, :].rearrange("p m e -> p (m e)"), in0=b[:, 0:2 * NE], scalar=1.0,
                                   in1=mask[:, 0:2, :].rearrange("p m e -> p (m e)"), op0=ALU.add, op1=ALU.mult)
            link(V.scalar_tensor_tensor(out=t32[0:DEC, 2, :], in0=b[0:DEC, 2 * NE:3 * NE], scalar=1.0,
                                        in1=mask[0:DEC, 2, :], op0=ALU.add, op1=ALU.mult))
            def picks(place, first):
                iota = cst[:, C_IOTA + first:C_IOTA + first + CAP].unsqueeze(1).unsqueeze(1)
                return V.tensor_tensor(pick, iota.to_broadcast([128, 3, 2, CAP]),
                                       place.unsqueeze(3).to_broadcast([128, 3, 2, CAP]), ALU.is_equal)

            picks(t32[:, :, 0:2], 1).then_inc(pick_ready, 1)
            V.memset(pos[:, :, PASSES * NE:], -1.0)
            V.tensor_scalar(pos[:, :, 0:NE], t32[:], -1.0, None, ALU.add)
            for n, a in enumerate((2, 0, 1)):
                rows_ = slice(0, TOK[a][1])
                g = gate[rows_, a, :]
                dve.wait_ge(ex_out, n + 1)
                dve.wait_ge(mask_ready, n + 1)
                link(V.scalar_tensor_tensor(out=g, in0=g, scalar=1.0, in1=mask[rows_, a, :], op0=ALU.mult,
                                            op1=ALU.mult, accum_out=stat[rows_, 60:61]))
                link(V.reciprocal(stat[rows_, 61:62], stat[rows_, 60:61]))
                link(V.tensor_scalar(g, g, stat[rows_, 61:62], None, ALU.mult))
            for q in range(1, PASSES):
                V.tensor_scalar(pos[:, :, q * NE:(q + 1) * NE], t32[:], -1.0 - CAP * q, None, ALU.add)
            link(V.tensor_reduce(stat[:, 60:61], b[:, 3 * NE:4 * NE], AX.X, ALU.max))
            link(V.tensor_scalar(flag_f32[:], stat[0:1, 60:61], float(CAP), None, ALU.is_gt))
            V.tensor_copy(flag[0:1, 0:1], flag_f32[:]).then_inc(misc_free, 1)
            fw = cols[:, V_FNORM:V_FNORM + KT].unsqueeze(2).to_broadcast([128, KT, 128])

            def gathered(half, b):
                return V.tensor_tensor(xsT[:, 4 * half:4 * half + 4, :], b.rearrange("p (k s) -> p k s", k=4),
                                       fw[:, 4 * half:4 * half + 4, :], ALU.mult)

            for half in range(2):
                gathered(half, misc_bank()).then_inc(misc_free, 1)
            misc0 = misc.n
            assert misc0 == PRE_FILLS, misc0
            step0 = step.n
            LINKS = 4

            def pair(g, i):
                n = 0
                base = step0 + LINKS * g

                def link(ins):
                    nonlocal n
                    n += 1
                    ins.then_inc(dve_step, 1)
                    dve.wait_ge(dve_step, base + n)

                def bank(k):
                    dve.wait_ge(misc_full, PAIR_FILLS * g + (misc0 + k + 1))
                    return pM[:, (misc0 + k) % 2, :]

                V.tensor_copy(sel[0:96], cst[0:96, C_SEL:C_SEL + NE][:, bass.ds(i * 2, 2)].unsqueeze(2)
                              .to_broadcast([96, 2, CAP])).then_inc(sel_ready, 1)
                dve.wait_ge(pick_ready, g + 1)
                V.tensor_tensor(gpick, pick, gate[:, :, bass.ds(i * 2, 2)].unsqueeze(3)
                                .to_broadcast([128, 3, 2, CAP]), ALU.mult).then_inc(gpick_ready, 1)
                dve.wait_ge(gpick_ready, g + 1)
                picks(pos[:, :, bass.ds((g + 1) * 2, 2)], 0).then_inc(pick_ready, 1)
                u = pA[:].rearrange("p (f two) -> p two f", two=2)
                for h in range(2):
                    f = slice(512 * h, 512 * h + 512)
                    dve.wait_ge(up_done, 2 * g + (h + 1))
                    V.tensor_scalar(glu[:, f], u[:, 0, f], LIMIT, None, ALU.min).then_inc(glu_ready, 1)
                    link(V.tensor_scalar(lin[:, f], u[:, 1, f], -LIMIT, LIMIT, ALU.max, ALU.min))
                    dve.wait_ge(glu_ready, 2 * g + (h + 1))
                    link(V.scalar_tensor_tensor(out=lin[:, f], in0=lin[:, f], scalar=1.0, in1=glu[:, f],
                                                op0=ALU.add, op1=ALU.mult))
                    dve.wait_ge(sig_ready, 2 * g + (h + 1))
                    V.tensor_tensor(act_out[:, f], lin[:, f], sig[:, f], ALU.mult).then_inc(a_ready, 1)
                for half in range(2):
                    gathered(half, bank(half)).then_inc(misc_free, 1)
                V.tensor_copy(gateT, bank(2)[:, 0:NT]).then_inc(misc_free, 1)
                dve.wait_ge(down_done, 2 * g + 2)
                V.tensor_copy(y_pair[:, 512:1024], pB[:, 1, :]).then_inc(y_ready_dve, 1)
                for k, (m, h) in enumerate(OUTPUTS):
                    r = TOK[m][1]
                    xs = x[0:r, m, 512 * h:512 * h + 512]
                    V.tensor_tensor(xs, bank(3 + k)[0:r], xs, ALU.add).then_inc(misc_free, 1)
                dve.wait_ge(misc_free, PAIR_FILLS * g + (misc0 + PAIR_FILLS))
                assert n == LINKS

            with dve.Fori(0, PAIRS) as i:
                pair(i, i)
            dve.wait_ge(misc_free, FILL["route", 0])
            over = dve.value_load(flag[0:1, 0:1], min_val=0, max_val=1)
            with dve.If(over > 0):
                dve.wait_ge(final_stored, 48)
                with dve.Fori(1, PASSES) as q:
                    with dve.Fori(0, PAIRS) as i:
                        pair(q * PAIRS + i, i)

        @block.tensor
        def _(pe):
            fills = Count(misc_full)

            def misc_bank():
                if fills.n >= 2:
                    pe.wait_ge(misc_free, fills.n - 1)
                return pM[:, (fills.next() - 1) % 2, :]

            def matmul(out, w, m, start=True, stop=True):
                return pe.matmul(out, w, m, start=start, stop=stop, skip_group_check=True)

            def tr(out, src):
                return pe.transpose(out, src, ident[0:src.shape[0], 0:src.shape[0]])

            def columns(n, src, b):
                m, k0, nk = COLS[n]
                r = TOK[m][1]
                mms = [tr(b[:, r * k:r * k + r], src[0:r, m, 128 * (k0 + k):128 * (k0 + k) + 128]) for k in range(nk)]
                mms[-1].then_inc(misc_full, 1)
                return mms[0]

            def keep_busy(w, m, n):
                for _ in range(n):
                    matmul(pB[:, 0, 0:m.shape[1]], w, m)

            pe.wait_ge(warm_ready, 1)
            keep_busy(zeros[:, 0:128], zeros, 15)
            pe.wait_ge(consts_loaded, 16)
            pe.wait_ge(vecs_loaded, 16 * VECS)
            for what, a in STEPS:
                if what == "vectors":
                    tr(misc_bank()[:, 0:V_N], rows[0:V_N, :]).then_inc(misc_full, 1)
                elif what == "bias_table":
                    matmul(misc_bank()[0:NH, 0:128], rb[:], cst[0:NBUCKET, C_BUCKET:C_BUCKET + 128]).then_inc(misc_full, 1)
                elif what == "h_cols":
                    if a == COLS_FIRST:
                        keep_busy(zeros[:, 0:128], zeros, 9)
                    b = misc_bank()
                    pe.wait_ge(h_ready, (3, 1, 1, 2, 2)[a])
                    columns(a, hn, b)
                elif what == "tile":
                    kind, c, j, t = TILES[a]
                    if j == 0:
                        pe.wait_ge(ring_full[c % SLOTS], filled(c))
                    if a == 0:
                        pe.wait_ge(misc_free, FILL["h_cols", 0])
                    if a >= 2:
                        if TILES[a - 2][0] in ("cg", "gc", "ga"):
                            pe.wait_ge(tile_free_act, ACT_TILES[a - 2] + 1)
                        else:
                            pe.wait_ge(tile_free_dve, DVE_TILES[a - 2] + 1)
                    for k in range(KT):
                        if c == 0:
                            w = ring[:, 0, 0:2048].rearrange("p (k n) -> p k n", k=KT)[:, k, 128 * j:128 * j + 128]
                            mm = matmul(pB[:, a % 2, 0:NT], w, hT[:, k, :], start=(k == 0), stop=(k == KT - 1))
                            continue
                        if kind != "q":
                            w = ring[:, c % SLOTS, :].rearrange("p (k n) -> p k n", k=KT)[:, k, 128 * j:128 * j + 128]
                            mm = matmul(pB[:, a % 2, 0:NT], w, hT[:, k, :], start=(k == 0), stop=(k == KT - 1))
                            if k == 0 and j == 0:
                                mm.then_inc(ring_free, 1)
                            continue
                        w = ring[:, c % SLOTS, :].rearrange("p (k h n) -> p k h n", k=KT, h=2)
                        for h in range(2):
                            mm = matmul(pB[HD * h:HD * h + HD, a % 2, 0:NT], w[:, k, h, HD * j:HD * j + HD],
                                        hT[:, k, :], start=(k == 0), stop=(k == KT - 1))
                            if k == 0 and j == 0 and h == 0:
                                mm.then_inc(ring_free, 1)
                    mm.then_inc(tile_full, 1)
                elif what == "square":
                    b = misc_bank()
                    pe.wait_ge(sq_ready, a + 1)
                    matmul(b[:, 0:NT], cst[:, C_BLK:C_BLK + 128], tmp[:, a % 2, :]).then_inc(misc_full, 1)
                elif what == "v_rows":
                    b = misc_bank()
                    pe.wait_ge(tile_free_dve, 2)
                    for m, (t0, r) in enumerate(TOK):
                        mm = tr(b[0:r, 128 * m:128 * m + 128], vT[:, t0:t0 + r])
                    mm.then_inc(misc_full, 1)
                elif what == "k_rows":
                    b = misc_bank()
                    pe.wait_ge(qk_normed, 1)
                    tr(b[:, 0:128], kT[:, 128:256])
                    tr(b[0:DEC, 128:256], kT[:, 256:NT]).then_inc(misc_full, 1)
                elif what == "state_cols":
                    b = misc_bank()
                    pe.wait_ge(state_loaded, 16)
                    for t in range(KT):
                        mm = tr(b[:, 16 * t:16 * t + 16], conv_row[0:2 * DEC, 128 * t:128 * t + 128])
                    mm.then_inc(misc_full, 1)
                elif what == "cache_cols":
                    b = misc_bank()
                    pe.wait_ge(cache_loaded, 32)
                    for n in range(4):
                        mm = tr(b[:, 128 * n:128 * n + 127], k_cache[0:WIN - 1, 4 * a + n, :])
                    mm.then_inc(misc_full, 1)
                elif what == "scores":
                    q, t0 = UNITS[a]
                    keys = WIN * (q + 1)
                    pe.wait_ge(qk_normed, 9)
                    if a:
                        pe.wait_ge(probT_ready, a)
                    for t in range(4):
                        for kv in range(NKV):
                            s = slice(HD * kv, HD * kv + HD)
                            o = 1024 * kv + t * keys
                            mm = matmul(pA[:, o:o + keys], qT[s, t0 + t, 128 * q:128 * q + 128],
                                        kT[s, 0:keys])
                    mm.then_inc(scores_full, 1)
                elif what == "turn":
                    q, t0 = UNITS[a]
                    pe.wait_ge(prob_ready, a + 1)
                    for b in range(q + 1):
                        for h in range(8):
                            o = (8 * b + h) * 128
                            mm = tr(pA[:, o:o + 128], prob[:, h, 128 * b:128 * b + 128])
                    mm.then_inc(turned, 1)
                elif what == "values":
                    q, t0 = UNITS[a]
                    o = misc_bank()
                    pe.wait_ge(probT_ready, a + 1)
                    for kv in range(NKV):
                        for b in range(q + 1):
                            for odd in range(2):
                                mm = matmul(o[HD * odd:HD * odd + HD, 256 * kv:256 * kv + 256],
                                            v_row[:, b, HD * kv:HD * kv + HD],
                                            probT[:, b, 4 * kv + odd:4 * kv + 4:2, :],
                                            start=(b == 0), stop=(b == q))
                    mm.then_inc(misc_full, 1)
                elif what == "s_scores":
                    b = misc_bank()
                    s = slice(HD * a, HD * a + HD)
                    for n in range(DEC):
                        mm = matmul(b[:, 8 * n:8 * n + 8], k_cacheT[s, n, :], qT[s, :, SEQ + n])
                    mm.then_inc(misc_full, 1)
                elif what == "s_bias":
                    b = misc_bank()
                    pe.wait_ge(misc_free, fills.n - 1)
                    tr(b[:, 0:128], sprobT[:]).then_inc(misc_full, 1)
                elif what == "s_turn":
                    b = misc_bank()
                    pe.wait_ge(sprob_ready, 1)
                    tr(b[:, 0:128], sprob[:]).then_inc(misc_full, 1)
                elif what == "s_values":
                    b = misc_bank()
                    pe.wait_ge(misc_free, fills.n - 1)
                    pe.wait_ge(vnew_loaded, 16)
                    pe.wait_ge(cache_loaded, 32)
                    for n in range(4 * a, 4 * a + 4):
                        for kv in range(NKV):
                            for odd in range(2):
                                o = 64 * kv + 8 * n
                                c = 8 * (n % 4) + 4 * kv
                                mm = matmul(b[HD * odd:HD * odd + HD, c:c + 4],
                                            v_cache[:, n, HD * kv:HD * kv + HD], sprobT[:, o + odd:o + 8:2])
                    mm.then_inc(misc_full, 1)
                elif what == "conv_rows":
                    b = misc_bank()
                    pe.wait_ge(tile_free_dve, DVE_TILES[XIN_END[a]])
                    for t in range(4):
                        mm = tr(b[0:2 + DEC, 128 * t:128 * t + 128], cx[:, 4 * a + t, SEQ:])
                    mm.then_inc(misc_full, 1)

            pe.wait_ge(probT_ready, len(UNITS))
            pe.wait_ge(tile_free_act, ACT_TILES[len(TILES)])
            norms = 0
            for what, a in BRANCH:
                if what == "out":
                    a, n = a
                    t0, r = TOK[a]
                    w = [ring[:, (W_IN_CHUNKS + h) % SLOTS, :].rearrange("p (k n) -> p k n", k=KT) for h in range(2)]
                    if a == 2:
                        for ch in (W_IN_CHUNKS, W_IN_CHUNKS + 1):
                            pe.wait_ge(ring_full[ch % SLOTS], filled(ch))
                        for k0 in (0, 4):
                            pe.wait_ge(sig_used, KT + k0 + 4)
                            for n in range(2):
                                for j in range(4):
                                    mm = matmul(pB[32 * j:32 * j + r, n, :], yc[:, k0 + j, t0:t0 + r],
                                                w[n][:, k0 + j], start=(k0 == 0), stop=(k0 == 4))
                                    if k0 == 0 and n == 0 and j == 0:
                                        mm.then_inc(ring_free, 1)
                        mm.then_inc(out_full, 1)
                        continue
                    for k in range(KT):
                        o = 1024 * a + 512 * n
                        mm = matmul(pA[:, o:o + 512], yc[:, k, t0:t0 + r], w[n][:, k], start=(k == 0), stop=(k == KT - 1))
                    mm.then_inc(out_full, 1)
                elif what == "x_cols":
                    b = misc_bank()
                    pe.wait_ge(x_added, (2, 3, 5, 4, 6)[a])
                    mm = columns(a, x, b)
                    if a in (1, 2):
                        mm.then_inc(ring_free, 1)
                elif what == "logits":
                    b = misc_bank()
                    t0, r = TOK[a]
                    pe.wait_ge(misc_free, FILL["x_cols", {2: 0, 0: 2, 1: 4}[a]])
                    pe.wait_ge(wr_ready, 1)
                    for k in range(KT):
                        mm = matmul(b[0:r, 0:NE], hT[:, k, t0:t0 + r], w_router_sb[:, k, :],
                                    start=(k == 0), stop=(k == KT - 1))
                    mm.then_inc(misc_full, 1)

            b = misc_bank()
            pe.wait_ge(wr_ready, 1)
            pe.wait_ge(mask_ready, 2)
            for m in range(4):
                out_rows = TOK[m][1] if m < 3 else 128
                if m == 1:
                    keep_busy(count_w[:, 0, :], count_w[:].rearrange("p a n -> p (a n)"), 12)
                    pe.wait_ge(mask_ready, 3)
                for s in range(min(m, 2) + 1):
                    rs = TOK[s][1]
                    mm = matmul(b[0:out_rows, NE * m:NE * m + NE], count_w[0:rs, int(s != m), 0:out_rows], mask[0:rs, s, :],
                                start=(s == 0), stop=(s == min(m, 2)))
            mm.then_inc(misc_full, 1)

            def gather(bank, half):
                b = bank(half)
                for k in range(4):
                    f = 128 * (4 * half + k)
                    for m, (_, r) in enumerate(TOK):
                        mm = matmul(b[:, 128 * k:128 * k + 128], hn[0:r, m, f:f + 128],
                                    pick[0:r, m].rearrange("p e s -> p (e s)"), start=(m == 0), stop=(m == 2))
                mm.then_inc(misc_full, 1)

            keep_busy(count_w[:, 0, :], count_w[:].rearrange("p a n -> p (a n)"), 12)
            pe.wait_ge(pick_ready, 1)
            pe.wait_ge(hn_ready, 3)
            for half in range(2):
                gather(lambda _: misc_bank(), half)
            misc0 = fills.n
            assert misc0 == PRE_FILLS, misc0
            pe.wait_ge(bias_cast, SPLITS)

            def pair(g, i, first=False):
                def bank(k):
                    pe.wait_ge(misc_free, PAIR_FILLS * g + (misc0 + k - 1))
                    return pM[:, (misc0 + k) % 2, :]

                def chunk(j):
                    if first and j in EXTRA:
                        pe.wait_ge(extra_full[EXTRA[j]], 32)
                        return extra[EXTRA[j]], False
                    if first:
                        c = FIRST_PAIR[j]
                        pe.wait_ge(ring_full[c % SLOTS], filled(c))
                    else:
                        c = LOOP_CHUNK + j
                        pe.wait_ge(ring_full[c % SLOTS], 64 * g + filled(c))
                    return ring[:, c % SLOTS, :], True

                for k in range(UP_CHUNKS):
                    if k % 4 == 0:
                        pe.wait_ge(misc_free, PAIR_FILLS * g + (misc0 - 1 + k // 4))
                    w, in_ring = chunk(k)
                    if k == UP_CHUNKS - 1:
                        pe.wait_ge(sel_ready, g + 1)
                    for n in range(4):
                        for e in range(2):
                            mm = matmul(pA[64 * e:64 * e + 64, 512 * n:512 * n + 512], xsT[:, k, 64 * e:64 * e + 64],
                                        w[:, 2048 * e + 512 * n:2048 * e + 512 * n + 512],
                                        start=(k == 0), stop=False)
                        if k == UP_CHUNKS - 1:
                            if n == 3 and in_ring:
                                mm.then_inc(ring_free, 1)
                            mm = matmul(pA[:, 512 * n:512 * n + 512], sel[0:96].rearrange("p e s -> p (e s)"),
                                        bias_up[0:96, 512 * n:512 * n + 512], start=False)
                            if n % 2:
                                mm.then_inc(up_done, 1)
                    if k < UP_CHUNKS - 1 and in_ring:
                        mm.then_inc(ring_free, 1)
                pe.wait_ge(pick_ready, g + 2)
                for half in range(2):
                    gather(bank, half)
                    pe.wait_ge(a_ready, 2 * g + (half + 1))
                    for k in range(4):
                        f = 128 * (4 * half + k)
                        mm = tr(pA[:, 1024 * half + 128 * k:1024 * half + 128 * k + 128], act_out[:, f:f + 128])
                    mm.then_inc(aT_full, 1)
                b = bank(2)
                pe.wait_ge(gpick_ready, g + 1)
                for m, (t0, r) in enumerate(TOK):
                    mm = tr(b[:, t0:t0 + r], gpick[0:r, m].rearrange("p e s -> p (e s)"))
                mm.then_inc(misc_full, 1)
                for k in range(KT):
                    if k % 4 == 0:
                        pe.wait_ge(aT_ready, 2 * g + (k // 4 + 1))
                    if k % 2 == 0:
                        w, in_ring = chunk(UP_CHUNKS + k // 2)
                    for n in range(2):
                        for e in range(2):
                            o = 2048 * e + 1024 * (k % 2) + 512 * n
                            mm = matmul(pB[64 * e:64 * e + 64, n, :], aT[:, k, 64 * e:64 * e + 64],
                                        w[:, o:o + 512], start=(k == 0), stop=False)
                        if k == KT - 1:
                            if n == 1 and in_ring:
                                mm.then_inc(ring_free, 1)
                            mm = matmul(pB[:, n, :], sel[0:96].rearrange("p e s -> p (e s)"),
                                        bias_down[0:96, 512 * n:512 * n + 512], start=False)
                            mm.then_inc(down_done, 1)
                    if k % 2 and k < KT - 1 and in_ring:
                        mm.then_inc(ring_free, 1)
                pe.wait_ge(misc_free, PAIR_FILLS * g + (misc0 + 3))
                for k, (m, h) in enumerate(OUTPUTS):
                    t0, r = TOK[m]
                    b = bank(3 + k)
                    if m == 0:
                        pe.wait_ge((y_ready, y_ready_dve)[h], g + 1)
                    matmul(b[0:r, :], gateT[:, t0:t0 + r], y_pair[:, 512 * h:512 * h + 512]).then_inc(misc_full, 1)

            pair(0, 0, first=True)
            with pe.Fori(1, PAIRS) as i:
                pair(i, i)
            pe.wait_ge(misc_free, FILL["route", 0])
            over = pe.value_load(flag[0:1, 0:1], min_val=0, max_val=1)
            with pe.If(over > 0):
                with pe.Fori(1, PASSES) as q:
                    with pe.Fori(0, PAIRS) as i:
                        pair(q * PAIRS + i, i)


_INS = ["x_prompt", "x_sample", "state_conv", "cache_k_win", "cache_v_win", "rel_bias", "attn_norm_w", "w_in",
        "conv_w", "q_norm_w", "k_norm_w", "sinks", "w_out", "ffn_norm_w", "w_router", "b_router", "w_up", "b_up",
        "w_down", "b_down"]
_BY_LAYER = set(_INS) - {"x_prompt", "x_sample", "rel_bias"}
_OUTS = [(1, SEQ, D), (DEC, 1, D), (1, 1, 2, D), (1, 1, WIN, NKV, HD), (1, 1, WIN, NKV, HD),
         (1, DEC, 2, D), (1, DEC, WIN, NKV, HD), (1, DEC, WIN, NKV, HD)]


def kernel(**inputs):
    import concourse.bacc as bacc
    from concourse.bass_utils import run_bass_kernel_spmd

    nc = bacc.Bacc("TRN2", target_bir_lowering=False, num_devices=1)
    arrays, args = {}, []
    for name in _INS:
        a = np.ascontiguousarray(inputs[name])
        arrays["in_" + name] = a
        ap = nc.dram_tensor("in_" + name, a.shape, F32, kind="ExternalInput").ap()
        args.append(ap[0] if name in _BY_LAYER else ap)
    arrays["in_consts"] = constants()
    args.append(nc.dram_tensor("in_consts", (128, C_N), F32, kind="ExternalInput").ap())
    for n, shape in enumerate(_OUTS):
        args.append(nc.dram_tensor(f"out_{n}", shape, F32, kind="ExternalOutput").ap())
    build(nc, *args)
    r = run_bass_kernel_spmd(nc, [arrays], core_ids=[0])
    return tuple(r.results[0][f"out_{n}"] for n in range(len(_OUTS)))
```
